# Optimizing a Trainium2 kernel written in Bass

```python
import jax, jax.numpy as jnp
from jax import lax
import numpy as np

D_MODEL = 2048
BATCH = 1
SEQ = 256
DEPTH = 1

BRANCH_WIDTH = D_MODEL // 4
NSA_HEADS = 8
NSA_KV_HEADS = 2
NSA_HD = BRANCH_WIDTH // NSA_HEADS
CMP_LEN = 32
CMP_STRIDE = 16
SLC_LEN = 64
SLC_TOP = 16
WINDOW = 512
Q_BLOCK = 128
HG_HEADS = 4
HG_DK = BRANCH_WIDTH // HG_HEADS
HG_DV = BRANCH_WIDTH // HG_HEADS
GLA_HEADS = 4
GLA_DK = BRANCH_WIDTH // 8
GLA_DV = BRANCH_WIDTH // GLA_HEADS
GLA_RANK = 16
GLA_TAU = 16.0
CHUNK = 64
N_GROUPS = 4
EXPERTS_PER_GROUP = 8
N_EXPERTS = N_GROUPS * EXPERTS_PER_GROUP
TOP_K = 2
D_FF_EXPERT = D_MODEL // 4
EPS = 1e-6
NEG = -1e30
FORCE = 1e4
TINY = 1e-30

IN_SPLITS = (
    ("nsa_q", NSA_HEADS * NSA_HD),
    ("nsa_k_cmp", NSA_KV_HEADS * NSA_HD), ("nsa_v_cmp", NSA_KV_HEADS * NSA_HD),
    ("nsa_k_slc", NSA_KV_HEADS * NSA_HD), ("nsa_v_slc", NSA_KV_HEADS * NSA_HD),
    ("nsa_k_win", NSA_KV_HEADS * NSA_HD), ("nsa_v_win", NSA_KV_HEADS * NSA_HD),
    ("nsa_gate", 3 * NSA_HEADS),
    ("hg_q", HG_HEADS * HG_DK), ("hg_f", HG_HEADS * HG_DK),
    ("hg_i", HG_HEADS * HG_DV), ("hg_g", HG_HEADS * HG_DV),
    ("gla_q", GLA_HEADS * GLA_DK), ("gla_k", GLA_HEADS * GLA_DK),
    ("gla_v", GLA_HEADS * GLA_DV), ("gla_r", GLA_HEADS * GLA_DV),
    ("gla_a", GLA_RANK),
    ("merge_gate", 3 * D_MODEL),
)
IN_COLS = sum(size for _, size in IN_SPLITS)

kernel_name = "hybrid_nsa_hgrn2_gla_hmoe"

def rmsnorm(x, gain):
    xf = x.astype(jnp.float32)
    y = xf * lax.rsqrt(jnp.mean(xf * xf, axis=-1, keepdims=True) + EPS)
    return (y * gain.astype(jnp.float32)).astype(x.dtype)

def split_cols(h):
    parts, off = {}, 0
    for name, size in IN_SPLITS:
        parts[name] = h[..., off:off + size]
        off += size
    return parts

def to_heads(a, n):
    B, T, _ = a.shape
    return a.reshape(B, T, n, -1).transpose(0, 2, 1, 3)

def from_heads(a):
    B, H, T, d = a.shape
    return a.transpose(0, 2, 1, 3).reshape(B, T, H * d)

def alibi_slopes(n):
    return jnp.exp2(-8.0 * jnp.arange(1, n + 1, dtype=jnp.float32) / n)

def compress_blocks(a, pe, w1, w2):
    B, G, T, hd = a.shape
    n_cmp = (T - CMP_LEN) // CMP_STRIDE + 1
    idx = jnp.arange(n_cmp)[:, None] * CMP_STRIDE + jnp.arange(CMP_LEN)[None, :]
    blocks = (a[:, :, idx, :] + pe).reshape(B, G, n_cmp, CMP_LEN * hd)
    return jax.nn.gelu(blocks @ w1) @ w2

def nsa_mixer(p, cmp_pe, cmp_w1, cmp_w2, q_gain, k_gain, slopes):
    B, T, _ = p["nsa_q"].shape
    G, R, hd = NSA_KV_HEADS, NSA_HEADS // NSA_KV_HEADS, NSA_HD
    scale = hd ** -0.5
    m = slopes.reshape(G, R)[None, :, :, None, None]
    q = rmsnorm(to_heads(p["nsa_q"], NSA_HEADS), q_gain).reshape(B, G, R, T, hd)
    t_pos = jnp.arange(T)

    kc = rmsnorm(compress_blocks(to_heads(p["nsa_k_cmp"], G), cmp_pe[0], cmp_w1[0], cmp_w2[0]), k_gain[0])
    vc = compress_blocks(to_heads(p["nsa_v_cmp"], G), cmp_pe[1], cmp_w1[1], cmp_w2[1])
    n_cmp = kc.shape[2]
    c_end = jnp.arange(n_cmp) * CMP_STRIDE + CMP_LEN - 1
    dist_c = (t_pos[:, None] - c_end[None, :]).astype(jnp.float32)
    vis_c = dist_c >= 0
    s = jnp.einsum('bgrtd,bgnd->bgrtn', q, kc).astype(jnp.float32) * scale - m * dist_c
    p_cmp = jax.nn.softmax(jnp.where(vis_c, s, NEG), axis=-1) * vis_c
    o_cmp = jnp.einsum('bgrtn,bgnd->bgrtd', p_cmp.astype(vc.dtype), vc)

    imp = p_cmp.sum(axis=2)
    n_slc = T // SLC_LEN
    ratio, span = SLC_LEN // CMP_STRIDE, CMP_LEN // CMP_STRIDE
    pad_l = span - 1
    pad_r = ratio * n_slc + ratio - 1 - n_cmp
    imp = jnp.pad(imp, ((0, 0), (0, 0), (0, 0), (pad_l, pad_r)))
    score = jnp.zeros((B, G, T, n_slc), jnp.float32)
    for mm in range(ratio):
        for nn in range(span):
            st = pad_l + mm - nn
            score = score + imp[..., st:st + ratio * n_slc:ratio]
    blk = jnp.arange(n_slc)[None, :]
    cur = (t_pos // SLC_LEN)[:, None]
    forced = (blk == 0) | (blk == cur) | (blk == cur - 1)
    score = jnp.where(forced, FORCE, score)
    score = jnp.where(blk <= cur, score, -1.0)
    n_top = min(SLC_TOP, n_slc)
    _, sel = lax.top_k(score, n_top)

    ks = rmsnorm(to_heads(p["nsa_k_slc"], G), k_gain[1]).reshape(B, G, n_slc, SLC_LEN, hd)
    vs = to_heads(p["nsa_v_slc"], G).reshape(B, G, n_slc, SLC_LEN, hd)
    nq = T // Q_BLOCK
    q_blocks = q.reshape(B, G, R, nq, Q_BLOCK, hd).transpose(3, 0, 1, 2, 4, 5)
    sel_blocks = sel.reshape(B, G, nq, Q_BLOCK, n_top).transpose(2, 0, 1, 3, 4)
    starts = jnp.arange(nq) * Q_BLOCK
    bi = jnp.arange(B)[:, None, None, None]
    gi = jnp.arange(G)[None, :, None, None]
    offs = jnp.arange(SLC_LEN)

    def attend_selected(args):
        qb, ib, st = args
        kb = ks[bi, gi, ib].reshape(B, G, Q_BLOCK, n_top * SLC_LEN, hd)
        vb = vs[bi, gi, ib].reshape(B, G, Q_BLOCK, n_top * SLC_LEN, hd)
        qpos = st + jnp.arange(Q_BLOCK)
        kpos = (ib[..., None] * SLC_LEN + offs).reshape(B, G, Q_BLOCK, n_top * SLC_LEN)
        dist = (qpos[:, None] - kpos).astype(jnp.float32)[:, :, None]
        sb = jnp.einsum('bgrqd,bgqkd->bgrqk', qb, kb).astype(jnp.float32) * scale - m * dist
        pb = jax.nn.softmax(jnp.where(dist >= 0, sb, NEG), axis=-1)
        return jnp.einsum('bgrqk,bgqkd->bgrqd', pb.astype(vb.dtype), vb)

    o_slc = lax.map(attend_selected, (q_blocks, sel_blocks, starts))
    o_slc = o_slc.transpose(1, 2, 3, 0, 4, 5).reshape(B, G, R, T, hd)

    kw = rmsnorm(to_heads(p["nsa_k_win"], G), k_gain[2])
    vw = to_heads(p["nsa_v_win"], G)
    nb = WINDOW // Q_BLOCK

    def band(a):
        a = jnp.pad(a, ((0, 0), (0, 0), (WINDOW, 0), (0, 0))).reshape(B, G, nq + nb, Q_BLOCK, hd)
        return jnp.concatenate([a[:, :, i:i + nq] for i in range(nb + 1)], axis=3)

    kbw, vbw = band(kw), band(vw)
    qw = q.reshape(B, G, R, nq, Q_BLOCK, hd)
    qpos = jnp.arange(nq)[:, None] * Q_BLOCK + jnp.arange(Q_BLOCK)[None, :]
    kpos = (jnp.arange(nq)[:, None] - nb) * Q_BLOCK + jnp.arange((nb + 1) * Q_BLOCK)[None, :]
    dist = qpos[:, :, None] - kpos[:, None, :]
    mask_w = (dist >= 0) & (dist < WINDOW) & (kpos[:, None, :] >= 0)
    sw = jnp.einsum('bgrcqd,bgckd->bgrcqk', qw, kbw).astype(jnp.float32) * scale \
        - m[..., None] * dist.astype(jnp.float32)
    pw = jax.nn.softmax(jnp.where(mask_w, sw, NEG), axis=-1)
    o_win = jnp.einsum('bgrcqk,bgckd->bgrcqd', pw.astype(vbw.dtype), vbw).reshape(B, G, R, T, hd)

    gates = jax.nn.sigmoid(p["nsa_gate"].astype(jnp.float32)).reshape(B, T, 3, G, R)
    gates = gates.transpose(2, 0, 3, 4, 1)[..., None]
    o = gates[0] * o_cmp + gates[1] * o_slc + gates[2] * o_win
    return o.transpose(0, 3, 1, 2, 4).reshape(B, T, NSA_HEADS * hd)

def gated_linear_recurrence(q, k, v, log_f):
    B, H, T, dk = q.shape
    dv = v.shape[-1]
    n = T // CHUNK

    def chunks(a):
        return a.astype(jnp.float32).reshape(B, H, n, CHUNK, a.shape[-1]).transpose(2, 0, 1, 3, 4)

    causal = jnp.tril(jnp.ones((CHUNK, CHUNK), dtype=bool))[:, :, None]

    def step(S, inp):
        qc, kc, vc, gc = inp
        b = jnp.cumsum(gc, axis=2)
        diff = b[:, :, :, None, :] - b[:, :, None, :, :]
        decay = jnp.where(causal, jnp.exp(jnp.where(causal, diff, 0.0)), 0.0)
        scores = jnp.einsum('bhid,bhjd,bhijd->bhij', qc, kc, decay)
        o = scores @ vc + jnp.einsum('bhid,bhdv->bhiv', qc * jnp.exp(b), S)
        b_end = b[:, :, -1:, :]
        S = jnp.exp(b_end[:, :, 0, :, None]) * S + jnp.einsum('bhjd,bhjv->bhdv', kc * jnp.exp(b_end - b), vc)
        return S, o

    S0 = jnp.zeros((B, H, dk, dv), jnp.float32)
    _, o = lax.scan(step, S0, (chunks(q), chunks(k), chunks(v), chunks(log_f)))
    return o.transpose(1, 2, 0, 3, 4).reshape(B, H, T, dv).astype(v.dtype)

def hgrn2_mixer(p, lower_bound, norm_gain):
    q = to_heads(p["hg_q"], HG_HEADS)
    z = to_heads(p["hg_f"], HG_HEADS).astype(jnp.float32)
    i = to_heads(p["hg_i"], HG_HEADS)
    lb = lower_bound.astype(jnp.float32).reshape(HG_HEADS, 1, HG_DK)
    f = lb + (1.0 - lb) * jax.nn.sigmoid(z)
    log_f = jnp.log(jnp.maximum(f, TINY))
    k = (1.0 - lb) * jax.nn.sigmoid(-z)
    o = gated_linear_recurrence(q, k, i, log_f)
    o = rmsnorm(o, norm_gain) * jax.nn.sigmoid(to_heads(p["hg_g"], HG_HEADS))
    return from_heads(o)

def gla_mixer(p, w_a2, b_a, norm_gain):
    q = to_heads(p["gla_q"], GLA_HEADS) * (GLA_DK ** -0.5)
    k = to_heads(p["gla_k"], GLA_HEADS)
    v = to_heads(p["gla_v"], GLA_HEADS)
    a = (p["gla_a"] @ w_a2 + b_a).astype(jnp.float32)
    log_a = to_heads(jax.nn.log_sigmoid(a) / GLA_TAU, GLA_HEADS)
    o = gated_linear_recurrence(q, k, v, log_a)
    o = rmsnorm(o, norm_gain) * jax.nn.silu(to_heads(p["gla_r"], GLA_HEADS))
    return from_heads(o)

def hybrid_mixer(h, w_in, cmp_pe, cmp_w1, cmp_w2, q_gain, k_gain, lower_bound, hg_norm,
                 gla_w_a2, gla_b_a, gla_norm, w_branch, w_out, slopes):
    B, T, D = h.shape
    p = split_cols(h @ w_in)
    o_a = nsa_mixer(p, cmp_pe, cmp_w1, cmp_w2, q_gain, k_gain, slopes).astype(h.dtype)
    o_b = hgrn2_mixer(p, lower_bound, hg_norm).astype(h.dtype)
    o_c = gla_mixer(p, gla_w_a2, gla_b_a, gla_norm).astype(h.dtype)
    branches = jnp.stack([o_a, o_b, o_c])
    proj = jnp.einsum('nbtw,nwd->nbtd', branches, w_branch)
    gates = jax.nn.sigmoid(p["merge_gate"].reshape(B, T, 3, D)).transpose(2, 0, 1, 3)
    merged = jnp.sum(gates * proj, axis=0)
    return (merged @ w_out).astype(h.dtype)

def hierarchical_moe(h, w_grp, b_grp, w_exp, b_exp, w_gate_up, w_down):
    B, T, D = h.shape
    N = B * T
    xt = h.reshape(N, D)
    grp_prob = jax.nn.softmax((xt @ w_grp).astype(jnp.float32) + b_grp, axis=-1)
    grp_w, grp_idx = lax.top_k(grp_prob, 1)
    exp_logits = ((xt @ w_exp).astype(jnp.float32) + b_exp).reshape(N, N_GROUPS, EXPERTS_PER_GROUP)
    exp_logits = jnp.take_along_axis(exp_logits, grp_idx[:, :, None], axis=1)[:, 0]
    top_w, top_idx = lax.top_k(jax.nn.softmax(exp_logits, axis=-1), TOP_K)
    top_w = top_w / jnp.sum(top_w, axis=-1, keepdims=True)
    weights = grp_w * top_w
    expert_id = grp_idx * EXPERTS_PER_GROUP + top_idx
    combine = jnp.zeros((N, N_EXPERTS), jnp.float32).at[jnp.arange(N)[:, None], expert_id].add(weights)
    y = jnp.zeros((N, D), jnp.float32)
    for g in range(N_GROUPS):
        sl = slice(g * EXPERTS_PER_GROUP, (g + 1) * EXPERTS_PER_GROUP)
        gu = jnp.einsum('nd,edf->nef', xt, w_gate_up[sl])
        gate, up = jnp.split(gu, 2, axis=-1)
        act = jax.nn.silu(gate) * up * combine[:, sl, None].astype(gu.dtype)
        y = y + jnp.einsum('nef,efd->nd', act, w_down[sl])
    return y.reshape(B, T, D).astype(h.dtype)

def setup_inputs(seed: int = 0) -> dict:
    key = jax.random.key(seed)
    ks = jax.random.split(key, 24)
    f32 = jnp.float32
    L, D = DEPTH, D_MODEL

    def nrm(k, shape, scale):
        return jax.random.normal(k, shape, f32) * scale

    return {
        "x": nrm(ks[0], (BATCH, SEQ, D), 1.0),
        "norm_mix": 1.0 + nrm(ks[1], (L, D), 0.02),
        "w_in": nrm(ks[2], (L, D, IN_COLS), D ** -0.5),
        "cmp_pe": nrm(ks[3], (L, 2, CMP_LEN, NSA_HD), 0.1),
        "cmp_w1": nrm(ks[4], (L, 2, CMP_LEN * NSA_HD, NSA_HD), (CMP_LEN * NSA_HD) ** -0.5),
        "cmp_w2": nrm(ks[5], (L, 2, NSA_HD, NSA_HD), NSA_HD ** -0.5),
        "q_norm": 1.0 + nrm(ks[6], (L, NSA_HD), 0.02),
        "k_norm": 1.0 + nrm(ks[7], (L, 3, NSA_HD), 0.02),
        "hg_lb_logits": nrm(ks[8], (L, HG_HEADS * HG_DK), 0.1),
        "hg_norm": 1.0 + nrm(ks[9], (L, HG_DV), 0.02),
        "gla_w_a2": nrm(ks[10], (L, GLA_RANK, GLA_HEADS * GLA_DK), GLA_RANK ** -0.5),
        "gla_b_a": nrm(ks[11], (L, GLA_HEADS * GLA_DK), 0.1),
        "gla_norm": 1.0 + nrm(ks[12], (L, GLA_DV), 0.02),
        "w_branch": nrm(ks[13], (L, 3, BRANCH_WIDTH, D), BRANCH_WIDTH ** -0.5),
        "w_out": nrm(ks[14], (L, D, D), D ** -0.5),
        "norm_ffn": 1.0 + nrm(ks[15], (L, D), 0.02),
        "w_grp": nrm(ks[16], (L, D, N_GROUPS), D ** -0.5),
        "b_grp": nrm(ks[17], (L, N_GROUPS), 0.01),
        "w_exp": nrm(ks[18], (L, D, N_EXPERTS), D ** -0.5),
        "b_exp": nrm(ks[19], (L, N_EXPERTS), 0.01),
        "w_gate_up": nrm(ks[20], (L, N_EXPERTS, D, 2 * D_FF_EXPERT), D ** -0.5),
        "w_down": nrm(ks[21], (L, N_EXPERTS, D_FF_EXPERT, D), D_FF_EXPERT ** -0.5),
    }

def reference(x, norm_mix, w_in, cmp_pe, cmp_w1, cmp_w2, q_norm, k_norm, hg_lb_logits, hg_norm,
              gla_w_a2, gla_b_a, gla_norm, w_branch, w_out, norm_ffn, w_grp, b_grp, w_exp, b_exp,
              w_gate_up, w_down):
    slopes = alibi_slopes(NSA_HEADS)
    P = jax.nn.softmax(hg_lb_logits.astype(jnp.float32), axis=0)
    lower_bounds = jnp.cumsum(P, axis=0) - P[0]
    for l in range(DEPTH):
        h = rmsnorm(x, norm_mix[l])
        x = x + hybrid_mixer(h, w_in[l], cmp_pe[l], cmp_w1[l], cmp_w2[l], q_norm[l], k_norm[l],
                             lower_bounds[l], hg_norm[l], gla_w_a2[l], gla_b_a[l], gla_norm[l],
                             w_branch[l], w_out[l], slopes)
        h = rmsnorm(x, norm_ffn[l])
        x = x + hierarchical_moe(h, w_grp[l], b_grp[l], w_exp[l], b_exp[l], w_gate_up[l], w_down[l])
    return x


_drawn_inputs = setup_inputs


def setup_inputs(seed=0):
    import zlib

    import numpy as np

    out = dict(_drawn_inputs(seed))
    spreads = {}
    factors = {'q_norm': 8.0,
     'k_norm': 8.0,
     'hg_norm': 20.266,
     'gla_norm': 22.226,
     'b_grp': 37.097,
     'b_exp': 16.162,
     'cmp_pe': 2.995,
     'norm_ffn': 5.565}
    for name, (base, spread) in spreads.items():
        noise = np.random.default_rng([zlib.crc32(name.encode()), seed]).standard_normal(out[name].shape)
        drawn = base * np.exp(spread * noise) if base else spread * noise
        out[name] = __import__('jax').numpy.asarray(drawn.astype(out[name].dtype))
    for name, factor in factors.items():
        out[name] = (out[name] * factor).astype(out[name].dtype)
    return out
```

```python
import numpy as np

import concourse.bass as bass
from concourse import mybir

F32 = mybir.dt.float32
F32R = mybir.dt.float32r
U32 = mybir.dt.uint32
I32 = mybir.dt.int32
ALU = mybir.AluOpType
ACT = mybir.ActivationFunctionType
AX = mybir.AxisListType

P = 128
D = 2048
T = 256
TT = T // P
KT = D // P
BW = D // 4
HEADS, KV, HD = 8, 2, 64
NCMP = (T - 32) // 16 + 1
CHUNK = 64
NG, EPG = 4, 8
NE = NG * EPG
FF = D // 4
EPS = 1e-6
NEG = -1e30
TINY = 1e-30
SLOTS = 32
OVER = 2 * T // SLOTS
ITEMS = NE + OVER
NROUTE = NG + NE

Q0, KC0, KW0 = 0, 512, 1024
HGQ0 = 1304
HGF0, HGI0, HGG0 = HGQ0 + 512, HGQ0 + 1024, HGQ0 + 1536
GLQ0 = HGQ0 + 2048
GLV0, GLR0, GLA0 = GLQ0 + 512, GLQ0 + 1024, GLQ0 + 1536
MG0 = GLA0 + 16

SLOPES = [2.0 ** (-8.0 * (h + 1) / HEADS) for h in range(HEADS)]


def constants():
    p = np.arange(P)
    a, b = {}, {}
    b["ident"] = np.eye(P)
    b["ones"] = np.ones((P, P))
    b["before"] = (p[:, None] < p[None, :]) * 1.0
    b["iota32"] = np.tile(np.arange(NE), (P, 1))
    b["iota48"] = np.tile(np.arange(ITEMS), (P, 1))
    b["slot4"] = np.tile(np.arange(P) % SLOTS, (P, 1))
    b["group"] = (p // SLOTS)[:, None]
    b["part"] = p[:, None]
    b["padmax"] = np.full((P, 8), NEG)
    a["halves"] = (p[:, None] // HD == p[None, :] // HD) * 1.0
    lv = [p[:, None] == p[None, :]]
    s = 1
    while s < P:
        lv.append((p[:, None] // (2 * s) == p[None, :] // (2 * s)) & (p[:, None] % (2 * s) < s) & (p[None, :] % (2 * s) >= s))
        s *= 2
    a["levels"] = np.concatenate([m * 1.0 for m in lv], 1)
    big = 1e32
    d0 = p[:, None] - p[None, :]
    d1 = p[:, None] + P - np.arange(T)[None, :]
    a["dist0"] = np.where(d0 >= 0, d0, big)
    a["dist1"] = np.where(d1 >= 0, d1, big)
    t = p[:, None] + P * np.arange(TT)[None, :]
    n = np.arange(16)
    dc = t[:, :, None] - (n * 16 + 31)[None, None, :]
    vis = (dc >= 0) & (n < NCMP)
    cb = np.zeros((P, TT, 4, KV, 16))
    for i in range(4):
        for g in range(KV):
            cb[:, :, i, g] = np.where(vis, -SLOPES[g * 4 + i] * dc, NEG)
    a["cbias"] = cb.reshape(P, -1)
    a["cvis"] = vis.reshape(P, -1) * 1.0
    r = np.ones((P, 4, T))
    r[:, :, ::CHUNK] = 0
    a["reset"] = r.reshape(P, -1)
    out = []
    for c in (a, b):
        off, where = 0, {}
        for k, v in c.items():
            where[k] = (off, v.shape[1])
            off += v.shape[1]
        out.append((np.concatenate([np.asarray(v, np.float32) for v in c.values()], 1), where))
    return out


class Chain:

    def __init__(self, eng, sem):
        self.eng, self.sem, self.n = eng, sem, 0

    def __call__(self, ins):
        self.n += 1
        ins.then_inc(self.sem, 1)
        self.eng.wait_ge(self.sem, self.n)


def build_program(nc, i_, consts, wa, wb_, out):
    ring_at = 16512
    ts = nc.alloc_sbuf_tensor_at
    K = 1024

    def at(name, shape, off, dt=F32):
        return ts(name, shape, dt, offset=off)

    RING = at("ring", [P, 6, 4096], ring_at)
    HR_AT = ring_at + 96 * K
    hr = at("hr", [P, 2, KT, T], HR_AT, F32R)
    WR_AT = HR_AT + 32 * K
    wr = at("wr", [P, 3, 2, 1024], WR_AT, F32R)
    XR = WR_AT + 24 * K
    MX = XR + 16 * K
    OV = ring_at + 48 * K
    x_sb = at("x_sb", [P, TT, D], XR)
    orr = at("orr", [P, 2, 12, T], MX, F32R)
    hgq = at("hgq", [P, 4, T], MX + 24 * K)
    SM = MX + 28 * K
    cb = at("cb", [P, wb_["_n"]], SM)
    SM2 = SM + (4 * wb_["_n"] + 31) // 32 * 32
    sm_off = [SM2]

    def small(name, shape, dt=F32):
        n = 4 * int(np.prod(shape[1:]))
        n = (n + 31) // 32 * 32
        t_ = at(name, shape, sm_off[0], dt)
        sm_off[0] += n
        assert sm_off[0] <= 229368, sm_off
        return t_

    o = OV
    ca = at("ca", [P, wa["_n"]], o); o += (4 * wa["_n"] + 31) // 32 * 32
    pn = at("pn", [P, 11, T], o)
    hgk = at("hgk", [P, 4, T], o)
    hgb = at("hgb", [P, 4, T], o + 4 * K)
    st2 = at("st2", [P, 4, P], o + 8 * K)
    o += 11 * K
    kz = at("kz", [P, 2, KV, T], o)
    wbuf = at("wbuf", [P, 4, T], o); o += 4 * K
    vz = at("vz", [P, TT, 2, KV, P], o)
    zb0 = at("zb0", [P, 4, T], o); o += 4 * K
    ax = at("ax", [P, 2, 32, 16], o)
    sq = at("sq", [P, 6, T], o)
    zb1 = at("zb1", [P, 4, T], o); o += 4 * K
    vcb = at("vcb", [P, 4, P], o); o += 2 * K
    ptc = at("ptc", [P, TT, P], o); o += K
    STG = o - 3 * K
    sb = at("sb", [P, 2, KV, T], o)
    rr = at("rr", [P, 6, T], o)
    st = at("st", [P, 8, P], o + K)
    stg = at("stg", [P, 1024], STG)
    o += 4 * K
    PT_AT = o
    pt = at("pt", [P, 4, P], o); o += 2 * K
    hgz = at("hgz", [P, 4, T], o)
    glqk = at("glqk", [P, 4, T], o); o += 4 * K
    assert o <= OV + 48 * K, (o - OV) / K
    w1 = at("w1", [P, 2, 32, HD], XR)
    hgi = at("hgi", [P, TT, 512], XR)
    hgg = at("hgg", [P, TT, 512], XR + 4 * K)
    glv = at("glv", [P, TT, 512], XR + 8 * K)
    glr = at("glr", [P, TT, 512], XR + 12 * K)
    stge = at("stge", [P, 2, 1024], XR + 8 * K)

    def stage(c):
        return stge[:, c % 2, :] if c < 6 else stg[:]
    gla = small("gla", [P, T])
    merged = at("merged", [P, TT, D], OV)
    gsb = at("gsb", [P, 2, TT * 512], OV + 16 * K)
    prod = at("prod", [P, TT * 512], OV + 24 * K)
    h2t = at("h2t", [P, KT, T], HR_AT)
    h2 = at("h2", [P, TT, D], HR_AT + 16 * K)
    wro = at("wro", [P, KT, NROUTE], WR_AT)
    ltb = at("ltb", [P, T], WR_AT + 3 * K)
    MC = WR_AT + 4 * K
    xg = at("xg", [P, 2, 512], MC)
    xt = at("xt", [P, 2, 4, P], MC + 4 * K)
    gu = at("gu", [P, 256], MC + 8 * K)
    sgm = at("sgm", [P, 2, 64], MC + 9 * K)
    up = at("up", [P, 2, 64], MC + 9 * K + 512)
    act_t = at("act_t", [P, 2, 64], MC + 10 * K)
    yb = at("yb", [P, 2, 512], MC + 12 * K)
    RT = MC + 16 * K
    y0 = at("y0", [P, TT, D], HR_AT)
    y1 = at("y1", [P, TT, D], HR_AT + 16 * K)

    pj = [nc.alloc_psum_tensor(f"pj{b}", [P, 1024], F32) for b in range(2)]
    px = [nc.alloc_psum_tensor(f"px{b}", [P, 512], F32) for b in range(4)]

    def C(name):
        w, t_ = (wa, ca) if name in wa else (wb_, cb)
        off, n = w[name]
        return t_[:, off:off + n]

    gates_d = nc.dram_tensor("gates_d", (12, P, 1024), F32, kind="Internal").ap()
    h2_d = nc.dram_tensor("h2_d", (T * 4, 512), F32, kind="Internal").ap()
    y_d = nc.dram_tensor("y_d", (2 * T * 4, 512), F32, kind="Internal").ap()

    SEQUENCES = {
        "nsa_dve": [("nsa_sq", 1), ("nsa_ms", 3), ("nsa_qk", 5), ("cmp_in", 1), ("cmp_hidden", 4), ("cmp_u", 1), ("cmp_g", 1), ("cmp_v", 2), ("cmp_sq", 1), ("cmp_ms", 1), ("cmp_k", 2), ("cmp_sub", 1), ("cmp_p", 1), ("cmp_ptc", 1)],
        "nsa_pe": [("nsa_ss", 1), ("nsa_turned", 1), ("cmp_h", 2), ("cmp_kv", 1), ("cmp_ss", 1), ("cmp_scores", 1), ("cmp_pt", 1)],
        "nsa_act": [("nsa_sd", 1), ("nsa_gates", 1), ("cmp_s", 1), ("cmp_sd", 1), ("cmp_exp", 1)],
        "router_dve": [("r_hi", 16), ("r_lt", 1), ("r_shift", 1), ("r_onehot", 1), ("r_val", 1), ("overflow_known", 1), ("r_tabread", 1)],
        "router_pe": [("r_turned", 8), ("r_logit", 1), ("r_lturned", 1), ("r_rank", 1), ("r_tab", 1)],
    }
    before_step = {}
    for seq, steps in SEQUENCES.items():
        n = 0
        for step_name, incs in steps:
            before_step[step_name] = (seq, n)
            n += incs

    def V(name):
        return before_step.get(name, (name, 0))[1]

    sems = {}

    def S(name):
        name = before_step.get(name, (name, 0))[0]
        if name not in sems:
            sems[name] = nc.alloc_semaphore(name)
        return sems[name]

    gmix = small("gmix", [P, KT])
    gffn = small("gffn", [P, KT])
    stat = small("stat", [P, 16])
    ngain = small("ngain", [P, 4])
    hgain = small("hgain", [P, P])
    ggain = small("ggain", [P, P])
    lb = small("lb", [P, 4, 4])
    bal = small("bal", [P, 2])
    wa2 = small("wa2", [16, T])
    w2 = small("w2", [P, 2, HD])
    pe2 = at("pe2", [64, P], MX + 24 * K)
    rows = at("rows", [16, 3, P], PT_AT)
    gate = small("gate", [P, TT, 24])
    hid = small("hid", [P, 6, 2, 16])
    kct = small("kct", [P, 4, 16])
    kcz = small("kcz", [P, KV, 16])
    vcs = small("vcs", [16, KV, HD])
    cs = small("cs", [P, 5, 16])
    csc = at("csc", [P, TT * P], PT_AT)
    am = small("am", [P, 2, 8])
    zr = small("zr", [P, 8])

    win, wbr, wout = i_["w_in"][0], i_["w_branch"][0], i_["w_out"][0]
    panels = []

    def in_panel(kind, c0, width, key):
        panels.append(dict(kind=kind, key=key, width=width, kts=KT, act="h",
                           src=[win[h * 1024:(h + 1) * 1024, c0:c0 + width].rearrange("(k p) c -> p k c", p=P) for h in range(2)]))

    in_panel("q", Q0, 512, "nsa_q")
    in_panel("t", KC0, 512, "nsa_k")
    in_panel("t3", KW0, 512, "nsa_w")
    in_panel("t", HGF0, 512, "hg_f")
    in_panel("t", HGQ0, 512, "hg_q")
    in_panel("n", HGI0, 512, "hg_i")
    in_panel("n", HGG0, 512, "hg_g")
    EARLY = 6
    for c in range(EARLY):
        in_panel("n", MG0 + 512 * c, 512, f"mg{c}")
    in_panel("t", GLQ0, 512, "gl_qk")
    in_panel("t1", GLA0, 128, "gl_a")
    in_panel("n", GLV0, 512, "gl_v")
    in_panel("n", GLR0, 512, "gl_r")
    for c in range(EARLY, 12):
        in_panel("n", MG0 + 512 * c, 512, f"mg{c}")
    PI = {pan["key"]: n for n, pan in enumerate(panels)}
    FIRST_B = len(panels)
    for n in range(3):
        for c in range(4):
            panels.append(dict(kind="n", key=f"br{n}{c}", width=512, kts=4, act=n,
                               src=[wbr[n][:, c * 512:(c + 1) * 512].rearrange("(k p) c -> p k c", p=P)]))
    FIRST_O = len(panels)
    for c in range(4):
        panels.append(dict(kind="n", key=f"wo{c}", width=512, kts=KT, act="m",
                           src=[wout[h * 1024:(h + 1) * 1024, c * 512:(c + 1) * 512].rearrange("(k p) c -> p k c", p=P) for h in range(2)]))
    slots, units = [], []
    for pi, pan in enumerate(panels):
        pan["u0"] = len(units)
        for s_ in range(len(pan["src"])):
            nk = min(8, pan["kts"] - 8 * s_)
            k_ = len(slots)
            for qd in range(nk // 2):
                units.append((pi, k_, qd, 8 * s_ + 2 * qd))
            slots.append((pi, s_, nk, len(units)))
        pan["u1"] = len(units)
    NU = len(units)
    UB = panels[FIRST_B]["u0"]
    UO = panels[FIRST_O]["u0"]

    def raw(u):
        pi, k_, qd, _ = units[u]
        w = panels[pi]["width"]
        return RING[:, k_ % 3, qd * 2 * w:(qd + 1) * 2 * w]

    gexp_w, down_w = i_["w_gate_up"][0], i_["w_down"][0]

    A0 = 26
    CM = A0 + 4
    AT0 = CM + 31
    HG0 = AT0 + 40
    GL0 = HG0 + 40
    NL = 8

    sched = {e: {} for e in ("pe", "act", "dve", "pool")}

    def put(e, pos, fn, *a):
        sched[e].setdefault(pos, []).append((fn, a))

    def go(e, pos):
        for fn, a in sched[e].get(pos, ()):
            fn(*a)

    hi, lo = 0, 1

    def consts_loads(sp):
        sp.dma_start(cb[:], consts["cb"]).then_inc(S("const_b"), 16)
        sp.dma_start(x_sb[:], i_["x"][0].rearrange("(a p) d -> p a d", p=P)).then_inc(S("x_in"), 16)
        sp.dma_start(rows[:, 0, :], i_["norm_mix"][0].rearrange("(k p) -> k p", p=P)).then_inc(S("rows_in"), 16)
        sp.dma_start(rows[:, 1, :], i_["norm_ffn"][0].rearrange("(k p) -> k p", p=P)).then_inc(S("rows_in"), 16)
        sp.dma_start(rows[0:4, 2, :], i_["hg_lb_logits"][0].rearrange("(k p) -> k p", p=P)).then_inc(S("rows_in"), 16)

    def small_loads(sp):
        def ld(dst, src):
            sp.dma_start(dst, src).then_inc(S("small_in"), 16)
            small_loads.n += 1
        small_loads.n = 0
        ld(ca[:], consts["ca"])
        for half in range(2):
            r = slice(half * HD, (half + 1) * HD)
            ld(ngain[r, 0:1], i_["q_norm"][0].rearrange("(d o) -> d o", o=1))
            for j in range(3):
                ld(ngain[r, 1 + j:2 + j], i_["k_norm"][0, j].rearrange("(d o) -> d o", o=1))
            ld(w2[r, :, :], i_["cmp_w2"][0].rearrange("v a b -> a v b"))
            ld(pe2[:, half * HD:(half + 1) * HD], i_["cmp_pe"][0].rearrange("v l d -> (v l) d"))
        ld(hgain[:], i_["hg_norm"].broadcast_to([P, P]))
        ld(ggain[:], i_["gla_norm"].broadcast_to([P, P]))
        ld(wa2[:], i_["gla_w_a2"][0])
        for a in range(2):
            ld(bal[:, a:a + 1], i_["gla_b_a"][0, a * P:(a + 1) * P].rearrange("(p o) -> p o", o=1))
        return small_loads.n * 16

    SMALL_IN = 16 * (1 + 2 * 6 + 5)

    def load_slot(sp, k_):
        pi, s_, nk, _ = slots[k_]
        if k_ >= 3:
            sp.wait_ge(S("split_lo"), slots[k_ - 3][3])
        w = panels[pi]["width"]
        dst = RING[:, k_ % 3, 0:nk * w].rearrange("p (k c) -> p k c", k=nk)
        src = panels[pi]["src"][s_]
        if panels[pi]["act"] == 0:
            c = int(panels[pi]["key"][3])
            for half in range(2):
                r = slice(half * HD, (half + 1) * HD)
                src = wbr[0][half * 256:(half + 1) * 256, c * 512:(c + 1) * 512].rearrange("(k p) c -> p k c", p=HD)
                sp.dma_start(dst[r], src).then_inc(S(f"landed{k_ % 3}"), 16)
        else:
            sp.dma_start(dst, src).then_inc(S(f"landed{k_ % 3}"), 16)

    landed, tot = {}, [0, 0, 0]
    for k_ in range(len(slots)):
        tot[k_ % 3] += 32 if panels[slots[k_][0]]["act"] == 0 else 16
        landed[k_] = tot[k_ % 3]

    def unit_parts(u):
        w = panels[units[u][0]]["width"]
        if panels[units[u][0]]["kind"] != "q":
            return [(raw(u), lambda h: wr[:, u % 3, h, 0:2 * w])]
        return [(raw(u)[:, k * w:(k + 1) * w].rearrange("p (g i d) -> p i g d", g=2, i=4),
                 lambda h, k=k: wr[:, u % 3, h, k * w:(k + 1) * w].rearrange("p (i g d) -> p i g d", g=2, i=4)) for k in range(2)]

    def act_hi(act, u):
        pi, k_, qd, kt = units[u]
        w = panels[pi]["width"]
        act.wait_ge(S(f"landed{k_ % 3}"), landed[k_])
        if u >= 3:
            act.wait_ge(S("unit_done"), u - 2)
        for src, half in unit_parts(u):
            ins = act.activation(half(hi), src, ACT.Copy)
        ins.then_inc(S("split_hi"), 1)

    def pool_lo(pool, u):
        pool.wait_ge(S("split_hi"), u + 1)
        for src, half in unit_parts(u):
            ins = pool.tensor_tensor(half(lo), src, half(hi).bitcast(F32), ALU.subtract)
        ins.then_inc(S("split_lo"), 1)

    evac_engine = {}
    for pi, pan in enumerate(panels):
        evac_engine[pi] = "dve"

    def pe_unit(pe, u):
        pi, k_, qd, kt = units[u]
        pan = panels[pi]
        bank = pj[pi % 2]
        if u == 0:
            pe.wait_ge(S("h_hi"), KT)
            pe.wait_ge(S("h_lo"), KT)
        if u == pan["u0"] and pi >= 2:
            pe.wait_ge(S("panel_read"), pi - 1)
        if pan["act"] != "h" and pan["act"] != "m" and u == pan["u0"]:
            pe.wait_ge(S("branch_lo"), 8 * (pan["act"] + 1))
            pe.wait_ge(S("branch_hi"), 8 * (pan["act"] + 1))
        if u == UO:
            pe.wait_ge(S("m_hi"), KT)
            pe.wait_ge(S("m_lo"), KT)
        pe.wait_ge(S("split_lo"), u + 1)
        pe.wait_ge(S("split_hi"), u + 1)
        w = pan["width"]
        mm = None
        for k in range(2):
            kk = kt + k
            first, last = kk == 0, kk == pan["kts"] - 1

            def a_(h, tt=None):
                if pan["act"] in ("h", "m"):
                    t_ = hr[:, h, kk, :]
                else:
                    t_ = orr[:, h, 4 * pan["act"] + kk, :]
                return t_ if tt is None else t_[:, tt * P:(tt + 1) * P]

            wu = [wr[:, u % 3, h, k * w:(k + 1) * w] for h in range(2)]
            if pan["kind"] == "n":
                for tt in range(TT):
                    for n, (ah, wh) in enumerate(((hi, hi), (lo, hi), (hi, lo))):
                        mm = pe.matmul(bank[:, tt * 512:(tt + 1) * 512], a_(ah, tt), wu[wh],
                                       start=first and n == 0, stop=last and n == 2)
            else:
                for m in range({"q": 4, "t": 4, "t3": 3, "t1": 1}[pan["kind"]]):
                    for n, (ah, wh) in enumerate(((hi, hi), (lo, hi), (hi, lo))):
                        lhs = wu[wh][:, m * P:(m + 1) * P]
                        mm = pe.matmul(bank[:, m * T:(m + 1) * T], lhs, a_(ah),
                                       start=first and n == 0 and m % 2 == 0, stop=last and n == 2,
                                       skip_group_check=True)
        mm.then_inc(S("unit_done"), 1)

    def dve_read_panel(dve, pi):
        pan = panels[pi]
        key = pan["key"]
        dve.wait_ge(S("unit_done"), pan["u1"])
        src = pj[pi % 2]
        dests = {"nsa_q": (pn[:, 0:4, :], 1024), "nsa_k": (pn[:, 4:8, :], 1024), "nsa_w": (pn[:, 8:11, :], 768),
                 "hg_f": (hgz[:], 1024), "hg_q": (hgq[:], 1024), "hg_i": (hgi[:], 1024), "hg_g": (hgg[:], 1024),
                 "gl_qk": (glqk[:], 1024), "gl_a": (gla[:], 256), "gl_v": (glv[:], 1024), "gl_r": (glr[:], 1024)}
        if key in dests:
            if key == "nsa_q":
                dve.wait_ge(S("small_in"), SMALL_IN)
            if key == "hg_i":
                dve.wait_ge(S("cmp_hidden"), V("cmp_hidden") + 4)
            if key in ("gl_v", "gl_r"):
                for j in range(2):
                    dve.wait_ge(S(f"gates_out{j}"), 16 * (EARLY // 2))
            if key == "gl_qk":
                dve.wait_ge(S("hg_sig"), 2)
            d_, n = dests[key]
            if len(d_.shape) == 3:
                d_ = d_.rearrange("p a b -> p (a b)")
            dve.tensor_copy(d_, src[:, 0:n]).then_inc(S("panel_read"), 1)
        elif key.startswith("mg"):
            c = int(key[2:])
            if c == 0:
                dve.wait_ge(S("cmp_hidden"), V("cmp_hidden") + 4)
            elif c == EARLY:
                dve.wait_ge(S("att_done"), 1)
            elif c >= 2:
                before = c - 2 if c < EARLY else c - 1
                dve.wait_ge(S(f"gates_out{before % 2}"), 16 * (before // 2 + 1))
            dve.tensor_copy(stage(c), src[:]).then_inc(S("panel_read"), 1)
        elif key.startswith("br"):
            n, c = int(key[2]), int(key[3])
            b = 4 * n + c
            if b == 0:
                dve.wait_ge(S("branch_lo"), 24)
                dve.wait_ge(S("branch_hi"), 24)
            dve.wait_ge(S("gate_sig"), b + 1)
            m = merged[:, :, c * 512:(c + 1) * 512]
            g3 = gsb[:, b % 2, :].rearrange("p (a b) -> p a b", a=TT)
            s3 = src[:].rearrange("p (a b) -> p a b", a=TT)
            if n == 0:
                dve.tensor_tensor(m, s3, g3, ALU.mult).then_inc(S("panel_read"), 1)
                dve.sem_inc if False else None
                dve.wait_ge(S("panel_read"), pi + 1)
                dve.tensor_scalar(zr[:, 0:1], zr[:, 1:2], 0.0, None, ALU.mult).then_inc(S("gate_used"), 1)
                dve.wait_ge(S("gate_used"), b + 1)
            else:
                p3 = prod[:].rearrange("p (a b) -> p a b", a=TT)
                dve.tensor_tensor(p3, s3, g3, ALU.mult).then_inc(S("panel_read"), 1)
                dve.wait_ge(S("panel_read"), pi + 1)
                dve.tensor_tensor(m, m, p3, ALU.add).then_inc(S("gate_used"), 1)
                dve.wait_ge(S("gate_used"), b + 1)
        else:
            c = int(key[2])
            if c == 0:
                dve.wait_ge(S("x_in"), 32)
            xs = x_sb[:, :, c * 512:(c + 1) * 512]
            dve.tensor_tensor(xs, src[:].rearrange("p (a b) -> p a b", a=TT), xs, ALU.add).then_inc(S("panel_read"), 1)

    eng = {}

    def rsqrt_steps_dve(link, dst, src, scale):
        link(eng["dve"].tensor_scalar(dst, src, scale, EPS, ALU.mult, ALU.add))

    def norm_act(act, first):
        nm = "n1" if first else "n2"
        if first:
            act.wait_ge(S("x_in"), 16)
        else:
            act.wait_ge(S("panel_read"), len(panels))
        for tt in range(TT):
            junk = pj[1][:]
            for h in range(2):
                ins = act.activation(junk, x_sb[:, tt, h * 1024:(h + 1) * 1024], ACT.Square,
                                     accum_out=stat[:, 2 * tt + h:2 * tt + h + 1])
                ins.then_inc(S(nm + "_sq"), 1)
                act.wait_ge(S(nm + "_sq"), 2 * tt + h + 1)
        act.wait_ge(S(nm + "_ms"), 1)
        act.activation(stat[:, 6:8], stat[:, 4:6], ACT.Sqrt).then_inc(S(nm + "_sd"), 1)

    def norm_dve(dve, link, first):
        nm = "n1" if first else "n2"
        dve.wait_ge(S(nm + "_sq"), 4)
        link(dve.tensor_tensor(stat[:, 4:6], stat[:, 0:4:2], stat[:, 1:4:2], ALU.add))
        dve.tensor_scalar(stat[:, 4:6], stat[:, 4:6], 1.0 / D, EPS, ALU.mult, ALU.add).then_inc(S(nm + "_ms"), 1)
        dve.wait_ge(S(nm + "_ms"), 1)
        dve.wait_ge(S(nm + "_sd"), 1)
        link(dve.reciprocal(stat[:, 8:10], stat[:, 6:8]))
        link(dve.tensor_tensor(stat[:, 10:12], stat[:, 8:10], stat[:, 8:10], ALU.mult))
        link(dve.tensor_tensor(stat[:, 10:12], stat[:, 10:12], stat[:, 4:6], ALU.mult))
        link(dve.tensor_scalar(stat[:, 10:12], stat[:, 10:12], -0.5, 1.5, ALU.mult, ALU.add))
        link(dve.tensor_tensor(stat[:, 8:10], stat[:, 8:10], stat[:, 10:12], ALU.mult))
        dst = x_sb if first else h2
        for tt in range(TT):
            dve.tensor_scalar(dst[:, tt, :], x_sb[:, tt, :], stat[:, 8 + tt:9 + tt], None, ALU.mult).then_inc(S(nm + "_x"), 1)

    def turn_pe(pe, src, ready, n_ready, pre):
        pe.wait_ge(S("const_b"), 16)
        pe.wait_ge(S(ready), n_ready)
        for b in range(8):
            if b >= 4:
                pe.wait_ge(S(pre + "_hi"), V(pre + "_hi") + 2 * (b - 4) + 2)
                if pre != "r":
                    pe.wait_ge(S(pre + "_lo"), 2 * (b - 4) + 2)
            for k in range(2):
                for tt in range(TT):
                    kt = 2 * b + k
                    mm = pe.transpose(px[b % 4][:, (k * TT + tt) * P:(k * TT + tt + 1) * P],
                                      src[:, tt, kt * P:(kt + 1) * P], C("ident"))
            mm.then_inc(S(pre + "_turned"), 1)

    def rows_pe(pe):
        pe.wait_ge(S("const_b"), 16)
        pe.wait_ge(S("rows_in"), 48)
        pe.transpose(pj[0][:, 0:16], rows[:, 0, :], C("ident")[0:16, 0:16])
        pe.transpose(pj[0][:, 16:32], rows[:, 1, :], C("ident")[0:16, 0:16])
        pe.transpose(pj[0][:, 32:36], rows[0:4, 2, :], C("ident")[0:4, 0:4]).then_inc(S("rows_turned"), 1)

    def rows_dve(dve, link):
        dve.wait_ge(S("rows_turned"), 1)
        link(dve.tensor_copy(gmix[:], pj[0][:, 0:16]))
        link(dve.tensor_copy(gffn[:], pj[0][:, 16:32]))
        l_, e_, p_ = lb[:, 0, :], lb[:, 1, :], lb[:, 2, :]
        dve.tensor_tensor(l_, pj[0][:, 32:36], gmix[:, 0:4], ALU.bypass) if False else None
        link(dve.tensor_copy(l_, pj[0][:, 32:36]))
        dve.tensor_tensor(l_, l_, l_, ALU.subtract).then_inc(S("lb_sub"), 1)

    def lb_act(act):
        act.wait_ge(S("lb_sub"), 1)
        act.activation(lb[:, 1, :], lb[:, 0, :], ACT.Exp).then_inc(S("lb_exp"), 1)

    def lb_dve(dve, link):
        dve.wait_ge(S("lb_exp"), 1)
        dve.wait_ge(S("lb_sub"), 1)
        link(dve.reciprocal(lb[:, 2, :], lb[:, 1, :]))
        link(dve.tensor_tensor(lb[:, 2, :], lb[:, 2, :], lb[:, 1, :], ALU.mult))
        link(dve.tensor_tensor(lb[:, 2, :], lb[:, 2, :], lb[:, 2, :], ALU.subtract))
        dve.tensor_scalar(lb[:, 3, :], lb[:, 2, :], -1.0, 1.0, ALU.mult, ALU.add).then_inc(S("lb_ready"), 1)

    def nsa_norm_dve1(dve, link):
        dve.wait_ge(S("panel_read"), 3)
        link(dve.tensor_tensor(sq[:, 0:4, :], pn[:, 0:4, :], pn[:, 0:4, :], ALU.mult))
        link(dve.tensor_tensor(sq[:, 4, :], pn[:, 6, :], pn[:, 6, :], ALU.mult))
        dve.tensor_tensor(sq[:, 5, :], pn[:, 8, :], pn[:, 8, :], ALU.mult).then_inc(S("nsa_sq"), 1)

    def nsa_norm_pe(pe):
        pe.wait_ge(S("nsa_sq"), V("nsa_sq") + 1)
        pe.wait_ge(S("h_hi"), KT)
        pe.wait_ge(S("h_lo"), KT)
        for b in range(3):
            mm = pe.matmul(px[b][:], C("halves"), sq[:, 2 * b:2 * b + 2, :].rearrange("p a b -> p (a b)"), start=True, stop=True)
        mm.then_inc(S("nsa_ss"), 1)

    def nsa_norm_dve2(dve, link):
        dve.wait_ge(S("nsa_ss"), V("nsa_ss") + 1)
        for b in range(3):
            dve.tensor_scalar(rr[:, 2 * b:2 * b + 2, :].rearrange("p a b -> p (a b)"), px[b][:], 1.0 / HD, EPS, ALU.mult, ALU.add).then_inc(S("nsa_ms"), 1)

    def nsa_norm_act(act):
        act.wait_ge(S("nsa_ms"), V("nsa_ms") + 3)
        act.activation(rr[:], rr[:], ACT.Sqrt).then_inc(S("nsa_sd"), 1)

    def nsa_norm_dve3(dve, link):
        dve.wait_ge(S("nsa_sd"), V("nsa_sd") + 1)
        dve.wait_ge(S("nsa_zero"), 1)
        link(dve.reciprocal(rr[:], rr[:]))
        link(dve.tensor_scalar(ngain[:, 0:1], ngain[:, 0:1], HD ** -0.5, None, ALU.mult))
        dve.scalar_tensor_tensor(pn[:, 0:4, :], pn[:, 0:4, :], ngain[:, 0:1], rr[:, 0:4, :], ALU.mult, ALU.mult).then_inc(S("nsa_qk"), 1)
        for ty in range(2):
            for g in range(KV):
                r = slice(g * HD, (g + 1) * HD)
                dve.scalar_tensor_tensor(kz[r, ty, g, :], pn[r, 6 + 2 * ty, :], ngain[r, 2 + ty:3 + ty], rr[r, 4 + ty, :], ALU.mult, ALU.mult).then_inc(S("nsa_qk"), 1)
        dve.wait_ge(S("nsa_qk"), V("nsa_qk") + 5)

    def nsa_zero_pool(pool):
        pool.wait_ge(S("h_lo"), KT)
        pool.memset(kz[:], 0.0).then_inc(S("nsa_z"), 1)
        pool.memset(vz[:], 0.0).then_inc(S("nsa_z"), 1)
        pool.memset(kcz[:], 0.0).then_inc(S("nsa_z"), 1)
        pool.wait_ge(S("nsa_z"), 3)
        pool.memset(zr[:], 0.0).then_inc(S("nsa_zero"), 1)

    def nsa_turn_pe(pe):
        pe.wait_ge(S("nsa_ms"), V("nsa_ms") + 3)
        for ty in range(2):
            for kt in range(TT):
                pe.transpose(px[3][:, (ty * TT + kt) * P:(ty * TT + kt + 1) * P], pn[:, 7 + 2 * ty, kt * P:(kt + 1) * P], C("ident"))
        for tt in range(TT):
            pe.transpose(px[2][:, tt * P:(tt + 1) * P], pn[:, 10, tt * P:(tt + 1) * P], C("ident"))
        pe.wait_ge(S("small_in"), SMALL_IN)
        pe.transpose(px[0][:, 0:64], pe2[:], C("ident")[0:64, 0:64]).then_inc(S("nsa_turned"), 1)

    def nsa_turn_dve(dve, link):
        dve.wait_ge(S("nsa_turned"), V("nsa_turned") + 1)
        v4 = px[3][:].rearrange("p (y k c) -> p y k c", y=2, k=TT)
        for g in range(KV):
            c = slice(g * HD, (g + 1) * HD)
            link(dve.tensor_copy(vz[:, :, :, g, c].rearrange("p k y c -> p y k c"), v4[:, :, :, c]))
        for v in range(2):
            kc = pn[:, 4 + v, :].rearrange("p (n l) -> p l n", l=16)
            link(dve.tensor_copy(ax[:, v, 0:16, 0:15], kc[:, :, 0:15]))
            link(dve.tensor_copy(ax[:, v, 16:32, 0:15], kc[:, :, 1:16]))
            link(dve.tensor_copy(ax[:, v, :, 15], px[0][:, v * 32:(v + 1) * 32]))
        dve.memset(vcb[:], 0.0).then_inc(S("cmp_in"), 1)
        dve.wait_ge(S("cmp_in"), V("cmp_in") + 1)

    def nsa_gate_act(act):
        act.wait_ge(S("nsa_turned"), V("nsa_turned") + 1)
        act.activation(gate[:], px[2][:, 0:2 * P].rearrange("p (a b) -> p a b", a=TT)[:, :, 0:24], ACT.Sigmoid).then_inc(S("nsa_gates"), 1)

    def cmp1_pe(pe, v, part):
        if v == 0 and part == 0:
            pe.wait_ge(S("cmp_in"), V("cmp_in") + 1)
            pe.wait_ge(S("w1_in"), 64)
            pe.wait_ge(S("nsa_gates"), V("nsa_gates") + 1)
        for l in range(part * 8, part * 8 + 8):
            for g in range(KV):
                r = slice(g * HD, (g + 1) * HD)
                mm = pe.matmul(px[2 * v + g][r, 0:16], w1[r, v, l, :], ax[r, v, l, :], start=l == 0, stop=l == 31)
        if part == 3:
            mm.then_inc(S("cmp_h"), 1)

    def cmp_dve1(dve, link):
        for v in range(2):
            dve.wait_ge(S("cmp_h"), V("cmp_h") + v + 1)
            for g in range(KV):
                r = slice(g * HD, (g + 1) * HD)
                dve.tensor_copy(hid[r, 0, v, :], px[2 * v + g][r, 0:16]).then_inc(S("cmp_hidden"), 1)
        dve.wait_ge(S("cmp_hidden"), V("cmp_hidden") + 4)
        z, a2, u = hid[:, 1], hid[:, 2], hid[:, 3]
        link(dve.memset(hid[:, 1:6], 0.0))
        for v in range(2):
            link(dve.tensor_scalar(hid[:, 1, v, 0:15], hid[:, 0, v, 0:15], hid[:, 0, v, 15:16], None, ALU.add))
        link(dve.tensor_tensor(a2, z, z, ALU.mult))
        link(dve.tensor_scalar(a2, a2, 0.044715, 1.0, ALU.mult, ALU.add))
        dve.tensor_tensor(u, z, a2, ALU.mult).then_inc(S("cmp_u"), 1)
        dve.wait_ge(S("cmp_u"), V("cmp_u") + 1)

    def cmp_act1(act):
        act.wait_ge(S("cmp_u"), V("cmp_u") + 1)
        act.activation(hid[:, 4], hid[:, 3], ACT.Sigmoid, scale=2.0 * 0.7978845608028654).then_inc(S("cmp_s"), 1)

    def cmp_dve2(dve, link):
        dve.wait_ge(S("cmp_s"), V("cmp_s") + 1)
        dve.tensor_tensor(hid[:, 5], hid[:, 1], hid[:, 4], ALU.mult).then_inc(S("cmp_g"), 1)

    def cmp2_pe(pe):
        pe.wait_ge(S("cmp_g"), V("cmp_g") + 1)
        pe.wait_ge(S("cmp_hidden"), V("cmp_hidden") + 4)
        for g in range(KV):
            r = slice(g * HD, (g + 1) * HD)
            pe.matmul(px[g][r, 0:16], w2[r, 0, :], hid[r, 5, 0, :], start=True, stop=True)
            mm = pe.matmul(px[2 + g][0:16, 0:HD], hid[r, 5, 1, :], w2[r, 1, :], start=True, stop=True)
        mm.then_inc(S("cmp_kv"), 1)

    def cmp_dve3(dve, link):
        dve.wait_ge(S("cmp_kv"), V("cmp_kv") + 1)
        for g in range(KV):
            r = slice(g * HD, (g + 1) * HD)
            link(dve.tensor_copy(kct[r, 0, :], px[g][r, 0:16]))
            dve.tensor_copy(vcs[:, g, :], px[2 + g][0:16, 0:HD]).then_inc(S("cmp_v"), 1)
        dve.tensor_tensor(kct[:, 1, :], kct[:, 0, :], kct[:, 0, :], ALU.mult).then_inc(S("cmp_sq"), 1)

    def cmp_v_dma(act):
        act.wait_ge(S("cmp_v"), V("cmp_v") + 2)
        for i in range(4):
            for g in range(KV):
                act.dma_start(vcb[(2 * i + g) * 16:(2 * i + g + 1) * 16, i, g * HD:(g + 1) * HD], vcs[:, g, :]).then_inc(S("vcb_in"), 16)

    def cmp3_pe(pe):
        pe.wait_ge(S("cmp_sq"), V("cmp_sq") + 1)
        pe.matmul(px[0][:, 0:16], C("halves"), kct[:, 1, :], start=True, stop=True).then_inc(S("cmp_ss"), 1)

    def cmp_dve4(dve, link):
        dve.wait_ge(S("cmp_ss"), V("cmp_ss") + 1)
        dve.tensor_scalar(kct[:, 2, :], px[0][:, 0:16], 1.0 / HD, EPS, ALU.mult, ALU.add).then_inc(S("cmp_ms"), 1)

    def cmp_act2(act):
        act.wait_ge(S("cmp_ms"), V("cmp_ms") + 1)
        act.activation(kct[:, 2, :], kct[:, 2, :], ACT.Sqrt).then_inc(S("cmp_sd"), 1)

    def cmp_dve5(dve, link):
        dve.wait_ge(S("cmp_sd"), V("cmp_sd") + 1)
        link(dve.reciprocal(kct[:, 3, :], kct[:, 2, :]))
        for g in range(KV):
            r = slice(g * HD, (g + 1) * HD)
            dve.scalar_tensor_tensor(kcz[r, g, :], kct[r, 0, :], ngain[r, 1:2], kct[r, 3, :], ALU.mult, ALU.mult).then_inc(S("cmp_k"), 1)

    def cmp4_pe(pe):
        pe.wait_ge(S("cmp_k"), V("cmp_k") + 2)
        pe.wait_ge(S("nsa_qk"), V("nsa_qk") + 5)
        for tt in range(TT):
            for i in range(4):
                mm = pe.matmul(px[1][:, tt * P + i * 32:tt * P + (i + 1) * 32], pn[:, i, tt * P:(tt + 1) * P],
                               kcz[:].rearrange("p a b -> p (a b)"), start=True, stop=True)
        mm.then_inc(S("cmp_scores"), 1)

    def cmp_dve6(dve, link):
        dve.wait_ge(S("cmp_scores"), V("cmp_scores") + 1)
        link(dve.tensor_tensor(csc[:], px[1][:, 0:256], C("cbias"), ALU.add))
        s3 = csc[:].rearrange("p (h n) -> p h n", n=16)
        link(dve.tensor_reduce(cs[:, 0, :], s3, AX.X, ALU.max))
        dve.tensor_tensor(s3, s3, cs[:, 0, :].unsqueeze(2).to_broadcast([P, 16, 16]), ALU.subtract).then_inc(S("cmp_sub"), 1)

    def cmp_act3(act):
        act.wait_ge(S("cmp_sub"), V("cmp_sub") + 1)
        act.activation(csc[:], csc[:], ACT.Exp).then_inc(S("cmp_exp"), 1)

    def cmp_dve7(dve, link):
        dve.wait_ge(S("cmp_exp"), V("cmp_exp") + 1)
        dve.wait_ge(S("nsa_gates"), V("nsa_gates") + 1)
        s3 = csc[:].rearrange("p (h n) -> p h n", n=16)
        link(dve.tensor_reduce(cs[:, 1, :], s3, AX.X, ALU.add))
        link(dve.reciprocal(cs[:, 2, :], cs[:, 1, :]))
        link(dve.tensor_tensor(cs[:, 3, :].rearrange("p (t i g) -> p t i g", t=TT, i=4), cs[:, 2, :].rearrange("p (t i g) -> p t i g", t=TT, i=4),
                               gate[:, :, 0:8].rearrange("p t (g i) -> p t i g", g=2), ALU.mult))
        link(dve.tensor_tensor(s3, s3, cs[:, 3, :].unsqueeze(2).to_broadcast([P, 16, 16]), ALU.mult))
        c4 = csc[:].rearrange("p (t h n) -> p t h n", t=TT, n=16)
        dve.tensor_tensor(c4, c4, C("cvis").rearrange("p (t n) -> p t n", t=TT).unsqueeze(2).to_broadcast([P, TT, 8, 16]), ALU.mult).then_inc(S("cmp_p"), 1)

    def cmp5_pe(pe):
        pe.wait_ge(S("cmp_p"), V("cmp_p") + 1)
        pe.wait_ge(S("cmp_sub"), V("cmp_sub") + 1)
        for tt in range(TT):
            mm = pe.transpose(px[2][:, tt * P:(tt + 1) * P], csc[:, tt * P:(tt + 1) * P], C("ident"))
        mm.then_inc(S("cmp_pt"), 1)

    def cmp_dve8(dve, link):
        dve.wait_ge(S("cmp_pt"), V("cmp_pt") + 1)
        dve.tensor_copy(ptc[:].rearrange("p a b -> p (a b)"), px[2][:, 0:256]).then_inc(S("cmp_ptc"), 1)
        dve.wait_ge(S("cmp_ptc"), V("cmp_ptc") + 1)

    AU = [(tt, i, ty) for tt in range(TT) for i in range(4) for ty in range(2)]
    NAU = len(AU)

    def att_scores(pe, m):
        tt, i, ty = AU[m]
        nk = P * (tt + 1)
        if m == 0:
            pe.wait_ge(S("cmp_sub"), V("cmp_sub") + 1)
            pe.wait_ge(S("cmp_ms"), V("cmp_ms") + 1)
        if m >= 2:
            pe.wait_ge(S("att_s"), 2 * (m - 1))
        pe.matmul(px[m % 2][:, 0:2 * nk].rearrange("p (g k) -> p g k", g=2), pn[:, i, tt * P:(tt + 1) * P], kz[:, ty, :, 0:nk], start=True, stop=True).then_inc(S("att_scores"), 1)

    def att_soft1(dve, link, m):
        tt, i, ty = AU[m]
        nk = P * (tt + 1)
        dve.wait_ge(S("att_scores"), m + 1)
        if m >= 2:
            dve.wait_ge(S("att_turned"), m - 1)
        dist = C(f"dist{tt}")
        for g in range(KV):
            dve.scalar_tensor_tensor(sb[:, m % 2, g, 0:nk], dist, -SLOPES[g * 4 + i], px[m % 2][:, g * nk:(g + 1) * nk], ALU.mult, ALU.add).then_inc(S("att_s"), 1)
        dve.wait_ge(S("att_s"), 2 * (m + 1))
        dve.tensor_reduce(am[:, m % 2, 0:2], sb[:, m % 2, :, 0:nk], AX.X, ALU.max, negate=True).then_inc(S("att_max"), 1)

    def att_exp(act, m):
        tt, i, ty = AU[m]
        nk = P * (tt + 1)
        act.wait_ge(S("att_max"), m + 1)
        for g in range(KV):
            act.activation(sb[:, m % 2, g, 0:nk], sb[:, m % 2, g, 0:nk], ACT.Exp, bias=am[:, m % 2, g:g + 1],
                           accum_out=am[:, m % 2, 2 + g:3 + g]).then_inc(S("att_exp"), 1)

    def att_soft2(dve, link, m):
        tt, i, ty = AU[m]
        nk = P * (tt + 1)
        dve.wait_ge(S("att_exp"), 2 * (m + 1))
        link(dve.reciprocal(am[:, m % 2, 4:6], am[:, m % 2, 2:4]))
        g0 = 8 * (1 + ty) + i
        link(dve.tensor_tensor(am[:, m % 2, 6:8], am[:, m % 2, 4:6], gate[:, tt, g0:g0 + 5:4], ALU.mult))
        for g in range(KV):
            dve.tensor_scalar(sb[:, m % 2, g, 0:nk], sb[:, m % 2, g, 0:nk], am[:, m % 2, 6 + g:7 + g], None, ALU.mult).then_inc(S("att_p"), 1)

    def att_turn(pe, m):
        tt, i, ty = AU[m]
        pe.wait_ge(S("att_p"), 2 * (m + 1))
        if m == 0:
            pe.wait_ge(S("cmp_ptc"), V("cmp_ptc") + 1)
        if m >= 1:
            pe.wait_ge(S("att_pt"), m)
        for g in range(KV):
            for kt in range(tt + 1):
                mm = pe.transpose(px[2][:, (g * 2 + kt) * P:(g * 2 + kt + 1) * P], sb[:, m % 2, g, kt * P:(kt + 1) * P], C("ident"))
        mm.then_inc(S("att_turned"), 1)

    def att_pt(dve, link, m):
        tt, i, ty = AU[m]
        dve.wait_ge(S("att_turned"), m + 1)
        if m >= 1:
            dve.wait_ge(S("att_pv"), m)
        else:
            dve.wait_ge(S("nsa_qk"), V("nsa_qk") + 5)
        n = tt + 1
        dve.tensor_copy(pt[:].rearrange("p (g k) c -> p g k c", g=2)[:, :, 0:n, :],
                        px[2][:].rearrange("p (g k c) -> p g k c", g=2, k=2)[:, :, 0:n, :]).then_inc(S("att_pt"), 1)

    def att_pv(pe, m):
        tt, i, ty = AU[m]
        pe.wait_ge(S("att_pt"), m + 1)
        n = m // 2
        dst = px[3][:, 0:P]
        if ty == 0:
            if n == 0:
                pe.wait_ge(S("vcb_in"), 16 * 8)
                pe.wait_ge(S("cmp_v"), V("cmp_v") + 2)
            else:
                pe.wait_ge(S("branch_hi"), n)
                pe.wait_ge(S("branch_lo"), n)
            pe.matmul(dst, vcb[:, i, :], ptc[:, tt, :], start=True, stop=False)
        for g in range(KV):
            for kt in range(tt + 1):
                mm = pe.matmul(dst, vz[:, kt, ty, g, :], pt[:, g * 2 + kt, :], start=False,
                               stop=ty == 1 and g == 1 and kt == tt)
        mm.then_inc(S("att_pv"), 1)

    def att_out_act(act, n):
        tt, i, _ = AU[2 * n]
        act.wait_ge(S("att_pv"), 2 * n + 2)
        act.activation(orr[:, hi, i, tt * P:(tt + 1) * P], px[3][:, 0:P], ACT.Copy).then_inc(S("branch_hi"), 1)

    def att_out_dve(dve, link, n):
        tt, i, _ = AU[2 * n]
        dve.wait_ge(S("att_pv"), 2 * n + 2)
        dve.wait_ge(S("branch_hi"), n + 1)
        dve.tensor_tensor(orr[:, lo, i, tt * P:(tt + 1) * P], px[3][:, 0:P], orr[:, hi, i, tt * P:(tt + 1) * P].bitcast(F32), ALU.subtract).then_inc(S("branch_lo"), 1)
        if n == NAU // 2 - 1:
            dve.wait_ge(S("branch_lo"), n + 1)
            dve.tensor_copy(zr[:, 2:3], zr[:, 3:4]).then_inc(S("att_done"), 1)

    class Rec:

        def __init__(self, which):
            self.w = which
            self.nt = 4 if which == "hg" else 2
            self.q = hgq if which == "hg" else None
            self.base = 0 if which == "hg" else 1
            self.step = 3 if which == "hg" else 2

        def n(self, s):
            return f"{self.w}_{s}"

    HGR, GLR_ = Rec("hg"), Rec("gl")

    def rq(R):
        return hgq[:] if R.w == "hg" else glqk[:, 0:2, :]

    def rk(R):
        return hgk[:] if R.w == "hg" else glqk[:, 2:4, :]

    def hg_act1(act):
        act.wait_ge(S("panel_read"), 5)
        act.wait_ge(S("att_done"), 1)
        act.activation(hgk[:], hgz[:], ACT.Sigmoid, scale=-1.0).then_inc(S("hg_sig"), 1)
        act.activation(hgb[:], hgz[:], ACT.Sigmoid).then_inc(S("hg_sig"), 1)

    def hg_act2(act):
        act.wait_ge(S("panel_read"), 7)
        act.activation(hgg[:], hgg[:], ACT.Sigmoid).then_inc(S("hg_gate"), 1)

    def gl_act2(act):
        act.wait_ge(S("panel_read"), PI["gl_r"] + 1)
        act.wait_ge(S("hg_bdone"), 1)
        act.activation(hgi[:], glr[:], ACT.Sigmoid).then_inc(S("gl_gate"), 1)

    def hg_dve1(dve, link):
        dve.wait_ge(S("hg_sig"), 2)
        dve.wait_ge(S("lb_ready"), 1)
        for h in range(4):
            link(dve.tensor_scalar(hgk[:, h, :], hgk[:, h, :], lb[:, 3, h:h + 1], None, ALU.mult))
            link(dve.tensor_scalar(hgb[:, h, :], hgb[:, h, :], lb[:, 3, h:h + 1], lb[:, 2, h:h + 1], ALU.mult, ALU.add))
        link(dve.tensor_scalar(zb0[:], hgb[:], 2.0 ** -60, None, ALU.max))
        link(dve.tensor_scalar(zb1[:], hgb[:], TINY, 2.0 ** 60, ALU.max, ALU.mult))
        dve.tensor_scalar(zb1[:], zb1[:], 1.0, None, ALU.min).then_inc(S("hg_f"), 1)
        dve.wait_ge(S("hg_f"), 1)

    def hg_act3(act):
        act.wait_ge(S("hg_f"), 1)
        act.activation(zb0[:], zb0[:], ACT.Ln).then_inc(S("hg_ln"), 1)
        act.activation(zb1[:], zb1[:], ACT.Ln).then_inc(S("hg_ln"), 1)

    def f2(ap):
        return ap.rearrange("p a b -> p (a b)")

    def hg_dve2(dve, link):
        dve.wait_ge(S("hg_ln"), 2)
        link(dve.tensor_tensor(wbuf[:], zb0[:], zb1[:], ALU.add))
        dve.tensor_tensor_scan(f2(hgb[:]), C("reset"), f2(wbuf[:]), 0.0, ALU.mult, ALU.add).then_inc(S("hg_b"), 1)
        dve.wait_ge(S("hg_b"), 1)

    def gl_pe1(pe):
        pe.wait_ge(S("panel_read"), PI["gl_a"] + 1)
        pe.wait_ge(S("hg_bdone"), 1)
        for a in range(2):
            mm = pe.matmul(px[0][:, a * T:(a + 1) * T], wa2[:, a * P:(a + 1) * P], gla[0:16, :], start=True, stop=True)
        mm.then_inc(S("gl_logit"), 1)

    glx = [wbuf[:, 0:2, :], wbuf[:, 2:4, :], hgk[:, 0:2, :], hgk[:, 2:4, :]]

    def gl_dve1(dve, link):
        dve.wait_ge(S("gl_logit"), 1)
        dve.wait_ge(S("hg_bdone"), 1)
        for a in range(2):
            link(dve.tensor_scalar(glx[0][:, a, :], px[0][:, a * T:(a + 1) * T], bal[:, a:a + 1], None, ALU.add))
        link(dve.tensor_scalar(glx[1], glx[0], -1.0, None, ALU.mult))
        link(dve.tensor_tensor(glx[1], glx[1], glx[0], ALU.min))
        dve.tensor_scalar(glx[0], glx[0], 0.0, None, ALU.min).then_inc(S("gl_u"), 1)
        dve.wait_ge(S("gl_u"), 1)

    def gl_act1(act):
        act.wait_ge(S("gl_u"), 1)
        act.activation(glx[1], glx[1], ACT.Exp).then_inc(S("gl_e"), 1)
        act.wait_ge(S("gl_e"), 1)
        act.activation(glx[1], glx[1], ACT.Ln, bias=1.0).then_inc(S("gl_ln"), 1)

    def gl_dve2(dve, link):
        dve.wait_ge(S("gl_ln"), 1)
        link(dve.tensor_tensor(glx[2], glx[0], glx[1], ALU.subtract))
        link(dve.tensor_scalar(glx[2], glx[2], 1.0 / 16.0, None, ALU.mult))
        link(dve.tensor_scalar(glqk[:, 0:2, :], glqk[:, 0:2, :], HD ** -0.5, None, ALU.mult))
        dve.tensor_tensor_scan(f2(hgb[:, 0:2, :]), C("reset")[:, 0:2 * T], f2(glx[2]), 0.0, ALU.mult, ALU.add).then_inc(S("gl_b"), 1)
        dve.wait_ge(S("gl_b"), 1)

    def zero_st(pool, R):
        if R.w == "hg":
            pool.wait_ge(S("att_done"), 1)
        else:
            pool.wait_ge(S("hg_bdone"), 1)
            pool.wait_ge(S("hg_o"), 2)
        pool.memset(st[:], 0.0).then_inc(S(R.n("zero")), 1)

    zbs = [zb0, zb1]

    def lev_x(dve, link, R, l):
        s_ = 1 << (l - 1)
        nt = R.nt
        if l >= 2:
            dve.wait_ge(S(R.n("z")), 2 * (l - 1))
        b = hgb[:, 0:nt, :]
        x_ = wbuf[:, 0:nt, :]
        if l < NL:
            nb = nt * T // (2 * s_)
            b4 = f2(b).rearrange("p (n h s) -> p n h s", h=2, s=s_)
            x4 = f2(x_).rearrange("p (n h s) -> p n h s", h=2, s=s_)
            mid = b4[:, :, 0, s_ - 1:s_].to_broadcast([P, nb, s_])
            dve.tensor_tensor(x4[:, :, 1, :], b4[:, :, 1, :], mid, ALU.subtract if s_ < CHUNK else ALU.bypass).then_inc(S(R.n("x")), 1) if s_ < CHUNK else \
                dve.tensor_copy(x4[:, :, 1, :], b4[:, :, 1, :]).then_inc(S(R.n("x")), 1)
            dve.tensor_tensor(x4[:, :, 0, :], mid, b4[:, :, 0, :], ALU.subtract).then_inc(S(R.n("x")), 1)
        else:
            b4 = b.rearrange("p n (c s) -> p n c s", c=4)
            x4 = x_.rearrange("p n (c s) -> p n c s", c=4)

            def end(c):
                return b4[:, :, c, CHUNK - 1:CHUNK].to_broadcast([P, nt, CHUNK])
            link(dve.tensor_tensor(x4[:, :, 0, :], end(0), b4[:, :, 0, :], ALU.subtract))
            link(dve.tensor_tensor(x4[:, :, 0, :], x4[:, :, 0, :], end(1), ALU.add))
            link(dve.tensor_tensor(x4[:, :, 1, :], end(1), b4[:, :, 1, :], ALU.subtract))
            dve.tensor_copy(x4[:, :, 2, :], b4[:, :, 2, :]).then_inc(S(R.n("x")), 1)
            dve.tensor_tensor(x4[:, :, 3, :], b4[:, :, 3, :], end(2), ALU.add).then_inc(S(R.n("x")), 1)

    def lev_exp(act, R, l):
        act.wait_ge(S(R.n("x")), 2 * l)
        act.activation(wbuf[:, 0:R.nt, :], wbuf[:, 0:R.nt, :], ACT.Exp).then_inc(S(R.n("w")), 1)

    def lev_z(dve, link, R, l):
        s_ = 1 << (l - 1)
        nt = R.nt
        dve.wait_ge(S(R.n("w")), l)
        if l >= 3:
            dve.wait_ge(S(R.n("sc")), l - 1)
        elif R.w == "gl":
            dve.wait_ge(S("hg_sc"), NL + 1)
        z = zbs[l % 2][:, 0:nt, :]
        x_ = wbuf[:, 0:nt, :]
        v = lambda a: f2(a).rearrange("p (n h s) -> p n h s", h=2, s=s_)
        if l == NL:
            v = lambda a: a.rearrange("p n (h s) -> p n h s", h=2)
        dve.tensor_tensor(v(z)[:, :, 0, :], v(x_)[:, :, 0, :], v(rk(R))[:, :, 0, :], ALU.mult).then_inc(S(R.n("z")), 1)
        dve.tensor_tensor(v(z)[:, :, 1, :], v(x_)[:, :, 1, :], v(rq(R))[:, :, 1, :], ALU.mult).then_inc(S(R.n("z")), 1)

    def head(R, a, h, tt):
        if R.w == "hg":
            return a[:, h, tt * P:(tt + 1) * P]
        return a[(h % 2) * HD:(h % 2 + 1) * HD, h // 2, tt * P:(tt + 1) * P]

    def place(R, h, tt):
        return (tt, h) if R.w == "hg" else (h % 2, 2 * tt + h // 2)

    def lev_pe(pe, R, l):
        if l == 0:
            pe.wait_ge(S(R.n("b")), 1)
            if R.w == "hg":
                pe.wait_ge(S("att_pt"), NAU)
                pe.wait_ge(S("branch_lo"), 8)
                pe.wait_ge(S("branch_hi"), 8)
            else:
                pe.wait_ge(S("gl_u"), 1)
                pe.wait_ge(S("branch_hi"), 16)
                pe.wait_ge(S("branch_lo"), 16)
        else:
            pe.wait_ge(S(R.n("z")), 2 * l)
        if l >= 2:
            pe.wait_ge(S(R.n("st")), l - 1)
        z = zbs[l % 2]
        if l < NL:
            for tt in range(TT):
                for h in range(4):
                    a = head(R, rk(R) if l == 0 else z, h, tt)
                    b = head(R, rq(R) if l == 0 else z, h, tt)
                    bk, at_ = place(R, h, tt)
                    mm = pe.matmul(px[2 * (l % 2) + bk][:, at_ * P:(at_ + 1) * P], a, b, start=True, stop=True)
        else:
            for h in range(4):
                bk, at_ = (0, h) if R.w == "hg" else (h % 2, h // 2)
                mm = pe.matmul(px[2 * (l % 2) + bk][:, at_ * P:(at_ + 1) * P], head(R, z, h, 0), head(R, z, h, 1), start=True, stop=True)
        mm.then_inc(S(R.n("sc")), 1)

    def lev_st(dve, link, R, l):
        dve.wait_ge(S(R.n("sc")), l + 1)
        if l == 0:
            dve.wait_ge(S(R.n("zero")), 1)
        if l < NL:
            mk = C("levels")[:, l * P:(l + 1) * P].bitcast(U32).unsqueeze(1).to_broadcast([P, 4, P])
            for tt in range(TT):
                ins = dve.copy_predicated(st[:, 4 * tt:4 * tt + 4, :], mk, px[2 * (l % 2) + tt][:].rearrange("p (h c) -> p h c", h=4))
                if tt == 0:
                    link(ins)
            ins.then_inc(S(R.n("st")), 1)
        else:
            if R.w == "hg":
                ins = dve.tensor_copy(f2(st2[:]), px[2 * (l % 2)][:])
            else:
                for bk in range(2):
                    ins = dve.tensor_copy(st2[:].rearrange("p (a b) c -> p b a c", b=2)[:, bk, :, :],
                                          px[2 * (l % 2) + bk][:, 0:2 * P].rearrange("p (a c) -> p a c", a=2))
            ins.then_inc(S(R.n("st")), 1)
        dve.wait_ge(S(R.n("st")), l + 1)

    def rec_out(pe, R):
        v = hgi if R.w == "hg" else glv
        pe.wait_ge(S(R.n("st")), NL + 1)
        if R.w == "gl":
            pe.wait_ge(S("panel_read"), PI["gl_v"] + 1)
        for tt in range(TT):
            for h in range(4):
                dst = px[2 + tt][:, h * P:(h + 1) * P]
                vs = lambda k: v[:, k, h * P:(h + 1) * P]
                bk, at_ = place(R, h, tt)
                mm = pe.matmul(dst, st[:, 4 * bk + at_, :], vs(tt), start=True, stop=tt == 0)
                if tt == 1:
                    mm = pe.matmul(dst, st2[:, h, :], vs(0), start=False, stop=True)
            mm.then_inc(S(R.n("o")), 1)

    def out_dve1(dve, link, R):
        ob = [wbuf[:, 0:2, :], wbuf[:, 2:4, :]]
        for tt in range(TT):
            dve.wait_ge(S(R.n("o")), tt + 1)
            link(dve.tensor_copy(f2(ob[tt]), px[2 + tt][:]))
            link(dve.tensor_tensor(f2(zb0[:, 2 * tt:2 * tt + 2, :]), f2(ob[tt]), f2(ob[tt]), ALU.mult))
        link(dve.tensor_reduce(cs[:, 0, 0:8], f2(zb0[:]).rearrange("p (h d) -> p h d", d=P), AX.X, ALU.add))
        dve.tensor_scalar(cs[:, 1, 0:8], cs[:, 0, 0:8], 1.0 / P, EPS, ALU.mult, ALU.add).then_inc(S(R.n("ms")), 1)

    def out_act(act, R):
        act.wait_ge(S(R.n("ms")), 1)
        act.activation(cs[:, 2, 0:8], cs[:, 1, 0:8], ACT.Sqrt).then_inc(S(R.n("sd")), 1)

    def out_dve2(dve, link, R):
        dve.wait_ge(S(R.n("sd")), 1)
        dve.wait_ge(S(R.n("gate")), 1)
        link(dve.reciprocal(cs[:, 3, 0:8], cs[:, 2, 0:8]))
        w3 = f2(wbuf[:]).rearrange("p (h d) -> p h d", d=P)
        link(dve.tensor_tensor(w3, w3, cs[:, 3, 0:8].unsqueeze(2).to_broadcast([P, 8, P]), ALU.mult))
        gn = hgain if R.w == "hg" else ggain
        link(dve.tensor_tensor(w3, w3, gn[:].unsqueeze(1).to_broadcast([P, 8, P]), ALU.mult))
        g = hgg if R.w == "hg" else hgi
        if R.w == "gl":
            link(dve.tensor_tensor(f2(wbuf[:]), f2(wbuf[:]), f2(glr[:]), ALU.mult))
        dve.tensor_tensor(f2(wbuf[:]), f2(wbuf[:]), f2(g[:]), ALU.mult).then_inc(S(R.n("on")), 1)

    def out_turn(pe, R):
        pe.wait_ge(S(R.n("on")), 1)
        w3 = f2(wbuf[:])
        for tt in range(TT):
            for h in range(4):
                mm = pe.transpose(px[h // 2][:, (h % 2) * T + tt * P:(h % 2) * T + (tt + 1) * P], w3[:, (tt * 4 + h) * P:(tt * 4 + h + 1) * P], C("ident"))
        mm.then_inc(S(R.n("ot")), 1)

    def out_hi(act, R):
        act.wait_ge(S(R.n("ot")), 1)
        n = 4 * (R.base + 1)
        for h in range(2):
            act.activation(f2(orr[:, hi, n + 2 * h:n + 2 * h + 2, :]), px[h][:], ACT.Copy).then_inc(S("branch_hi"), 4)

    def out_lo(dve, link, R):
        n = 4 * (R.base + 1)
        for h in range(2):
            dve.wait_ge(S("branch_hi"), 8 * (R.base + 1) + 4 * (h + 1))
            dve.tensor_tensor(f2(orr[:, lo, n + 2 * h:n + 2 * h + 2, :]), px[h][:], f2(orr[:, hi, n + 2 * h:n + 2 * h + 2, :]).bitcast(F32), ALU.subtract).then_inc(S("branch_lo"), 4)
        if R.w == "hg":
            dve.wait_ge(S("branch_lo"), 16)
            dve.tensor_copy(zr[:, 4:5], zr[:, 5:6]).then_inc(S("hg_bdone"), 1)
            dve.wait_ge(S("hg_bdone"), 1)

    LAG = 3
    put("dve", A0 - 2, nsa_norm_dve1)
    put("pool", 18, nsa_zero_pool)
    put("pe", A0, nsa_norm_pe)
    put("dve", A0, nsa_norm_dve2)
    put("act", A0 + LAG, nsa_norm_act)
    put("dve", A0 + 1, nsa_norm_dve3)
    put("pe", CM, nsa_turn_pe)
    put("dve", CM, nsa_turn_dve)
    put("act", CM + LAG, nsa_gate_act)
    for v in range(2):
        for part in range(4):
            put("pe", CM + 4 + 4 * v + part, cmp1_pe, v, part)
    put("dve", CM + 11, cmp_dve1)
    put("act", CM + 11 + LAG, cmp_act1)
    put("dve", CM + 11, cmp_dve2)
    put("pe", CM + 16, cmp2_pe)
    put("dve", CM + 16, cmp_dve3)
    put("act", CM + 16 + LAG, cmp_v_dma)
    put("pe", CM + 18, cmp3_pe)
    put("dve", CM + 18, cmp_dve4)
    put("act", CM + 18 + LAG, cmp_act2)
    put("dve", CM + 18, cmp_dve5)
    put("pe", CM + 23, cmp4_pe)
    put("dve", CM + 23, cmp_dve6)
    put("act", CM + 23 + LAG, cmp_act3)
    put("dve", CM + 23, cmp_dve7)
    put("pe", CM + 28, cmp5_pe)
    put("dve", CM + 28, cmp_dve8)
    for m in range(NAU + 4):
        pos = AT0 + 2 * m
        if m < NAU:
            put("pe", pos, att_scores, m)
            put("dve", pos, att_soft1, m)
            put("act", pos + LAG, att_exp, m)
        if 1 <= m <= NAU:
            put("dve", pos, att_soft2, m - 1)
        if 2 <= m < NAU + 2:
            put("pe", pos, att_turn, m - 2)
            put("dve", pos, att_pt, m - 2)
        if 3 <= m < NAU + 3:
            put("pe", pos, att_pv, m - 3)
            if (m - 3) % 2 == 1:
                put("act", pos + LAG, att_out_act, (m - 3) // 2)
                put("dve", pos + 1, att_out_dve, (m - 3) // 2)

    def rec_sched(R, r0):
        put("pool", r0, zero_st, R)
        for l in range(NL + 1):
            pos = r0 + 6 + R.step * l
            put("pe", pos, lev_pe, R, l)
            if l >= 1:
                put("dve", pos - R.step, lev_x, R, l)
                put("act", pos - R.step + LAG, lev_exp, R, l)
                put("dve", pos - R.step, lev_z, R, l)
            put("dve", pos, lev_st, R, l)
        e = r0 + 6 + R.step * (NL + 1)
        put("pe", e, rec_out, R)
        put("dve", e, out_dve1, R)
        put("act", e + LAG, out_act, R)
        put("dve", e, out_dve2, R)
        put("pe", e + 5, out_turn, R)
        put("act", e + 5 + LAG, out_hi, R)
        put("dve", e + 5, out_lo, R)
        return e + 9

    put("act", HG0 + 1, hg_act1)
    put("act", HG0 + 1, hg_act2)
    put("dve", HG0 + 1, hg_dve1)
    put("act", HG0 + 3, hg_act3)
    put("dve", HG0 + 1, hg_dve2)
    e_hg = rec_sched(HGR, HG0 + 4)
    G = e_hg
    put("act", G + 3, gl_act2)
    put("pe", G, gl_pe1)
    put("dve", G, gl_dve1)
    put("act", G + 3, gl_act1)
    put("dve", G, gl_dve2)
    e_gl = rec_sched(GLR_, G + 4)
    assert e_gl <= UB + 3, (e_gl, UB)

    block = nc.Block()
    block.__enter__()

    NOV = small("nov", [1, 20], I32)

    gu_items = [None]

    rt_off = [RT]

    def rt(name, shape, dt=F32):
        n = (4 * int(np.prod(shape[1:])) + 31) // 32 * 32
        t_ = at(name, shape, rt_off[0], dt)
        rt_off[0] += n
        return t_
    assert RT + 4 * K <= WR_AT + 24 * K
    brt = rt("brt", [P, NROUTE])
    lg = rt("lg", [P, TT, NROUTE])
    gl8 = rt("gl8", [P, TT, 8])
    elm = rt("elm", [P, TT, NE])
    mx8 = rt("mx8", [P, TT, 2, 8])
    ix8 = rt("ix8", [P, TT, 2, 8], U32)
    ixf = rt("ixf", [P, TT, 4])
    ohg = rt("ohg", [P, NG])
    ex8 = rt("ex8", [P, TT, 2, 8])
    rs = rt("rs", [P, TT, 8])
    rt_b = rt_off[0]
    RB = MX
    rb_off = [RB]

    def rb(name, shape, dt=F32):
        n = (4 * int(np.prod(shape[1:])) + 31) // 32 * 32
        t_ = at(name, shape, rb_off[0], dt)
        rb_off[0] += n
        assert rb_off[0] <= MX + 28 * K
        return t_
    ek = rb("ek", [P, TT, 2, NE])
    e12 = rb("e12", [P, TT, NE])
    rank = rb("rank", [P, TT, NE])
    cnt = rb("cnt", [P, NE])
    fl = rb("fl", [P, TT, NE])
    tmp = rb("tmp", [P, TT, NE])
    xtra = rb("xtra", [P, NE])
    base = rb("base", [P, NE])
    item = rb("item", [P, TT, NE])
    pos_ = rb("pos_", [P, TT, NE])
    sel = rb("sel", [P, TT, 2, 4])
    ohp = rb("ohp", [P, TT, 2, P])
    val = rb("val", [P, TT, 2, 3, ITEMS])
    oh48 = rb("oh48", [P, ITEMS])
    tab = rb("tab", [P, 3, ITEMS])
    tabi = rb("tabi", [P, 2, ITEMS], I32)
    oe = rb("oe", [P, 4, NE])
    oe32 = rb("oe32", [32, 2, 32])
    zx = rb("zx", [P, ITEMS])
    idx = rb("idx", [P, 2, 2], I32)
    wcol = rb("wcol", [P, 2])

    def gate_load(sp, b):
        sp.wait_ge(S("gates_out0"), 16 * 6)
        sp.wait_ge(S("gates_out1"), 16 * 6)
        if b >= 2:
            sp.wait_ge(S("gate_used"), b - 1)
        else:
            sp.wait_ge(S("branch_lo"), 24)
            sp.wait_ge(S("branch_hi"), 24)
        sp.dma_start(gsb[:, b % 2, :], gates_d[b]).then_inc(S(f"gate_in{b % 2}"), 16)

    def item_loop(e, body, unroll):
        with e.Fori(0, NE) as n:
            body(n)
        e.wait_ge(S("overflow_known"), V("overflow_known") + 1)
        nov = e.value_load(NOV[0:1, 0:1], min_val=0, max_val=OVER)
        with e.If(nov > 0):
            with e.Fori(0, nov) as m:
                body(m + NE)
        return nov

    @block.sync
    def _(sp):
        consts_loads(sp)
        for k_ in range(3):
            load_slot(sp, k_)
        small_loads(sp)
        sp.wait_ge(S("h_turned"), 8)
        sp.wait_ge(S("h_lo"), KT)
        for v in range(2):
            for half in range(2):
                sp.dma_start(w1[half * HD:(half + 1) * HD, v, :, :], i_["cmp_w1"][0, v].rearrange("(l d) c -> d l c", d=HD)).then_inc(S("w1_in"), 16)
        for k_ in range(3, len(slots)):
            pi, s_, _, _ = slots[k_]
            key = panels[pi]["key"]
            load_slot(sp, k_)
            old = panels[pi - 2]["key"] if pi >= 2 and s_ == len(panels[pi]["src"]) - 1 else ""
            if old.startswith("mg"):
                c = int(old[2:])
                sp.wait_ge(S("panel_read"), pi - 1)
                sp.dma_start(gates_d[c], stage(c)).then_inc(S(f"gates_out{c % 2}"), 16)
            if key.startswith("br"):
                b = int(key[2]) * 4 + int(key[3])
                if b >= 2:
                    gate_load(sp, b - 2)
            if k_ == len(slots) - 8:
                gate_load(sp, 10)
                gate_load(sp, 11)
                sp.wait_ge(S("branch_lo"), 24)
                sp.dma_start(x_sb[:], i_["x"][0].rearrange("(a p) d -> p a d", p=P)).then_inc(S("x_in"), 16)
        sp.wait_ge(S("unit_done"), NU)
        sp.dma_start(wro[:, :, 0:NG], i_["w_grp"][0].rearrange("(k p) c -> p k c", p=P)).then_inc(S("router_in"), 16)
        sp.dma_start(wro[:, :, NG:NROUTE], i_["w_exp"][0].rearrange("(k p) c -> p k c", p=P)).then_inc(S("router_in"), 16)
        sp.dma_start(brt[:, 0:NG], i_["b_grp"].broadcast_to([P, NG])).then_inc(S("router_in"), 16)
        sp.dma_start(brt[:, NG:NROUTE], i_["b_exp"].broadcast_to([P, NE])).then_inc(S("router_in"), 16)

        def expert(e, n, wait):
            for s_ in range(6):
                if wait:
                    sp.wait_ge(S(f"used{s_}"), n)
                if s_ < 4:
                    src = gexp_w[bass.ds(e, 1), s_ * 512:(s_ + 1) * 512, :].rearrange("e (k p) c -> p (e k) c", p=P)
                    dst = RING[:, s_, :].rearrange("p (k c) -> p k c", k=4)
                else:
                    src = down_w[bass.ds(e, 1), (s_ - 4) * 256:(s_ - 3) * 256, :].rearrange("e (k p) c -> p (e k) c", p=P)
                    dst = RING[:, s_, :].rearrange("p (k c) -> p k c", k=2)
                sp.dma_start(dst, src).then_inc(S(f"expert{s_}"), 16)
        sp.wait_ge(S("panel_read"), FIRST_O)
        sp.wait_ge(S("m_lo"), KT)
        expert(0, 0, False)
        sp.wait_ge(S("n2_x"), 2)
        for tt in range(TT):
            sp.dma_start(h2_d[tt * 512:(tt + 1) * 512, :].rearrange("(p q) c -> p (q c)", q=4), h2[:, tt, :]).then_inc(S("h2_out"), 16)
        with sp.Fori(1, NE) as e:
            expert(e, e, True)
        sp.wait_ge(S("overflow_known"), V("overflow_known") + 1)
        nov = sp.value_load(NOV[0:1, 0:1], min_val=0, max_val=OVER)
        with sp.If(nov > 0):
            with sp.Fori(0, nov) as n:
                eo = sp.value_load(NOV[0:1, bass.ds(n + 1, 1)], min_val=0, max_val=NE - 1)
                expert(eo, n + NE, True)
        sp.wait_ge(S("all_out"), 1)
        yv = y_d.rearrange("(k a p q) c -> k p a (q c)", k=2, a=TT, p=P)
        for k, dst in enumerate((y0, y1)):
            sp.dma_start(dst[:], yv[k]).then_inc(S(f"y{k}_in"), 16)
        ov = out[0].rearrange("(a p) d -> p a d", p=P)
        for tt in range(TT):
            sp.wait_ge(S("sum2"), tt + 1)
            sp.dma_start(ov[:, tt, :], x_sb[:, tt, :]).then_inc(S("out_done"), 16)
        sp.wait_ge(S("out_done"), 32)
        sp.wait_ge(S("gates_out0"), 16 * 6)
        sp.wait_ge(S("gates_out1"), 16 * 6)

    @block.scalar
    def _(act):
        eng["act"] = act
        norm_act(act, True)
        lb_act(act)
        for kt in range(KT):
            b = kt // 2
            act.wait_ge(S("h_turned"), b + 1)
            act.wait_ge(S("lb_ready"), 1)
            act.activation(hr[:, hi, kt, :], px[b % 4][:, (kt % 2) * T:(kt % 2 + 1) * T], ACT.Copy, scale=gmix[:, kt:kt + 1]).then_inc(S("h_hi"), 1)
        for u in range(NU):
            if u == UO:
                for kt in range(KT):
                    act.wait_ge(S("m_turned"), kt // 2 + 1)
                    act.activation(hr[:, hi, kt, :], px[kt // 2 % 4][:, (kt % 2) * T:(kt % 2 + 1) * T], ACT.Copy).then_inc(S("m_hi"), 1)
            act_hi(act, u)
            for fn, a in sched["act"].get(u, ()):
                fn(act, *a)
            if u >= UB and (u - UB) % 2 == 0 and u < UO:
                b = (u - UB) // 2
                act.wait_ge(S(f"gate_in{b % 2}"), 16 * (b // 2 + 1))
                act.activation(gsb[:, b % 2, :], gsb[:, b % 2, :], ACT.Sigmoid).then_inc(S("gate_sig"), 1)
        norm_act(act, False)
        act.wait_ge(S("r_shift"), V("r_shift") + 1)
        for tt in range(TT):
            for j in range(2):
                act.activation(ex8[:, tt, j, :], ex8[:, tt, j, :], ACT.Exp).then_inc(S("r_exp"), 1)

        def item_act(n):
            act.wait_ge(S("gt_turned"), n + 1)
            act.activation(sgm[:], px[2][:, 0:256].rearrange("p (h c) -> p h c", h=2)[:, :, 0:64], ACT.Sigmoid).then_inc(S("sig_done"), 1)

        item_loop(act, item_act, 1)

    @block.gpsimd
    def _(pool):
        for u in range(NU):
            pool_lo(pool, u)
            for fn, a in sched["pool"].get(u, ()):
                fn(pool, *a)
        pool.wait_ge(S("h2_out"), 32)

        def gather(n):
            pool.wait_ge(S("idx_ready"), n + 1)
            pool.sem_inc(S("pool_passed"), 1)
            pool.indirect_dma_start(out=xg[:, 0, :], out_offset=None, in_=h2_d,
                                    in_offset=bass.IndirectOffsetOnAxis(ap=idx[:, 0, 0:1].bitcast(U32), axis=0)).then_inc(S("x_rows"), 16)

        def scatter(n):
            pool.wait_ge(S("y_ready"), n + 1)
            pool.sem_inc(S("pool_passed"), 1)
            pool.indirect_dma_start(out=y_d, out_offset=bass.IndirectOffsetOnAxis(ap=idx[:, 0, 1:2].bitcast(U32), axis=0),
                                    in_=yb[:, 0, :], in_offset=None, bounds_check=2 * T * 4 - 1, oob_is_err=False).then_inc(S("y_rows"), 16)

        def body(n):
            gather(n)
            scatter(n)
        nov = item_loop(pool, body, 1)
        pool.wait_ge(S("y_rows"), (nov + NE) * 16)
        pool.sem_inc(S("pool_passed"), 1)
        pool.memset(zx[:, 0:1], 0.0).then_inc(S("all_out"), 1)

    @block.tensor
    def _(pe):
        eng["pe"] = pe
        rows_pe(pe)
        turn_pe(pe, x_sb, "n1_x", 2, "h")
        for u in range(NU):
            if u == UO:
                turn_pe(pe, merged, "gate_used", 12, "m")
            pe_unit(pe, u)
            for fn, a in sched["pe"].get(u, ()):
                fn(pe, *a)
        turn_pe(pe, h2, "n2_x", 2, "r")
        pe.wait_ge(S("router_in"), 64)
        pe.wait_ge(S("r_hi"), V("r_hi") + KT)
        for kt in range(KT):
            mm = pe.matmul(pj[0][0:NROUTE, 0:T], wro[:, kt, :], h2t[:, kt, :], start=kt == 0, stop=kt == KT - 1)
        mm.then_inc(S("r_logit"), 1)
        pe.wait_ge(S("r_lt"), V("r_lt") + 1)
        for tt in range(TT):
            mm = pe.transpose(px[0][:, tt * 64:tt * 64 + NROUTE], ltb[0:NROUTE, tt * P:(tt + 1) * P], C("ident")[0:NROUTE, 0:NROUTE])
        mm.then_inc(S("r_lturned"), 1)
        pe.wait_ge(S("r_onehot"), V("r_onehot") + 1)
        pe.matmul(px[0][:, 0:NE], C("before"), e12[:, 0, :], start=True, stop=True)
        pe.matmul(px[0][:, NE:2 * NE], C("ones"), e12[:, 0, :], start=True, stop=False)
        pe.matmul(px[0][:, NE:2 * NE], C("before"), e12[:, 1, :], start=False, stop=True)
        pe.matmul(px[0][:, 2 * NE:3 * NE], C("ones"), e12[:, 0, :], start=True, stop=False)
        pe.matmul(px[0][:, 2 * NE:3 * NE], C("ones"), e12[:, 1, :], start=False, stop=True).then_inc(S("r_rank"), 1)
        pe.wait_ge(S("r_val"), V("r_val") + 1)
        n = 0
        for tt in range(TT):
            for k in range(2):
                mm = pe.matmul(px[1][:, 0:3 * ITEMS], ohp[:, tt, k, :], val[:, tt, k, :, :].rearrange("p a b -> p (a b)"), start=n == 0, stop=n == 3)
                n += 1
        mm.then_inc(S("r_tab"), 1)

        def item_pe(n):
            pe.wait_ge(S("x_rows"), (n + 1) * 16)
            pe.wait_ge(S("r_tabread"), V("r_tabread") + 1)
            for j in range(4):
                mm = pe.transpose(px[0][:, j * P:(j + 1) * P], xg[:, 0, j * P:(j + 1) * P], C("ident"))
            mm.then_inc(S("x_turned"), 1)
            pe.wait_ge(S("xt_ready"), n + 1)
            for s_ in range(4):
                pe.wait_ge(S(f"expert{s_}"), (n + 1) * 16)
                for j in range(4):
                    for c in range(4):
                        mm = pe.matmul(px[1][c * 32:(c + 1) * 32, 0:256], xt[:, 0, j, s_ * 32:(s_ + 1) * 32],
                                       RING[:, s_, j * 1024 + c * 256:j * 1024 + (c + 1) * 256],
                                       start=s_ == 0 and j == 0, stop=s_ == 3 and j == 3)
                mm.then_inc(S(f"used{s_}"), 1)
            pe.wait_ge(S("gu_ready"), n + 1)
            for h in range(2):
                mm = pe.transpose(px[2][:, h * P:(h + 1) * P], gu[:, h * P:(h + 1) * P], C("ident"))
            mm.then_inc(S("gt_turned"), 1)
            pe.wait_ge(S("act_ready"), n + 1)
            for f in range(4):
                g, h = f // 2, f % 2
                if f % 2 == 0:
                    pe.wait_ge(S(f"expert{4 + f // 2}"), (n + 1) * 16)
                for c in range(4):
                    mm = pe.matmul(px[3][c * 32:(c + 1) * 32, :], act_t[:, h, g * 32:(g + 1) * 32],
                                   RING[:, 4 + f // 2, (f % 2) * 2048 + c * 512:(f % 2) * 2048 + (c + 1) * 512],
                                   start=f == 0, stop=f == 3)
                if f % 2 == 1:
                    mm.then_inc(S(f"used{4 + f // 2}"), 1)
        item_loop(pe, item_pe, 1)

    @block.vector
    def _(dve):
        eng["dve"] = dve
        link = Chain(dve, S("dve_step"))
        rows_dve(dve, link)
        norm_dve(dve, link, True)
        lb_dve(dve, link)
        dve.wait_ge(S("lb_ready"), 1)
        for kt in range(KT):
            b = kt // 2
            dve.wait_ge(S("h_hi"), 2 * b + 2)
            dve.scalar_tensor_tensor(hr[:, lo, kt, :], px[b % 4][:, (kt % 2) * T:(kt % 2 + 1) * T], gmix[:, kt:kt + 1],
                                     hr[:, hi, kt, :].bitcast(F32), ALU.mult, ALU.subtract).then_inc(S("h_lo"), 1)
        ends = {pan["u1"]: pi for pi, pan in enumerate(panels)}
        for u in range(NU + 1):
            if u in ends:
                dve_read_panel(dve, ends[u])
            if u == UO:
                for kt in range(KT):
                    dve.wait_ge(S("m_hi"), 2 * (kt // 2) + 2)
                    dve.tensor_tensor(hr[:, lo, kt, :], px[kt // 2 % 4][:, (kt % 2) * T:(kt % 2 + 1) * T], hr[:, hi, kt, :].bitcast(F32), ALU.subtract).then_inc(S("m_lo"), 1)
            for fn, a in sched["dve"].get(u, ()):
                fn(dve, link, *a)
        norm_dve(dve, link, False)
        for kt in range(KT):
            b = kt // 2
            dve.wait_ge(S("r_turned"), V("r_turned") + b + 1)
            if kt == 0:
                dve.wait_ge(S("n2_x"), 2)
            dve.tensor_scalar(h2t[:, kt, :], px[b % 4][:, (kt % 2) * T:(kt % 2 + 1) * T], gffn[:, kt:kt + 1], None, ALU.mult).then_inc(S("r_hi"), 1)
        dve.wait_ge(S("r_logit"), V("r_logit") + 1)
        dve.tensor_copy(ltb[0:NROUTE, :], pj[0][0:NROUTE, 0:T]).then_inc(S("r_lt"), 1)
        dve.wait_ge(S("r_lturned"), V("r_lturned") + 1)
        dve.wait_ge(S("router_in"), 64)
        for tt in range(TT):
            link(dve.tensor_tensor(lg[:, tt, :], px[0][:, tt * 64:tt * 64 + NROUTE], brt[:], ALU.add))
        for tt in range(TT):
            link(dve.tensor_copy(gl8[:, tt, :], C("padmax")))
            link(dve.tensor_copy(gl8[:, tt, 0:NG], lg[:, tt, 0:NG]))
            link(dve.max(mx8[:, tt, 0, :], gl8[:, tt, :]))
            link(dve.max_index(ix8[:, tt, 0, :], mx8[:, tt, 0, :], gl8[:, tt, :]))
            link(dve.tensor_copy(ixf[:, tt, 0:1], ix8[:, tt, 0, 0:1]))
            link(dve.tensor_scalar(ohg[:], C("iota32")[:, 0:NG], ixf[:, tt, 0:1], None, ALU.is_equal))
            link(dve.tensor_scalar(ohg[:], ohg[:], -1.0, 1e30, ALU.add, ALU.mult))
            link(dve.tensor_tensor(elm[:, tt, :].rearrange("p (g e) -> p g e", g=NG), lg[:, tt, NG:NROUTE].rearrange("p (g e) -> p g e", g=NG),
                                   ohg[:].unsqueeze(2).to_broadcast([P, NG, EPG]), ALU.add))
            link(dve.max(mx8[:, tt, 1, :], elm[:, tt, :]))
            link(dve.max_index(ix8[:, tt, 1, :], mx8[:, tt, 1, :], elm[:, tt, :]))
            link(dve.tensor_copy(ixf[:, tt, 1:3], ix8[:, tt, 1, 0:2]))
            for j in range(2):
                ins = dve.tensor_scalar(ex8[:, tt, j, :], mx8[:, tt, j, :], mx8[:, tt, j, 0:1], None, ALU.subtract)
                if tt == 1 and j == 1:
                    ins.then_inc(S("r_shift"), 1)
                else:
                    link(ins)
        dve.wait_ge(S("r_exp"), 4)
        for tt in range(TT):
            link(dve.tensor_reduce(rs[:, tt, 0:2], ex8[:, tt, :, :], AX.X, ALU.add))
            link(dve.reciprocal(rs[:, tt, 2:4], rs[:, tt, 0:2]))
            link(dve.tensor_scalar(rs[:, tt, 4:6], ex8[:, tt, 1, 0:2], rs[:, tt, 3:4], None, ALU.mult))
            link(dve.tensor_tensor(rs[:, tt, 6:7], rs[:, tt, 4:5], rs[:, tt, 5:6], ALU.add))
            link(dve.reciprocal(rs[:, tt, 7:8], rs[:, tt, 6:7]))
            link(dve.tensor_scalar(rs[:, tt, 4:6], rs[:, tt, 4:6], rs[:, tt, 7:8], rs[:, tt, 2:3], ALU.mult, ALU.mult))
            for k in range(2):
                link(dve.tensor_scalar(ek[:, tt, k, :], C("iota32"), ixf[:, tt, 1 + k:2 + k], None, ALU.is_equal))
        dve.tensor_tensor(e12[:], ek[:, :, 0, :], ek[:, :, 1, :], ALU.add).then_inc(S("r_onehot"), 1)
        dve.wait_ge(S("r_rank"), V("r_rank") + 1)
        link(dve.tensor_copy(f2(rank[:]), px[0][:, 0:2 * NE]))
        link(dve.tensor_copy(cnt[:], px[0][:, 2 * NE:3 * NE]))
        link(dve.tensor_scalar(xtra[:], cnt[:], float(SLOTS), None, ALU.is_gt))
        link(dve.tensor_scalar(fl[:], rank[:], float(SLOTS), None, ALU.is_ge))
        for j in range(2, T // SLOTS):
            link(dve.tensor_scalar(tmp[:, 0, :], cnt[:], float(SLOTS * j), None, ALU.is_gt))
            link(dve.tensor_tensor(xtra[:], xtra[:], tmp[:, 0, :], ALU.add))
            link(dve.tensor_scalar(tmp[:], rank[:], float(SLOTS * j), None, ALU.is_ge))
            link(dve.tensor_tensor(fl[:], fl[:], tmp[:], ALU.add))
        link(dve.tensor_scalar(pos_[:], fl[:], -float(SLOTS), None, ALU.mult))
        link(dve.tensor_tensor(pos_[:], pos_[:], rank[:], ALU.add))
        link(dve.tensor_tensor_scan(base[:], C("ones")[:, 0:NE], xtra[:], 0.0, ALU.mult, ALU.add))
        link(dve.tensor_copy(oe[:, 0, :], base[:]))
        link(dve.tensor_tensor(base[:], base[:], xtra[:], ALU.subtract))
        for tt in range(TT):
            link(dve.tensor_tensor(item[:, tt, :], fl[:, tt, :], base[:], ALU.add))
            link(dve.tensor_scalar(item[:, tt, :], item[:, tt, :], float(NE - 1), None, ALU.add))
            link(dve.tensor_tensor(item[:, tt, :], item[:, tt, :], C("iota32"), ALU.subtract))
            link(dve.tensor_scalar(tmp[:, tt, :], fl[:, tt, :], 0.0, None, ALU.is_gt))
            link(dve.tensor_tensor(item[:, tt, :], item[:, tt, :], tmp[:, tt, :], ALU.mult))
            link(dve.tensor_tensor(item[:, tt, :], item[:, tt, :], C("iota32"), ALU.add))
            for k in range(2):
                link(dve.tensor_tensor(tmp[:, tt, :], item[:, tt, :], ek[:, tt, k, :], ALU.mult))
                link(dve.tensor_reduce(sel[:, tt, k, 0:1], tmp[:, tt, :], AX.X, ALU.add))
                link(dve.tensor_tensor(tmp[:, tt, :], pos_[:, tt, :], ek[:, tt, k, :], ALU.mult))
                link(dve.tensor_reduce(sel[:, tt, k, 1:2], tmp[:, tt, :], AX.X, ALU.add))
                link(dve.tensor_scalar(ohp[:, tt, k, :], C("slot4"), sel[:, tt, k, 1:2], None, ALU.is_equal))
                link(dve.tensor_scalar(oh48[:], C("iota48"), sel[:, tt, k, 0:1], None, ALU.is_equal))
                link(dve.tensor_scalar(sel[:, tt, k, 2:3], C("part"), 4.0, float(4 * P * tt), ALU.mult, ALU.add))
                link(dve.tensor_scalar(sel[:, tt, k, 3:4], C("part"), 4.0, float(4 * P * tt + 4 * T * k + 1), ALU.mult, ALU.add))
                link(dve.tensor_scalar(val[:, tt, k, 0, :], oh48[:], sel[:, tt, k, 2:3], None, ALU.mult))
                link(dve.tensor_scalar(val[:, tt, k, 1, :], oh48[:], rs[:, tt, 4 + k:5 + k], None, ALU.mult))
                link(dve.tensor_scalar(val[:, tt, k, 2, :], oh48[:], sel[:, tt, k, 3:4], None, ALU.mult))
        link(dve.tensor_scalar(oe[:, 1, :], oe[:, 0, :], C("part"), None, ALU.is_gt))
        link(dve.tensor_scalar(oe[:, 2, :], base[:], C("part"), None, ALU.is_le))
        link(dve.tensor_tensor(oe[:, 1, :], oe[:, 1, :], oe[:, 2, :], ALU.mult))
        link(dve.tensor_tensor(oe[:, 1, :], oe[:, 1, :], C("iota32"), ALU.mult))
        link(dve.memset(oe32[:], 0.0))
        link(dve.tensor_reduce(oe32[:, 0, 0:1], oe[0:32, 1, :], AX.X, ALU.add))
        link(dve.transpose(oe32[:, 1, :], oe32[:, 0, :]))
        link(dve.tensor_copy(NOV[0:1, 0:1], oe[0:1, 0, NE - 1:NE]))
        link(dve.tensor_copy(NOV[0:1, 1:1 + OVER], oe32[0:1, 1, 0:OVER]))
        dve.memset(zx[:, 1:2], 0.0).then_inc(S("r_val"), 1)
        dve.wait_ge(S("r_val"), V("r_val") + 1)
        dve.memset(zx[:, 2:3], 0.0).then_inc(S("overflow_known"), 1)
        dve.wait_ge(S("r_tab"), V("r_tab") + 1)
        link(dve.tensor_copy(tab[:].rearrange("p a b -> p (a b)"), px[1][:, 0:3 * ITEMS]))
        link(dve.tensor_scalar(tabi[:, 0, :], tab[:, 0, :], C("group"), None, ALU.add))
        link(dve.tensor_scalar(zx[:], tab[:, 2, :], 0.0, float(8 * T * 4), ALU.is_equal, ALU.mult))
        link(dve.tensor_tensor(zx[:], zx[:], tab[:, 2, :], ALU.add))
        link(dve.tensor_scalar(zx[:], zx[:], C("group"), -1.0, ALU.add, ALU.add))
        dve.tensor_copy(tabi[:, 1, :], zx[:]).then_inc(S("r_tabread"), 1)
        dve.wait_ge(S("r_tabread"), V("r_tabread") + 1)

        def item_dve(n):
            dve.tensor_copy(wcol[:, 0:1], tab[:, 1, bass.ds(n, 1)]).then_inc(S("w_ready"), 1)
            dve.tensor_copy(idx[:, 0, :], tabi[:, :, bass.ds(n, 1)].rearrange("p a b -> p (a b)")).then_inc(S("idx_ready"), 1)
            dve.wait_ge(S("x_turned"), n + 1)
            dve.tensor_tensor(xt[:, 0, :, :].rearrange("p j (q s) -> p j q s", q=4), px[0][:].rearrange("p (j q s) -> p j q s", j=4, q=4),
                              gffn[:].rearrange("p (q j) -> p j q", q=4).unsqueeze(3).to_broadcast([P, 4, 4, 32]), ALU.mult).then_inc(S("xt_ready"), 1)
            dve.wait_ge(S("used3"), n + 1)
            dve.tensor_copy(gu[:], px[1][:, 0:256]).then_inc(S("gu_ready"), 1)
            dve.wait_ge(S("sig_done"), n + 1)
            dve.wait_ge(S("gt_turned"), n + 1)
            g3 = px[2][:, 0:256].rearrange("p (h c) -> p h c", h=2)
            dve.tensor_tensor(up[:], g3[:, :, 0:64], sgm[:], ALU.mult).then_inc(S("silu_done"), 1)
            dve.wait_ge(S("silu_done"), n + 1)
            dve.tensor_tensor(act_t[:], g3[:, :, 64:128], up[:], ALU.mult).then_inc(S("act_ready"), 1)
            dve.wait_ge(S("used5"), n + 1)
            dve.wait_ge(S("w_ready"), n + 1)
            dve.tensor_scalar(yb[:, 0, :], px[3][:], wcol[:, 0:1], None, ALU.mult).then_inc(S("y_ready"), 1)
            dve.wait_ge(S("y_rows"), (n + 1) * 16)
        item_loop(dve, item_dve, 1)
        for k, ys in enumerate((y0, y1)):
            dve.wait_ge(S(f"y{k}_in"), 16)
            for tt in range(TT):
                if k:
                    dve.wait_ge(S("sum1"), tt + 1)
                dve.tensor_tensor(x_sb[:, tt, :], x_sb[:, tt, :], ys[:, tt, :], ALU.add).then_inc(S(f"sum{k + 1}"), 1)

    block.__exit__(None, None, None)


_INS = ["x", "norm_mix", "w_in", "cmp_pe", "cmp_w1", "cmp_w2", "q_norm", "k_norm", "hg_lb_logits", "hg_norm",
        "gla_w_a2", "gla_b_a", "gla_norm", "w_branch", "w_out", "norm_ffn", "w_grp", "b_grp", "w_exp", "b_exp",
        "w_gate_up", "w_down"]


def kernel(**inputs):
    import concourse.bacc as bacc
    from concourse.bass_utils import run_bass_kernel_spmd

    nc = bacc.Bacc("TRN2", target_bir_lowering=False, num_devices=1)
    arrays, aps = {}, {}
    for name in _INS:
        a = np.ascontiguousarray(inputs[name])
        arrays["in_" + name] = a
        aps[name] = nc.dram_tensor("in_" + name, a.shape, mybir.dt.from_np(a.dtype), kind="ExternalInput").ap()
    (ca, wa), (cb, wb) = constants()
    consts = {}
    for n, c, w in (("ca", ca, wa), ("cb", cb, wb)):
        w["_n"] = c.shape[1]
        arrays["const_" + n] = c
        consts[n] = nc.dram_tensor("const_" + n, c.shape, F32, kind="ExternalInput").ap()
    out = nc.dram_tensor("out_dram", (1, T, D), F32, kind="ExternalOutput").ap()
    build_program(nc, aps, consts, wa, wb, out)
    r = run_bass_kernel_spmd(nc, [arrays], core_ids=[0])
    return r.results[0]["out_dram"]
```

```python
import numpy as np

import concourse.bass as bass
from concourse import mybir

F32 = mybir.dt.float32
F32R = mybir.dt.float32r
U32 = mybir.dt.uint32
I32 = mybir.dt.int32
ALU = mybir.AluOpType
ACT = mybir.ActivationFunctionType
AX = mybir.AxisListType

P = 128
D = 2048
T = 256
TT = T // P
KT = D // P
BW = D // 4
HEADS, KV, HD = 8, 2, 64
NCMP = (T - 32) // 16 + 1
CHUNK = 64
NG, EPG = 4, 8
NE = NG * EPG
FF = D // 4
EPS = 1e-6
NEG = -1e30
TINY = 1e-30
SLOTS = 32
OVER = 2 * T // SLOTS
ITEMS = NE + OVER
COLS = ITEMS + 1
NROUTE = NG + NE

Q0, KC0, KW0 = 0, 512, 1024
HGQ0 = 1304
HGF0, HGI0, HGG0 = HGQ0 + 512, HGQ0 + 1024, HGQ0 + 1536
GLQ0 = HGQ0 + 2048
GLV0, GLR0, GLA0 = GLQ0 + 512, GLQ0 + 1024, GLQ0 + 1536
MG0 = GLA0 + 16

SLOPES = [2.0 ** (-8.0 * (h + 1) / HEADS) for h in range(HEADS)]


def constants():
    p = np.arange(P)
    a, b = {}, {}
    b["ident"] = np.eye(P)
    b["ones"] = np.ones((P, P))
    b["before"] = (p[:, None] < p[None, :]) * 1.0
    b["iota32"] = np.tile(np.arange(NE), (P, 1))
    b["iota48"] = np.tile(np.arange(COLS), (P, 1))
    b["slot4"] = np.tile(np.arange(P) % SLOTS + 1, (P, 1))
    b["steps"] = np.tile(SLOTS * np.arange(1, T // SLOTS), (P, 1))
    b["part"] = p[:, None]
    b["padmax"] = np.full((P, 8), NEG)
    a["halves"] = (p[:, None] // HD == p[None, :] // HD) * 1.0
    lv = [p[:, None] == p[None, :]]
    s = 1
    while s < P:
        lv.append((p[:, None] // (2 * s) == p[None, :] // (2 * s)) & (p[:, None] % (2 * s) < s) & (p[None, :] % (2 * s) >= s))
        s *= 2
    a["levels"] = np.concatenate([m * 1.0 for m in lv], 1)
    big = 1e32
    d0 = p[:, None] - p[None, :]
    d1 = p[:, None] + P - np.arange(T)[None, :]
    a["dist0"] = np.where(d0 >= 0, d0, big)
    a["dist1"] = np.where(d1 >= 0, d1, big)
    t = p[:, None] + P * np.arange(TT)[None, :]
    n = np.arange(16)
    dc = t[:, :, None] - (n * 16 + 31)[None, None, :]
    vis = (dc >= 0) & (n < NCMP)
    cb = np.zeros((P, TT, 4, KV, 16))
    for i in range(4):
        for g in range(KV):
            cb[:, :, i, g] = np.where(vis, -SLOPES[g * 4 + i] * dc, NEG)
    a["cbias"] = cb.reshape(P, -1)
    a["cvis"] = vis.reshape(P, -1) * 1.0
    r = np.ones((P, 4, T))
    r[:, :, ::CHUNK] = 0
    a["reset"] = r.reshape(P, -1)
    out = []
    for c in (a, b):
        off, where = 0, {}
        for k, v in c.items():
            where[k] = (off, v.shape[1])
            off += v.shape[1]
        out.append((np.concatenate([np.asarray(v, np.float32) for v in c.values()], 1), where))
    return out


class Chain:

    def __init__(self, eng, sem):
        self.eng, self.sem, self.n = eng, sem, 0

    def __call__(self, ins):
        self.n += 1
        ins.then_inc(self.sem, 1)
        self.eng.wait_ge(self.sem, self.n)


def build_program(nc, i_, consts, wa, wb_, out):
    ring_at = 16512
    ts = nc.alloc_sbuf_tensor_at
    K = 1024

    def at(name, shape, off, dt=F32):
        return ts(name, shape, dt, offset=off)

    RING = at("ring", [P, 6, 4096], ring_at)
    HR_AT = ring_at + 96 * K
    hr = at("hr", [P, 2, KT, T], HR_AT, F32R)
    WR_AT = HR_AT + 32 * K
    wr = at("wr", [P, 3, 2, 1024], WR_AT, F32R)
    XR = WR_AT + 24 * K
    MX = XR + 16 * K
    OV = ring_at + 48 * K
    x_sb = at("x_sb", [P, TT, D], XR)
    orr = at("orr", [P, 2, 12, T], MX, F32R)
    hgq = at("hgq", [P, 4, T], MX + 24 * K)
    SM = MX + 28 * K
    cb = at("cb", [P, wb_["_n"]], SM)
    SM2 = SM + (4 * wb_["_n"] + 31) // 32 * 32
    sm_off = [SM2]

    def small(name, shape, dt=F32):
        n = 4 * int(np.prod(shape[1:]))
        n = (n + 31) // 32 * 32
        t_ = at(name, shape, sm_off[0], dt)
        sm_off[0] += n
        assert sm_off[0] <= 229368, sm_off
        return t_

    o = OV
    ca = at("ca", [P, wa["_n"]], o); o += (4 * wa["_n"] + 31) // 32 * 32
    pn = at("pn", [P, 11, T], o)
    hgk = at("hgk", [P, 4, T], o)
    hgb = at("hgb", [P, 4, T], o + 4 * K)
    st2 = at("st2", [P, 4, P], o + 8 * K)
    o += 11 * K
    kz = at("kz", [P, 2, KV, T], o)
    wbuf = at("wbuf", [P, 4, T], o); o += 4 * K
    vz = at("vz", [P, TT, 2, KV, P], o)
    zb0 = at("zb0", [P, 4, T], o); o += 4 * K
    ax = at("ax", [P, 2, 32, 16], o)
    sq = at("sq", [P, 6, T], o)
    zb1 = at("zb1", [P, 4, T], o); o += 4 * K
    vcb = at("vcb", [P, 4, P], o); o += 2 * K
    ptc = at("ptc", [P, TT, P], o); o += K
    STG = o - 3 * K
    sb = at("sb", [P, 2, KV, T], o)
    rr = at("rr", [P, 6, T], o)
    st = at("st", [P, 8, P], o + K)
    stg = at("stg", [P, 1024], STG)
    o += 4 * K
    PT_AT = o
    pt = at("pt", [P, 4, P], o); o += 2 * K
    hgz = at("hgz", [P, 4, T], o)
    glqk = at("glqk", [P, 4, T], o); o += 4 * K
    assert o <= OV + 48 * K, (o - OV) / K
    w1 = at("w1", [P, 2, 32, HD], XR)
    hgi = at("hgi", [P, TT, 512], XR)
    hgg = at("hgg", [P, TT, 512], XR + 4 * K)
    glv = at("glv", [P, TT, 512], XR + 8 * K)
    glr = at("glr", [P, TT, 512], XR + 12 * K)
    stge = at("stge", [P, 2, 1024], XR + 8 * K)

    def stage(c):
        return stge[:, c % 2, :] if c < 6 else stg[:]
    gla = small("gla", [P, T])
    merged = at("merged", [P, TT, D], OV)
    gsb = at("gsb", [P, 2, TT * 512], OV + 16 * K)
    prod = at("prod", [P, TT * 512], OV + 24 * K)
    h2 = at("h2", [P, TT, D], HR_AT + 16 * K)
    ltb = at("ltb", [P, T], WR_AT + 3 * K)
    MC = WR_AT + 4 * K
    xg = at("xg", [P, 512], MC)
    yt = at("yt", [P, 2, 512], MC + 2 * K)
    xt = at("xt", [P, 4, P], MC + 6 * K)
    gu = at("gu", [P, 256], MC + 8 * K)
    sgm = at("sgm", [P, 2, 64], MC + 9 * K)
    up = at("up", [P, 2, 64], MC + 9 * K + 512)
    act_t = at("act_t", [P, 2, 64], MC + 10 * K)
    ohw = at("ohw", [P, TT, P], MC + 11 * K)
    ohwt = at("ohwt", [P, T], MC + 12 * K)
    oh = at("oh", [P, TT, SLOTS], MC + 13 * K)
    wc = at("wc", [P, 2, TT], MC + 13 * K + 512)

    pj = [nc.alloc_psum_tensor(f"pj{b}", [P, 1024], F32) for b in range(2)]
    px = [nc.alloc_psum_tensor(f"px{b}", [P, 512], F32) for b in range(4)]

    def C(name):
        w, t_ = (wa, ca) if name in wa else (wb_, cb)
        off, n = w[name]
        return t_[:, off:off + n]

    gates_d = nc.dram_tensor("gates_d", (12, P, 1024), F32, kind="Internal").ap()

    SEQUENCES = {
        "nsa_dve": [("nsa_sq", 1), ("nsa_ms", 3), ("nsa_qk", 5), ("cmp_in", 1), ("cmp_hidden", 4), ("cmp_u", 1), ("cmp_g", 1), ("cmp_v", 2), ("cmp_sq", 1), ("cmp_ms", 1), ("cmp_k", 2), ("cmp_sub", 1), ("cmp_p", 1), ("cmp_ptc", 1)],
        "nsa_pe": [("nsa_ss", 1), ("nsa_turned", 1), ("cmp_h", 2), ("cmp_kv", 1), ("cmp_ss", 1), ("cmp_scores", 1), ("cmp_pt", 1)],
        "nsa_act": [("nsa_sd", 1), ("nsa_gates", 1), ("cmp_s", 1), ("cmp_sd", 1), ("cmp_exp", 1)],
        "router_dve": [("r_hi", 16), ("r_lt", 1), ("r_shift", 1), ("r_onehot", 1), ("overflow_known", 1)],
        "router_pe": [("r_turned", 8), ("r_logit", 1), ("r_lturned", 1), ("r_rank", 1)],
    }
    before_step = {}
    for seq, steps in SEQUENCES.items():
        n = 0
        for step_name, incs in steps:
            before_step[step_name] = (seq, n)
            n += incs

    def V(name):
        return before_step.get(name, (name, 0))[1]

    sems = {}

    def S(name):
        name = before_step.get(name, (name, 0))[0]
        if name not in sems:
            sems[name] = nc.alloc_semaphore(name)
        return sems[name]

    gmix = small("gmix", [P, KT])
    gffn = small("gffn", [P, KT])
    stat = small("stat", [P, 20])
    ngain = small("ngain", [P, 4])
    hgain = small("hgain", [P, P])
    ggain = small("ggain", [P, P])
    lb = small("lb", [P, 4, 4])
    bal = small("bal", [P, 2])
    wa2 = small("wa2", [16, T])
    w2 = small("w2", [P, 2, HD])
    pe2 = at("pe2", [64, P], MX + 24 * K)
    rows = at("rows", [16, 3, P], PT_AT)
    gate = small("gate", [P, TT, 24])
    hid = small("hid", [P, 6, 2, 16])
    kct = small("kct", [P, 4, 16])
    kcz = small("kcz", [P, KV, 16])
    vcs = small("vcs", [16, KV, HD])
    cs = small("cs", [P, 5, 16])
    csc = at("csc", [P, TT * P], PT_AT)
    am = small("am", [P, 2, 8])
    zr = small("zr", [P, 8])

    win, wbr, wout = i_["w_in"][0], i_["w_branch"][0], i_["w_out"][0]
    panels = []

    def in_panel(kind, c0, width, key):
        panels.append(dict(kind=kind, key=key, width=width, kts=KT, act="h",
                           src=[win[h * 1024:(h + 1) * 1024, c0:c0 + width].rearrange("(k p) c -> p k c", p=P) for h in range(2)]))

    in_panel("q", Q0, 512, "nsa_q")
    in_panel("t", KC0, 512, "nsa_k")
    in_panel("t3", KW0, 512, "nsa_w")
    in_panel("t", HGF0, 512, "hg_f")
    in_panel("t", HGQ0, 512, "hg_q")
    in_panel("n", HGI0, 512, "hg_i")
    in_panel("n", HGG0, 512, "hg_g")
    EARLY = 6
    for c in range(EARLY):
        in_panel("n", MG0 + 512 * c, 512, f"mg{c}")
    in_panel("t", GLQ0, 512, "gl_qk")
    in_panel("t1", GLA0, 128, "gl_a")
    in_panel("n", GLV0, 512, "gl_v")
    in_panel("n", GLR0, 512, "gl_r")
    for c in range(EARLY, 12):
        in_panel("n", MG0 + 512 * c, 512, f"mg{c}")
    PI = {pan["key"]: n for n, pan in enumerate(panels)}
    FIRST_B = len(panels)
    for n in range(3):
        for c in range(4):
            panels.append(dict(kind="n", key=f"br{n}{c}", width=512, kts=4, act=n,
                               src=[wbr[n][:, c * 512:(c + 1) * 512].rearrange("(k p) c -> p k c", p=P)]))
    FIRST_O = len(panels)
    for c in range(4):
        panels.append(dict(kind="n", key=f"wo{c}", width=512, kts=KT, act="m",
                           src=[wout[h * 1024:(h + 1) * 1024, c * 512:(c + 1) * 512].rearrange("(k p) c -> p k c", p=P) for h in range(2)]))
    slots, units = [], []
    for pi, pan in enumerate(panels):
        pan["u0"] = len(units)
        for s_ in range(len(pan["src"])):
            nk = min(8, pan["kts"] - 8 * s_)
            k_ = len(slots)
            for qd in range(nk // 2):
                units.append((pi, k_, qd, 8 * s_ + 2 * qd))
            slots.append((pi, s_, nk, len(units)))
        pan["u1"] = len(units)
    NU = len(units)
    UB = panels[FIRST_B]["u0"]
    UO = panels[FIRST_O]["u0"]

    def raw(u):
        pi, k_, qd, _ = units[u]
        w = panels[pi]["width"]
        return RING[:, k_ % 3, qd * 2 * w:(qd + 1) * 2 * w]

    gexp_w, down_w = i_["w_gate_up"][0], i_["w_down"][0]

    A0 = 26
    CM = A0 + 4
    AT0 = CM + 31
    HG0 = AT0 + 40
    GL0 = HG0 + 40
    NL = 8

    sched = {e: {} for e in ("pe", "act", "dve", "pool")}

    def put(e, pos, fn, *a):
        sched[e].setdefault(pos, []).append((fn, a))

    def go(e, pos):
        for fn, a in sched[e].get(pos, ()):
            fn(*a)

    hi, lo = 0, 1

    def consts_loads(sp):
        sp.dma_start(x_sb[:, 0, :], i_["x"][0, 0:P, :]).then_inc(S("x_in"), 16)
        sp.dma_start(x_sb[:, 1, :], i_["x"][0, P:T, :]).then_inc(S("x_in1"), 16)
        sp.dma_start(cb[:], consts["cb"]).then_inc(S("const_b"), 16)
        sp.dma_start(rows[:, 0, :], i_["norm_mix"][0].rearrange("(k p) -> k p", p=P)).then_inc(S("rows_in"), 16)
        sp.dma_start(rows[:, 1, :], i_["norm_ffn"][0].rearrange("(k p) -> k p", p=P)).then_inc(S("rows_in"), 16)
        sp.dma_start(rows[0:4, 2, :], i_["hg_lb_logits"][0].rearrange("(k p) -> k p", p=P)).then_inc(S("rows_in"), 16)

    def small_loads(sp):
        def ld(dst, src):
            sp.dma_start(dst, src).then_inc(S("small_in"), 16)
            small_loads.n += 1
        small_loads.n = 0
        ld(ca[:], consts["ca"])
        for half in range(2):
            r = slice(half * HD, (half + 1) * HD)
            ld(ngain[r, 0:1], i_["q_norm"][0].rearrange("(d o) -> d o", o=1))
            for j in range(3):
                ld(ngain[r, 1 + j:2 + j], i_["k_norm"][0, j].rearrange("(d o) -> d o", o=1))
            ld(w2[r, :, :], i_["cmp_w2"][0].rearrange("v a b -> a v b"))
            ld(pe2[:, half * HD:(half + 1) * HD], i_["cmp_pe"][0].rearrange("v l d -> (v l) d"))
        ld(hgain[:], i_["hg_norm"].broadcast_to([P, P]))
        ld(ggain[:], i_["gla_norm"].broadcast_to([P, P]))
        ld(wa2[:], i_["gla_w_a2"][0])
        for a in range(2):
            ld(bal[:, a:a + 1], i_["gla_b_a"][0, a * P:(a + 1) * P].rearrange("(p o) -> p o", o=1))
        return small_loads.n * 16

    SMALL_IN = 16 * (1 + 2 * 6 + 5)

    def load_slot(sp, k_):
        pi, s_, nk, _ = slots[k_]
        if k_ >= 3:
            sp.wait_ge(S("split_lo"), slots[k_ - 3][3])
        w = panels[pi]["width"]
        dst = RING[:, k_ % 3, 0:nk * w].rearrange("p (k c) -> p k c", k=nk)
        src = panels[pi]["src"][s_]
        if panels[pi]["act"] == 0:
            c = int(panels[pi]["key"][3])
            for half in range(2):
                r = slice(half * HD, (half + 1) * HD)
                src = wbr[0][half * 256:(half + 1) * 256, c * 512:(c + 1) * 512].rearrange("(k p) c -> p k c", p=HD)
                sp.dma_start(dst[r], src).then_inc(S(f"landed{k_ % 3}"), 16)
        else:
            sp.dma_start(dst, src).then_inc(S(f"landed{k_ % 3}"), 16)

    landed, tot = {}, [0, 0, 0]
    for k_ in range(len(slots)):
        tot[k_ % 3] += 32 if panels[slots[k_][0]]["act"] == 0 else 16
        landed[k_] = tot[k_ % 3]

    def unit_parts(u):
        w = panels[units[u][0]]["width"]
        if panels[units[u][0]]["kind"] != "q":
            return [(raw(u), lambda h: wr[:, u % 3, h, 0:2 * w])]
        return [(raw(u)[:, k * w:(k + 1) * w].rearrange("p (g i d) -> p i g d", g=2, i=4),
                 lambda h, k=k: wr[:, u % 3, h, k * w:(k + 1) * w].rearrange("p (i g d) -> p i g d", g=2, i=4)) for k in range(2)]

    def act_hi(act, u):
        pi, k_, qd, kt = units[u]
        w = panels[pi]["width"]
        act.wait_ge(S(f"landed{k_ % 3}"), landed[k_])
        if u >= 3:
            act.wait_ge(S("unit_done"), u - 2)
        for src, half in unit_parts(u):
            ins = act.activation(half(hi), src, ACT.Copy)
        ins.then_inc(S("split_hi"), 1)

    def pool_lo(pool, u):
        pool.wait_ge(S("split_hi"), u + 1)
        for src, half in unit_parts(u):
            ins = pool.tensor_tensor(half(lo), src, half(hi).bitcast(F32), ALU.subtract)
        ins.then_inc(S("split_lo"), 1)

    evac_engine = {}
    for pi, pan in enumerate(panels):
        evac_engine[pi] = "dve"

    def pe_unit(pe, u):
        pi, k_, qd, kt = units[u]
        pan = panels[pi]
        bank = pj[pi % 2]
        if u < KT // 2:
            pe.wait_ge(S("h_hi"), kt + 2)
            pe.wait_ge(S("h_lo"), kt + 2)
        if u == pan["u0"] and pi >= 2:
            pe.wait_ge(S("panel_read"), pi - 1)
        if pan["act"] != "h" and pan["act"] != "m" and u == pan["u0"]:
            pe.wait_ge(S("branch_lo"), 8 * (pan["act"] + 1))
            pe.wait_ge(S("branch_hi"), 8 * (pan["act"] + 1))
        if u == UO:
            pe.wait_ge(S("m_hi"), KT)
            pe.wait_ge(S("m_lo"), KT)
        pe.wait_ge(S("split_lo"), u + 1)
        pe.wait_ge(S("split_hi"), u + 1)
        w = pan["width"]
        mm = None
        for k in range(2):
            kk = kt + k
            first, last = kk == 0, kk == pan["kts"] - 1

            def a_(h, tt=None):
                if pan["act"] in ("h", "m"):
                    t_ = hr[:, h, kk, :]
                else:
                    t_ = orr[:, h, 4 * pan["act"] + kk, :]
                return t_ if tt is None else t_[:, tt * P:(tt + 1) * P]

            wu = [wr[:, u % 3, h, k * w:(k + 1) * w] for h in range(2)]
            if pan["kind"] == "n":
                for tt in range(TT):
                    for n, (ah, wh) in enumerate(((hi, hi), (lo, hi), (hi, lo))):
                        mm = pe.matmul(bank[:, tt * 512:(tt + 1) * 512], a_(ah, tt), wu[wh],
                                       start=first and n == 0, stop=last and n == 2)
            else:
                for m in range({"q": 4, "t": 4, "t3": 3, "t1": 1}[pan["kind"]]):
                    for n, (ah, wh) in enumerate(((hi, hi), (lo, hi), (hi, lo))):
                        lhs = wu[wh][:, m * P:(m + 1) * P]
                        mm = pe.matmul(bank[:, m * T:(m + 1) * T], lhs, a_(ah),
                                       start=first and n == 0 and m % 2 == 0, stop=last and n == 2,
                                       skip_group_check=True)
        mm.then_inc(S("unit_done"), 1)

    def dve_read_panel(dve, pi):
        pan = panels[pi]
        key = pan["key"]
        dve.wait_ge(S("unit_done"), pan["u1"])
        src = pj[pi % 2]
        dests = {"nsa_q": (pn[:, 0:4, :], 1024), "nsa_k": (pn[:, 4:8, :], 1024), "nsa_w": (pn[:, 8:11, :], 768),
                 "hg_f": (hgz[:], 1024), "hg_q": (hgq[:], 1024), "hg_i": (hgi[:], 1024), "hg_g": (hgg[:], 1024),
                 "gl_qk": (glqk[:], 1024), "gl_a": (gla[:], 256), "gl_v": (glv[:], 1024), "gl_r": (glr[:], 1024)}
        if key in dests:
            if key == "nsa_q":
                dve.wait_ge(S("small_in"), SMALL_IN)
            if key == "hg_i":
                dve.wait_ge(S("cmp_hidden"), V("cmp_hidden") + 4)
            if key in ("gl_v", "gl_r"):
                for j in range(2):
                    dve.wait_ge(S(f"gates_out{j}"), 16 * (EARLY // 2))
            if key == "gl_qk":
                dve.wait_ge(S("hg_sig"), 2)
            d_, n = dests[key]
            if len(d_.shape) == 3:
                d_ = d_.rearrange("p a b -> p (a b)")
            dve.tensor_copy(d_, src[:, 0:n]).then_inc(S("panel_read"), 1)
        elif key.startswith("mg"):
            c = int(key[2:])
            if c == 0:
                dve.wait_ge(S("cmp_hidden"), V("cmp_hidden") + 4)
            elif c == EARLY:
                dve.wait_ge(S("att_done"), 1)
            elif c >= 2:
                before = c - 2 if c < EARLY else c - 1
                dve.wait_ge(S(f"gates_out{before % 2}"), 16 * (before // 2 + 1))
            dve.tensor_copy(stage(c), src[:]).then_inc(S("panel_read"), 1)
        elif key.startswith("br"):
            n, c = int(key[2]), int(key[3])
            b = 4 * n + c
            if b == 0:
                dve.wait_ge(S("branch_lo"), 24)
                dve.wait_ge(S("branch_hi"), 24)
            dve.wait_ge(S("gate_sig"), b + 1)
            m = merged[:, :, c * 512:(c + 1) * 512]
            g3 = gsb[:, b % 2, :].rearrange("p (a b) -> p a b", a=TT)
            s3 = src[:].rearrange("p (a b) -> p a b", a=TT)
            if n == 0:
                dve.tensor_tensor(m, s3, g3, ALU.mult).then_inc(S("panel_read"), 1)
                dve.sem_inc if False else None
                dve.wait_ge(S("panel_read"), pi + 1)
                dve.tensor_scalar(zr[:, 0:1], zr[:, 1:2], 0.0, None, ALU.mult).then_inc(S("gate_used"), 1)
                dve.wait_ge(S("gate_used"), b + 1)
            else:
                p3 = prod[:].rearrange("p (a b) -> p a b", a=TT)
                dve.tensor_tensor(p3, s3, g3, ALU.mult).then_inc(S("panel_read"), 1)
                dve.wait_ge(S("panel_read"), pi + 1)
                dve.tensor_tensor(m, m, p3, ALU.add).then_inc(S("gate_used"), 1)
                dve.wait_ge(S("gate_used"), b + 1)
        else:
            c = int(key[2])
            if c == 0:
                dve.wait_ge(S("x_in"), 32)
            xs = x_sb[:, :, c * 512:(c + 1) * 512]
            dve.tensor_tensor(xs, src[:].rearrange("p (a b) -> p a b", a=TT), xs, ALU.add).then_inc(S("panel_read"), 1)

    eng = {}

    def rsqrt_steps_dve(link, dst, src, scale):
        link(eng["dve"].tensor_scalar(dst, src, scale, EPS, ALU.mult, ALU.add))

    def norm_act(act):
        for tt in range(TT):
            act.wait_ge(S("x_in1" if tt else "x_in"), 16)
            for h in range(2):
                ins = act.activation(pj[1][:], x_sb[:, tt, h * 1024:(h + 1) * 1024], ACT.Square,
                                     accum_out=stat[:, 2 * tt + h:2 * tt + h + 1])
                ins.then_inc(S("n1_sq"), 1)
                act.wait_ge(S("n1_sq"), 2 * tt + h + 1)
        root_act(act, "n1")

    def root_act(act, nm):
        act.wait_ge(S(nm + "_ms"), 1)
        act.activation(stat[:, 6:8], stat[:, 4:6], ACT.Sqrt).then_inc(S(nm + "_sd"), 1)

    def norm_dve(dve, link):
        dve.wait_ge(S("n1_sq"), 4)
        link(dve.tensor_tensor(stat[:, 4:6], stat[:, 0:4:2], stat[:, 1:4:2], ALU.add))
        rstd_dve(dve, link, "n1")
        for tt in range(TT):
            dve.tensor_scalar(x_sb[:, tt, :], x_sb[:, tt, :], stat[:, 8 + tt:9 + tt], None, ALU.mult).then_inc(S("n1_x"), 1)

    def rstd_dve(dve, link, nm):
        dve.tensor_scalar(stat[:, 4:6], stat[:, 4:6], 1.0 / D, EPS, ALU.mult, ALU.add).then_inc(S(nm + "_ms"), 1)
        dve.wait_ge(S(nm + "_ms"), 1)
        dve.wait_ge(S(nm + "_sd"), 1)
        link(dve.reciprocal(stat[:, 8:10], stat[:, 6:8]))
        link(dve.tensor_tensor(stat[:, 10:12], stat[:, 8:10], stat[:, 8:10], ALU.mult))
        link(dve.tensor_tensor(stat[:, 10:12], stat[:, 10:12], stat[:, 4:6], ALU.mult))
        link(dve.tensor_scalar(stat[:, 10:12], stat[:, 10:12], -0.5, 1.5, ALU.mult, ALU.add))
        dve.tensor_tensor(stat[:, 8:10], stat[:, 8:10], stat[:, 10:12], ALU.mult).then_inc(S(nm + "_r"), 1)
        dve.wait_ge(S(nm + "_r"), 1)

    def turn_pe(pe, src, pre, pairs, banks=4):
        for b in pairs:
            if b >= banks:
                pe.wait_ge(S(pre + "_hi"), V(pre + "_hi") + 2 * (b - banks) + 2)
                if pre != "r":
                    pe.wait_ge(S(pre + "_lo"), 2 * (b - banks) + 2)
            for k in range(2):
                for tt in range(TT):
                    kt = 2 * b + k
                    mm = pe.transpose(px[b % banks][:, (k * TT + tt) * P:(k * TT + tt + 1) * P],
                                      src[:, tt, kt * P:(kt + 1) * P], C("ident"))
            mm.then_inc(S(pre + "_turned"), 1)

    def m_turn_pe(pe, c):
        pe.wait_ge(S("gate_used"), 9 + c)
        turn_pe(pe, merged, "m", (2 * c, 2 * c + 1))

    def m_hi_act(act, c):
        for kt in range(4 * c, 4 * c + 4):
            act.wait_ge(S("m_turned"), kt // 2 + 1)
            act.activation(hr[:, hi, kt, :], px[kt // 2 % 4][:, (kt % 2) * T:(kt % 2 + 1) * T], ACT.Copy).then_inc(S("m_hi"), 1)

    def m_lo_dve(dve, c):
        for kt in range(4 * c, 4 * c + 4):
            dve.wait_ge(S("m_hi"), 2 * (kt // 2) + 2)
            dve.tensor_tensor(hr[:, lo, kt, :], px[kt // 2 % 4][:, (kt % 2) * T:(kt % 2 + 1) * T], hr[:, hi, kt, :].bitcast(F32), ALU.subtract).then_inc(S("m_lo"), 1)

    def r_sq_act(act, c):
        act.wait_ge(S("panel_read"), FIRST_O + c + 1)
        for tt in range(TT):
            n = c * TT + tt
            act.wait_ge(S("n2_sq"), n) if n else None
            act.activation(junk2[:], x_sb[:, tt, c * 512:(c + 1) * 512], ACT.Square,
                           accum_out=stat[:, 12 + 4 * tt + c:13 + 4 * tt + c]).then_inc(S("n2_sq"), 1)

    def r_turn_pe(pe, c):
        pe.wait_ge(S("panel_read"), FIRST_O + c + 1)
        turn_pe(pe, x_sb, "r", (2 * c, 2 * c + 1), 2)

    def r_gain_dve(dve, c):
        for b in (2 * c, 2 * c + 1):
            dve.wait_ge(S("r_turned"), V("r_turned") + b + 1)
            dve.tensor_tensor(h2t[:, 2 * b:2 * b + 2, :], px[b % 2][:].rearrange("p (k t) -> p k t", k=2),
                              gffn[:, 2 * b:2 * b + 2].unsqueeze(2).to_broadcast([P, 2, T]), ALU.mult).then_inc(S("r_hi"), 2)

    def r_logit_pe(pe, c):
        pe.wait_ge(S("router_in"), 64)
        pe.wait_ge(S("r_hi"), V("r_hi") + 4 * c + 4)
        for kt in range(4 * c, 4 * c + 4):
            mm = pe.matmul(px[3][0:NROUTE, 0:T], wro[:, kt, :], h2t[:, kt, :], start=kt == 0, stop=kt == KT - 1)
        if c == 3:
            mm.then_inc(S("r_logit"), 1)

    def rows_pe(pe):
        pe.wait_ge(S("const_b"), 16)
        pe.wait_ge(S("rows_in"), 48)
        pe.transpose(pj[0][:, 0:16], rows[:, 0, :], C("ident")[0:16, 0:16])
        pe.transpose(pj[0][:, 16:32], rows[:, 1, :], C("ident")[0:16, 0:16])
        pe.transpose(pj[0][:, 32:36], rows[0:4, 2, :], C("ident")[0:4, 0:4]).then_inc(S("rows_turned"), 1)

    def rows_dve(dve, link):
        dve.wait_ge(S("rows_turned"), 1)
        link(dve.tensor_copy(gmix[:], pj[0][:, 0:16]))
        link(dve.tensor_copy(gffn[:], pj[0][:, 16:32]))
        l_, e_, p_ = lb[:, 0, :], lb[:, 1, :], lb[:, 2, :]
        dve.tensor_tensor(l_, pj[0][:, 32:36], gmix[:, 0:4], ALU.bypass) if False else None
        link(dve.tensor_copy(l_, pj[0][:, 32:36]))
        dve.tensor_tensor(l_, l_, l_, ALU.subtract).then_inc(S("lb_sub"), 1)

    def lb_act(act):
        act.wait_ge(S("lb_sub"), 1)
        act.activation(lb[:, 1, :], lb[:, 0, :], ACT.Exp).then_inc(S("lb_exp"), 1)

    def lb_dve(dve, link):
        dve.wait_ge(S("lb_exp"), 1)
        dve.wait_ge(S("lb_sub"), 1)
        link(dve.reciprocal(lb[:, 2, :], lb[:, 1, :]))
        link(dve.tensor_tensor(lb[:, 2, :], lb[:, 2, :], lb[:, 1, :], ALU.mult))
        link(dve.tensor_tensor(lb[:, 2, :], lb[:, 2, :], lb[:, 2, :], ALU.subtract))
        dve.tensor_scalar(lb[:, 3, :], lb[:, 2, :], -1.0, 1.0, ALU.mult, ALU.add).then_inc(S("lb_ready"), 1)
        dve.wait_ge(S("lb_ready"), 1)

    def nsa_norm_dve1(dve, link):
        dve.wait_ge(S("panel_read"), 3)
        link(dve.tensor_tensor(sq[:, 0:4, :], pn[:, 0:4, :], pn[:, 0:4, :], ALU.mult))
        link(dve.tensor_tensor(sq[:, 4, :], pn[:, 6, :], pn[:, 6, :], ALU.mult))
        dve.tensor_tensor(sq[:, 5, :], pn[:, 8, :], pn[:, 8, :], ALU.mult).then_inc(S("nsa_sq"), 1)

    def nsa_norm_pe(pe):
        pe.wait_ge(S("nsa_sq"), V("nsa_sq") + 1)
        pe.wait_ge(S("h_hi"), KT)
        pe.wait_ge(S("h_lo"), KT)
        for b in range(3):
            mm = pe.matmul(px[b][:], C("halves"), sq[:, 2 * b:2 * b + 2, :].rearrange("p a b -> p (a b)"), start=True, stop=True)
        mm.then_inc(S("nsa_ss"), 1)

    def nsa_norm_dve2(dve, link):
        dve.wait_ge(S("nsa_ss"), V("nsa_ss") + 1)
        for b in range(3):
            dve.tensor_scalar(rr[:, 2 * b:2 * b + 2, :].rearrange("p a b -> p (a b)"), px[b][:], 1.0 / HD, EPS, ALU.mult, ALU.add).then_inc(S("nsa_ms"), 1)

    def nsa_norm_act(act):
        act.wait_ge(S("nsa_ms"), V("nsa_ms") + 3)
        act.activation(rr[:], rr[:], ACT.Sqrt).then_inc(S("nsa_sd"), 1)

    def nsa_norm_dve3(dve, link):
        dve.wait_ge(S("nsa_sd"), V("nsa_sd") + 1)
        dve.wait_ge(S("nsa_zero"), 1)
        link(dve.reciprocal(rr[:], rr[:]))
        link(dve.tensor_scalar(ngain[:, 0:1], ngain[:, 0:1], HD ** -0.5, None, ALU.mult))
        dve.scalar_tensor_tensor(pn[:, 0:4, :], pn[:, 0:4, :], ngain[:, 0:1], rr[:, 0:4, :], ALU.mult, ALU.mult).then_inc(S("nsa_qk"), 1)
        for ty in range(2):
            for g in range(KV):
                r = slice(g * HD, (g + 1) * HD)
                dve.scalar_tensor_tensor(kz[r, ty, g, :], pn[r, 6 + 2 * ty, :], ngain[r, 2 + ty:3 + ty], rr[r, 4 + ty, :], ALU.mult, ALU.mult).then_inc(S("nsa_qk"), 1)
        dve.wait_ge(S("nsa_qk"), V("nsa_qk") + 5)

    def nsa_zero_pool(pool):
        pool.wait_ge(S("h_lo"), KT)
        pool.memset(kz[:], 0.0).then_inc(S("nsa_z"), 1)
        pool.memset(vz[:], 0.0).then_inc(S("nsa_z"), 1)
        pool.memset(kcz[:], 0.0).then_inc(S("nsa_z"), 1)
        pool.wait_ge(S("nsa_z"), 3)
        pool.memset(zr[:], 0.0).then_inc(S("nsa_zero"), 1)

    def nsa_turn_pe(pe):
        pe.wait_ge(S("nsa_ms"), V("nsa_ms") + 3)
        for ty in range(2):
            for kt in range(TT):
                pe.transpose(px[3][:, (ty * TT + kt) * P:(ty * TT + kt + 1) * P], pn[:, 7 + 2 * ty, kt * P:(kt + 1) * P], C("ident"))
        for tt in range(TT):
            pe.transpose(px[2][:, tt * P:(tt + 1) * P], pn[:, 10, tt * P:(tt + 1) * P], C("ident"))
        pe.wait_ge(S("small_in"), SMALL_IN)
        pe.transpose(px[0][:, 0:64], pe2[:], C("ident")[0:64, 0:64]).then_inc(S("nsa_turned"), 1)

    def nsa_turn_dve(dve, link):
        dve.wait_ge(S("nsa_turned"), V("nsa_turned") + 1)
        v4 = px[3][:].rearrange("p (y k c) -> p y k c", y=2, k=TT)
        for g in range(KV):
            c = slice(g * HD, (g + 1) * HD)
            link(dve.tensor_copy(vz[:, :, :, g, c].rearrange("p k y c -> p y k c"), v4[:, :, :, c]))
        for v in range(2):
            kc = pn[:, 4 + v, :].rearrange("p (n l) -> p l n", l=16)
            link(dve.tensor_copy(ax[:, v, 0:16, 0:15], kc[:, :, 0:15]))
            link(dve.tensor_copy(ax[:, v, 16:32, 0:15], kc[:, :, 1:16]))
            link(dve.tensor_copy(ax[:, v, :, 15], px[0][:, v * 32:(v + 1) * 32]))
        dve.memset(vcb[:], 0.0).then_inc(S("cmp_in"), 1)
        dve.wait_ge(S("cmp_in"), V("cmp_in") + 1)

    def nsa_gate_act(act):
        act.wait_ge(S("nsa_turned"), V("nsa_turned") + 1)
        act.activation(gate[:], px[2][:, 0:2 * P].rearrange("p (a b) -> p a b", a=TT)[:, :, 0:24], ACT.Sigmoid).then_inc(S("nsa_gates"), 1)

    def cmp1_pe(pe, v, part):
        if v == 0 and part == 0:
            pe.wait_ge(S("cmp_in"), V("cmp_in") + 1)
            pe.wait_ge(S("w1_in"), 64)
            pe.wait_ge(S("nsa_gates"), V("nsa_gates") + 1)
        for l in range(part * 8, part * 8 + 8):
            for g in range(KV):
                r = slice(g * HD, (g + 1) * HD)
                mm = pe.matmul(px[2 * v + g][r, 0:16], w1[r, v, l, :], ax[r, v, l, :], start=l == 0, stop=l == 31)
        if part == 3:
            mm.then_inc(S("cmp_h"), 1)

    def cmp_dve1(dve, link):
        for v in range(2):
            dve.wait_ge(S("cmp_h"), V("cmp_h") + v + 1)
            for g in range(KV):
                r = slice(g * HD, (g + 1) * HD)
                dve.tensor_copy(hid[r, 0, v, :], px[2 * v + g][r, 0:16]).then_inc(S("cmp_hidden"), 1)
        dve.wait_ge(S("cmp_hidden"), V("cmp_hidden") + 4)
        z, a2, u = hid[:, 1], hid[:, 2], hid[:, 3]
        link(dve.memset(hid[:, 1:6], 0.0))
        for v in range(2):
            link(dve.tensor_scalar(hid[:, 1, v, 0:15], hid[:, 0, v, 0:15], hid[:, 0, v, 15:16], None, ALU.add))
        link(dve.tensor_tensor(a2, z, z, ALU.mult))
        link(dve.tensor_scalar(a2, a2, 0.044715, 1.0, ALU.mult, ALU.add))
        dve.tensor_tensor(u, z, a2, ALU.mult).then_inc(S("cmp_u"), 1)
        dve.wait_ge(S("cmp_u"), V("cmp_u") + 1)

    def cmp_act1(act):
        act.wait_ge(S("cmp_u"), V("cmp_u") + 1)
        act.activation(hid[:, 4], hid[:, 3], ACT.Sigmoid, scale=2.0 * 0.7978845608028654).then_inc(S("cmp_s"), 1)

    def cmp_dve2(dve, link):
        dve.wait_ge(S("cmp_s"), V("cmp_s") + 1)
        dve.tensor_tensor(hid[:, 5], hid[:, 1], hid[:, 4], ALU.mult).then_inc(S("cmp_g"), 1)

    def cmp2_pe(pe):
        pe.wait_ge(S("cmp_g"), V("cmp_g") + 1)
        pe.wait_ge(S("cmp_hidden"), V("cmp_hidden") + 4)
        for g in range(KV):
            r = slice(g * HD, (g + 1) * HD)
            pe.matmul(px[g][r, 0:16], w2[r, 0, :], hid[r, 5, 0, :], start=True, stop=True)
            mm = pe.matmul(px[2 + g][0:16, 0:HD], hid[r, 5, 1, :], w2[r, 1, :], start=True, stop=True)
        mm.then_inc(S("cmp_kv"), 1)

    def cmp_dve3(dve, link):
        dve.wait_ge(S("cmp_kv"), V("cmp_kv") + 1)
        for g in range(KV):
            r = slice(g * HD, (g + 1) * HD)
            link(dve.tensor_copy(kct[r, 0, :], px[g][r, 0:16]))
            dve.tensor_copy(vcs[:, g, :], px[2 + g][0:16, 0:HD]).then_inc(S("cmp_v"), 1)
        dve.tensor_tensor(kct[:, 1, :], kct[:, 0, :], kct[:, 0, :], ALU.mult).then_inc(S("cmp_sq"), 1)

    def cmp_v_dma(act):
        act.wait_ge(S("cmp_v"), V("cmp_v") + 2)
        for i in range(4):
            for g in range(KV):
                act.dma_start(vcb[(2 * i + g) * 16:(2 * i + g + 1) * 16, i, g * HD:(g + 1) * HD], vcs[:, g, :]).then_inc(S("vcb_in"), 16)

    def cmp3_pe(pe):
        pe.wait_ge(S("cmp_sq"), V("cmp_sq") + 1)
        pe.matmul(px[0][:, 0:16], C("halves"), kct[:, 1, :], start=True, stop=True).then_inc(S("cmp_ss"), 1)

    def cmp_dve4(dve, link):
        dve.wait_ge(S("cmp_ss"), V("cmp_ss") + 1)
        dve.tensor_scalar(kct[:, 2, :], px[0][:, 0:16], 1.0 / HD, EPS, ALU.mult, ALU.add).then_inc(S("cmp_ms"), 1)

    def cmp_act2(act):
        act.wait_ge(S("cmp_ms"), V("cmp_ms") + 1)
        act.activation(kct[:, 2, :], kct[:, 2, :], ACT.Sqrt).then_inc(S("cmp_sd"), 1)

    def cmp_dve5(dve, link):
        dve.wait_ge(S("cmp_sd"), V("cmp_sd") + 1)
        link(dve.reciprocal(kct[:, 3, :], kct[:, 2, :]))
        for g in range(KV):
            r = slice(g * HD, (g + 1) * HD)
            dve.scalar_tensor_tensor(kcz[r, g, :], kct[r, 0, :], ngain[r, 1:2], kct[r, 3, :], ALU.mult, ALU.mult).then_inc(S("cmp_k"), 1)

    def cmp4_pe(pe):
        pe.wait_ge(S("cmp_k"), V("cmp_k") + 2)
        pe.wait_ge(S("nsa_qk"), V("nsa_qk") + 5)
        for tt in range(TT):
            for i in range(4):
                mm = pe.matmul(px[1][:, tt * P + i * 32:tt * P + (i + 1) * 32], pn[:, i, tt * P:(tt + 1) * P],
                               kcz[:].rearrange("p a b -> p (a b)"), start=True, stop=True)
        mm.then_inc(S("cmp_scores"), 1)

    def cmp_dve6(dve, link):
        dve.wait_ge(S("cmp_scores"), V("cmp_scores") + 1)
        link(dve.tensor_tensor(csc[:], px[1][:, 0:256], C("cbias"), ALU.add))
        s3 = csc[:].rearrange("p (h n) -> p h n", n=16)
        link(dve.tensor_reduce(cs[:, 0, :], s3, AX.X, ALU.max))
        dve.tensor_tensor(s3, s3, cs[:, 0, :].unsqueeze(2).to_broadcast([P, 16, 16]), ALU.subtract).then_inc(S("cmp_sub"), 1)

    def cmp_act3(act):
        act.wait_ge(S("cmp_sub"), V("cmp_sub") + 1)
        act.activation(csc[:], csc[:], ACT.Exp).then_inc(S("cmp_exp"), 1)

    def cmp_dve7(dve, link):
        dve.wait_ge(S("cmp_exp"), V("cmp_exp") + 1)
        dve.wait_ge(S("nsa_gates"), V("nsa_gates") + 1)
        s3 = csc[:].rearrange("p (h n) -> p h n", n=16)
        link(dve.tensor_reduce(cs[:, 1, :], s3, AX.X, ALU.add))
        link(dve.reciprocal(cs[:, 2, :], cs[:, 1, :]))
        link(dve.tensor_tensor(cs[:, 3, :].rearrange("p (t i g) -> p t i g", t=TT, i=4), cs[:, 2, :].rearrange("p (t i g) -> p t i g", t=TT, i=4),
                               gate[:, :, 0:8].rearrange("p t (g i) -> p t i g", g=2), ALU.mult))
        link(dve.tensor_tensor(s3, s3, cs[:, 3, :].unsqueeze(2).to_broadcast([P, 16, 16]), ALU.mult))
        c4 = csc[:].rearrange("p (t h n) -> p t h n", t=TT, n=16)
        dve.tensor_tensor(c4, c4, C("cvis").rearrange("p (t n) -> p t n", t=TT).unsqueeze(2).to_broadcast([P, TT, 8, 16]), ALU.mult).then_inc(S("cmp_p"), 1)

    def cmp5_pe(pe):
        pe.wait_ge(S("cmp_p"), V("cmp_p") + 1)
        pe.wait_ge(S("cmp_sub"), V("cmp_sub") + 1)
        for tt in range(TT):
            mm = pe.transpose(px[2][:, tt * P:(tt + 1) * P], csc[:, tt * P:(tt + 1) * P], C("ident"))
        mm.then_inc(S("cmp_pt"), 1)

    def cmp_dve8(dve, link):
        dve.wait_ge(S("cmp_pt"), V("cmp_pt") + 1)
        dve.tensor_copy(ptc[:].rearrange("p a b -> p (a b)"), px[2][:, 0:256]).then_inc(S("cmp_ptc"), 1)
        dve.wait_ge(S("cmp_ptc"), V("cmp_ptc") + 1)

    AU = [(tt, i, ty) for tt in range(TT) for i in range(4) for ty in range(2)]
    NAU = len(AU)

    def att_scores(pe, m):
        tt, i, ty = AU[m]
        nk = P * (tt + 1)
        if m == 0:
            pe.wait_ge(S("cmp_sub"), V("cmp_sub") + 1)
            pe.wait_ge(S("cmp_ms"), V("cmp_ms") + 1)
        if m >= 2:
            pe.wait_ge(S("att_s"), 2 * (m - 1))
        pe.matmul(px[m % 2][:, 0:2 * nk].rearrange("p (g k) -> p g k", g=2), pn[:, i, tt * P:(tt + 1) * P], kz[:, ty, :, 0:nk], start=True, stop=True).then_inc(S("att_scores"), 1)

    def att_soft1(dve, link, m):
        tt, i, ty = AU[m]
        nk = P * (tt + 1)
        dve.wait_ge(S("att_scores"), m + 1)
        if m >= 2:
            dve.wait_ge(S("att_turned"), m - 1)
        dist = C(f"dist{tt}")
        for g in range(KV):
            dve.scalar_tensor_tensor(sb[:, m % 2, g, 0:nk], dist, -SLOPES[g * 4 + i], px[m % 2][:, g * nk:(g + 1) * nk], ALU.mult, ALU.add).then_inc(S("att_s"), 1)
        dve.wait_ge(S("att_s"), 2 * (m + 1))
        dve.tensor_reduce(am[:, m % 2, 0:2], sb[:, m % 2, :, 0:nk], AX.X, ALU.max, negate=True).then_inc(S("att_max"), 1)

    def att_exp(act, m):
        tt, i, ty = AU[m]
        nk = P * (tt + 1)
        act.wait_ge(S("att_max"), m + 1)
        for g in range(KV):
            act.activation(sb[:, m % 2, g, 0:nk], sb[:, m % 2, g, 0:nk], ACT.Exp, bias=am[:, m % 2, g:g + 1],
                           accum_out=am[:, m % 2, 2 + g:3 + g]).then_inc(S("att_exp"), 1)

    def att_soft2(dve, link, m):
        tt, i, ty = AU[m]
        nk = P * (tt + 1)
        dve.wait_ge(S("att_exp"), 2 * (m + 1))
        link(dve.reciprocal(am[:, m % 2, 4:6], am[:, m % 2, 2:4]))
        g0 = 8 * (1 + ty) + i
        link(dve.tensor_tensor(am[:, m % 2, 6:8], am[:, m % 2, 4:6], gate[:, tt, g0:g0 + 5:4], ALU.mult))
        for g in range(KV):
            dve.tensor_scalar(sb[:, m % 2, g, 0:nk], sb[:, m % 2, g, 0:nk], am[:, m % 2, 6 + g:7 + g], None, ALU.mult).then_inc(S("att_p"), 1)

    def att_turn(pe, m):
        tt, i, ty = AU[m]
        pe.wait_ge(S("att_p"), 2 * (m + 1))
        if m == 0:
            pe.wait_ge(S("cmp_ptc"), V("cmp_ptc") + 1)
        if m >= 1:
            pe.wait_ge(S("att_pt"), m)
        for g in range(KV):
            for kt in range(tt + 1):
                mm = pe.transpose(px[2][:, (g * 2 + kt) * P:(g * 2 + kt + 1) * P], sb[:, m % 2, g, kt * P:(kt + 1) * P], C("ident"))
        mm.then_inc(S("att_turned"), 1)

    def att_pt(dve, link, m):
        tt, i, ty = AU[m]
        dve.wait_ge(S("att_turned"), m + 1)
        if m >= 1:
            dve.wait_ge(S("att_pv"), m)
        else:
            dve.wait_ge(S("nsa_qk"), V("nsa_qk") + 5)
        n = tt + 1
        dve.tensor_copy(pt[:].rearrange("p (g k) c -> p g k c", g=2)[:, :, 0:n, :],
                        px[2][:].rearrange("p (g k c) -> p g k c", g=2, k=2)[:, :, 0:n, :]).then_inc(S("att_pt"), 1)

    def att_pv(pe, m):
        tt, i, ty = AU[m]
        pe.wait_ge(S("att_pt"), m + 1)
        n = m // 2
        dst = px[3][:, 0:P]
        if ty == 0:
            if n == 0:
                pe.wait_ge(S("vcb_in"), 16 * 8)
                pe.wait_ge(S("cmp_v"), V("cmp_v") + 2)
            else:
                pe.wait_ge(S("branch_hi"), n)
                pe.wait_ge(S("branch_lo"), n)
            pe.matmul(dst, vcb[:, i, :], ptc[:, tt, :], start=True, stop=False)
        for g in range(KV):
            for kt in range(tt + 1):
                mm = pe.matmul(dst, vz[:, kt, ty, g, :], pt[:, g * 2 + kt, :], start=False,
                               stop=ty == 1 and g == 1 and kt == tt)
        mm.then_inc(S("att_pv"), 1)

    def att_out_act(act, n):
        tt, i, _ = AU[2 * n]
        act.wait_ge(S("att_pv"), 2 * n + 2)
        act.activation(orr[:, hi, i, tt * P:(tt + 1) * P], px[3][:, 0:P], ACT.Copy).then_inc(S("branch_hi"), 1)

    def att_out_dve(dve, link, n):
        tt, i, _ = AU[2 * n]
        dve.wait_ge(S("att_pv"), 2 * n + 2)
        dve.wait_ge(S("branch_hi"), n + 1)
        dve.tensor_tensor(orr[:, lo, i, tt * P:(tt + 1) * P], px[3][:, 0:P], orr[:, hi, i, tt * P:(tt + 1) * P].bitcast(F32), ALU.subtract).then_inc(S("branch_lo"), 1)
        if n == NAU // 2 - 1:
            dve.wait_ge(S("branch_lo"), n + 1)
            dve.tensor_copy(zr[:, 2:3], zr[:, 3:4]).then_inc(S("att_done"), 1)

    class Rec:

        def __init__(self, which):
            self.w = which
            self.nt = 4 if which == "hg" else 2
            self.q = hgq if which == "hg" else None
            self.base = 0 if which == "hg" else 1
            self.step = 3 if which == "hg" else 2

        def n(self, s):
            return f"{self.w}_{s}"

    HGR, GLR_ = Rec("hg"), Rec("gl")

    def rq(R):
        return hgq[:] if R.w == "hg" else glqk[:, 0:2, :]

    def rk(R):
        return hgk[:] if R.w == "hg" else glqk[:, 2:4, :]

    def hg_act1(act):
        act.wait_ge(S("panel_read"), 5)
        act.wait_ge(S("att_done"), 1)
        act.activation(hgk[:], hgz[:], ACT.Sigmoid, scale=-1.0).then_inc(S("hg_sig"), 1)
        act.activation(hgb[:], hgz[:], ACT.Sigmoid).then_inc(S("hg_sig"), 1)

    def hg_act2(act):
        act.wait_ge(S("panel_read"), 7)
        act.activation(hgg[:], hgg[:], ACT.Sigmoid).then_inc(S("hg_gate"), 1)

    def gl_act2(act):
        act.wait_ge(S("panel_read"), PI["gl_r"] + 1)
        act.wait_ge(S("hg_bdone"), 1)
        act.activation(hgi[:], glr[:], ACT.Sigmoid).then_inc(S("gl_gate"), 1)

    def hg_dve1(dve, link):
        dve.wait_ge(S("hg_sig"), 2)
        dve.wait_ge(S("lb_ready"), 1)
        for h in range(4):
            link(dve.tensor_scalar(hgk[:, h, :], hgk[:, h, :], lb[:, 3, h:h + 1], None, ALU.mult))
            link(dve.tensor_scalar(hgb[:, h, :], hgb[:, h, :], lb[:, 3, h:h + 1], lb[:, 2, h:h + 1], ALU.mult, ALU.add))
        link(dve.tensor_scalar(zb0[:], hgb[:], 2.0 ** -60, None, ALU.max))
        link(dve.tensor_scalar(zb1[:], hgb[:], TINY, 2.0 ** 60, ALU.max, ALU.mult))
        dve.tensor_scalar(zb1[:], zb1[:], 1.0, None, ALU.min).then_inc(S("hg_f"), 1)
        dve.wait_ge(S("hg_f"), 1)

    def hg_act3(act):
        act.wait_ge(S("hg_f"), 1)
        act.activation(zb0[:], zb0[:], ACT.Ln).then_inc(S("hg_ln"), 1)
        act.activation(zb1[:], zb1[:], ACT.Ln).then_inc(S("hg_ln"), 1)

    def f2(ap):
        return ap.rearrange("p a b -> p (a b)")

    def hg_dve2(dve, link):
        dve.wait_ge(S("hg_ln"), 2)
        link(dve.tensor_tensor(wbuf[:], zb0[:], zb1[:], ALU.add))
        dve.tensor_tensor_scan(f2(hgb[:]), C("reset"), f2(wbuf[:]), 0.0, ALU.mult, ALU.add).then_inc(S("hg_b"), 1)
        dve.wait_ge(S("hg_b"), 1)

    def gl_pe1(pe):
        pe.wait_ge(S("panel_read"), PI["gl_a"] + 1)
        pe.wait_ge(S("hg_bdone"), 1)
        for a in range(2):
            mm = pe.matmul(px[0][:, a * T:(a + 1) * T], wa2[:, a * P:(a + 1) * P], gla[0:16, :], start=True, stop=True)
        mm.then_inc(S("gl_logit"), 1)

    glx = [wbuf[:, 0:2, :], wbuf[:, 2:4, :], hgk[:, 0:2, :], hgk[:, 2:4, :]]

    def gl_dve1(dve, link):
        dve.wait_ge(S("gl_logit"), 1)
        dve.wait_ge(S("hg_bdone"), 1)
        for a in range(2):
            link(dve.tensor_scalar(glx[0][:, a, :], px[0][:, a * T:(a + 1) * T], bal[:, a:a + 1], None, ALU.add))
        link(dve.tensor_scalar(glx[1], glx[0], -1.0, None, ALU.mult))
        link(dve.tensor_tensor(glx[1], glx[1], glx[0], ALU.min))
        dve.tensor_scalar(glx[0], glx[0], 0.0, None, ALU.min).then_inc(S("gl_u"), 1)
        dve.wait_ge(S("gl_u"), 1)

    def gl_act1(act):
        act.wait_ge(S("gl_u"), 1)
        act.activation(glx[1], glx[1], ACT.Exp).then_inc(S("gl_e"), 1)
        act.wait_ge(S("gl_e"), 1)
        act.activation(glx[1], glx[1], ACT.Ln, bias=1.0).then_inc(S("gl_ln"), 1)

    def gl_dve2(dve, link):
        dve.wait_ge(S("gl_ln"), 1)
        link(dve.tensor_tensor(glx[2], glx[0], glx[1], ALU.subtract))
        link(dve.tensor_scalar(glx[2], glx[2], 1.0 / 16.0, None, ALU.mult))
        link(dve.tensor_scalar(glqk[:, 0:2, :], glqk[:, 0:2, :], HD ** -0.5, None, ALU.mult))
        dve.tensor_tensor_scan(f2(hgb[:, 0:2, :]), C("reset")[:, 0:2 * T], f2(glx[2]), 0.0, ALU.mult, ALU.add).then_inc(S("gl_b"), 1)
        dve.wait_ge(S("gl_b"), 1)

    def zero_st(pool, R):
        if R.w == "hg":
            pool.wait_ge(S("att_done"), 1)
        else:
            pool.wait_ge(S("hg_bdone"), 1)
            pool.wait_ge(S("hg_o"), 2)
        pool.memset(st[:], 0.0).then_inc(S(R.n("zero")), 1)

    zbs = [zb0, zb1]

    def lev_x(dve, link, R, l):
        s_ = 1 << (l - 1)
        nt = R.nt
        if l >= 2:
            dve.wait_ge(S(R.n("z")), 2 * (l - 1))
        b = hgb[:, 0:nt, :]
        x_ = wbuf[:, 0:nt, :]
        if l < NL:
            nb = nt * T // (2 * s_)
            b4 = f2(b).rearrange("p (n h s) -> p n h s", h=2, s=s_)
            x4 = f2(x_).rearrange("p (n h s) -> p n h s", h=2, s=s_)
            mid = b4[:, :, 0, s_ - 1:s_].to_broadcast([P, nb, s_])
            dve.tensor_tensor(x4[:, :, 1, :], b4[:, :, 1, :], mid, ALU.subtract if s_ < CHUNK else ALU.bypass).then_inc(S(R.n("x")), 1) if s_ < CHUNK else \
                dve.tensor_copy(x4[:, :, 1, :], b4[:, :, 1, :]).then_inc(S(R.n("x")), 1)
            dve.tensor_tensor(x4[:, :, 0, :], mid, b4[:, :, 0, :], ALU.subtract).then_inc(S(R.n("x")), 1)
        else:
            b4 = b.rearrange("p n (c s) -> p n c s", c=4)
            x4 = x_.rearrange("p n (c s) -> p n c s", c=4)

            def end(c):
                return b4[:, :, c, CHUNK - 1:CHUNK].to_broadcast([P, nt, CHUNK])
            link(dve.tensor_tensor(x4[:, :, 0, :], end(0), b4[:, :, 0, :], ALU.subtract))
            link(dve.tensor_tensor(x4[:, :, 0, :], x4[:, :, 0, :], end(1), ALU.add))
            link(dve.tensor_tensor(x4[:, :, 1, :], end(1), b4[:, :, 1, :], ALU.subtract))
            dve.tensor_copy(x4[:, :, 2, :], b4[:, :, 2, :]).then_inc(S(R.n("x")), 1)
            dve.tensor_tensor(x4[:, :, 3, :], b4[:, :, 3, :], end(2), ALU.add).then_inc(S(R.n("x")), 1)

    def lev_exp(act, R, l):
        act.wait_ge(S(R.n("x")), 2 * l)
        act.activation(wbuf[:, 0:R.nt, :], wbuf[:, 0:R.nt, :], ACT.Exp).then_inc(S(R.n("w")), 1)

    def lev_z(dve, link, R, l):
        s_ = 1 << (l - 1)
        nt = R.nt
        dve.wait_ge(S(R.n("w")), l)
        if l >= 3:
            dve.wait_ge(S(R.n("sc")), l - 1)
        elif R.w == "gl":
            dve.wait_ge(S("hg_sc"), NL + 1)
        z = zbs[l % 2][:, 0:nt, :]
        x_ = wbuf[:, 0:nt, :]
        v = lambda a: f2(a).rearrange("p (n h s) -> p n h s", h=2, s=s_)
        if l == NL:
            v = lambda a: a.rearrange("p n (h s) -> p n h s", h=2)
        dve.tensor_tensor(v(z)[:, :, 0, :], v(x_)[:, :, 0, :], v(rk(R))[:, :, 0, :], ALU.mult).then_inc(S(R.n("z")), 1)
        dve.tensor_tensor(v(z)[:, :, 1, :], v(x_)[:, :, 1, :], v(rq(R))[:, :, 1, :], ALU.mult).then_inc(S(R.n("z")), 1)

    def head(R, a, h, tt):
        if R.w == "hg":
            return a[:, h, tt * P:(tt + 1) * P]
        return a[(h % 2) * HD:(h % 2 + 1) * HD, h // 2, tt * P:(tt + 1) * P]

    def place(R, h, tt):
        return (tt, h) if R.w == "hg" else (h % 2, 2 * tt + h // 2)

    def lev_pe(pe, R, l):
        if l == 0:
            pe.wait_ge(S(R.n("b")), 1)
            if R.w == "hg":
                pe.wait_ge(S("att_pt"), NAU)
                pe.wait_ge(S("branch_lo"), 8)
                pe.wait_ge(S("branch_hi"), 8)
            else:
                pe.wait_ge(S("gl_u"), 1)
                pe.wait_ge(S("branch_hi"), 16)
                pe.wait_ge(S("branch_lo"), 16)
        else:
            pe.wait_ge(S(R.n("z")), 2 * l)
        if l >= 2:
            pe.wait_ge(S(R.n("st")), l - 1)
        z = zbs[l % 2]
        if l < NL:
            for tt in range(TT):
                for h in range(4):
                    a = head(R, rk(R) if l == 0 else z, h, tt)
                    b = head(R, rq(R) if l == 0 else z, h, tt)
                    bk, at_ = place(R, h, tt)
                    mm = pe.matmul(px[2 * (l % 2) + bk][:, at_ * P:(at_ + 1) * P], a, b, start=True, stop=True)
        else:
            for h in range(4):
                bk, at_ = (0, h) if R.w == "hg" else (h % 2, h // 2)
                mm = pe.matmul(px[2 * (l % 2) + bk][:, at_ * P:(at_ + 1) * P], head(R, z, h, 0), head(R, z, h, 1), start=True, stop=True)
        mm.then_inc(S(R.n("sc")), 1)

    def lev_st(dve, link, R, l):
        dve.wait_ge(S(R.n("sc")), l + 1)
        if l == 0:
            dve.wait_ge(S(R.n("zero")), 1)
        if l < NL:
            mk = C("levels")[:, l * P:(l + 1) * P].bitcast(U32).unsqueeze(1).to_broadcast([P, 4, P])
            for tt in range(TT):
                ins = dve.copy_predicated(st[:, 4 * tt:4 * tt + 4, :], mk, px[2 * (l % 2) + tt][:].rearrange("p (h c) -> p h c", h=4))
                if tt == 0:
                    link(ins)
            ins.then_inc(S(R.n("st")), 1)
        else:
            if R.w == "hg":
                ins = dve.tensor_copy(f2(st2[:]), px[2 * (l % 2)][:])
            else:
                for bk in range(2):
                    ins = dve.tensor_copy(st2[:].rearrange("p (a b) c -> p b a c", b=2)[:, bk, :, :],
                                          px[2 * (l % 2) + bk][:, 0:2 * P].rearrange("p (a c) -> p a c", a=2))
            ins.then_inc(S(R.n("st")), 1)
        dve.wait_ge(S(R.n("st")), l + 1)

    def rec_out(pe, R):
        v = hgi if R.w == "hg" else glv
        pe.wait_ge(S(R.n("st")), NL + 1)
        if R.w == "gl":
            pe.wait_ge(S("panel_read"), PI["gl_v"] + 1)
        for tt in range(TT):
            for h in range(4):
                dst = px[2 + tt][:, h * P:(h + 1) * P]
                vs = lambda k: v[:, k, h * P:(h + 1) * P]
                bk, at_ = place(R, h, tt)
                mm = pe.matmul(dst, st[:, 4 * bk + at_, :], vs(tt), start=True, stop=tt == 0)
                if tt == 1:
                    mm = pe.matmul(dst, st2[:, h, :], vs(0), start=False, stop=True)
            mm.then_inc(S(R.n("o")), 1)

    def out_dve1(dve, link, R):
        ob = [wbuf[:, 0:2, :], wbuf[:, 2:4, :]]
        for tt in range(TT):
            dve.wait_ge(S(R.n("o")), tt + 1)
            link(dve.tensor_copy(f2(ob[tt]), px[2 + tt][:]))
            link(dve.tensor_tensor(f2(zb0[:, 2 * tt:2 * tt + 2, :]), f2(ob[tt]), f2(ob[tt]), ALU.mult))
        link(dve.tensor_reduce(cs[:, 0, 0:8], f2(zb0[:]).rearrange("p (h d) -> p h d", d=P), AX.X, ALU.add))
        dve.tensor_scalar(cs[:, 1, 0:8], cs[:, 0, 0:8], 1.0 / P, EPS, ALU.mult, ALU.add).then_inc(S(R.n("ms")), 1)

    def out_act(act, R):
        act.wait_ge(S(R.n("ms")), 1)
        act.activation(cs[:, 2, 0:8], cs[:, 1, 0:8], ACT.Sqrt).then_inc(S(R.n("sd")), 1)

    def out_dve2(dve, link, R):
        dve.wait_ge(S(R.n("sd")), 1)
        dve.wait_ge(S(R.n("gate")), 1)
        link(dve.reciprocal(cs[:, 3, 0:8], cs[:, 2, 0:8]))
        w3 = f2(wbuf[:]).rearrange("p (h d) -> p h d", d=P)
        link(dve.tensor_tensor(w3, w3, cs[:, 3, 0:8].unsqueeze(2).to_broadcast([P, 8, P]), ALU.mult))
        gn = hgain if R.w == "hg" else ggain
        link(dve.tensor_tensor(w3, w3, gn[:].unsqueeze(1).to_broadcast([P, 8, P]), ALU.mult))
        g = hgg if R.w == "hg" else hgi
        if R.w == "gl":
            link(dve.tensor_tensor(f2(wbuf[:]), f2(wbuf[:]), f2(glr[:]), ALU.mult))
        dve.tensor_tensor(f2(wbuf[:]), f2(wbuf[:]), f2(g[:]), ALU.mult).then_inc(S(R.n("on")), 1)

    def out_turn(pe, R):
        pe.wait_ge(S(R.n("on")), 1)
        w3 = f2(wbuf[:])
        for tt in range(TT):
            for h in range(4):
                mm = pe.transpose(px[h // 2][:, (h % 2) * T + tt * P:(h % 2) * T + (tt + 1) * P], w3[:, (tt * 4 + h) * P:(tt * 4 + h + 1) * P], C("ident"))
        mm.then_inc(S(R.n("ot")), 1)

    def out_hi(act, R):
        act.wait_ge(S(R.n("ot")), 1)
        n = 4 * (R.base + 1)
        for h in range(2):
            act.activation(f2(orr[:, hi, n + 2 * h:n + 2 * h + 2, :]), px[h][:], ACT.Copy).then_inc(S("branch_hi"), 4)

    def out_lo(dve, link, R):
        n = 4 * (R.base + 1)
        for h in range(2):
            dve.wait_ge(S("branch_hi"), 8 * (R.base + 1) + 4 * (h + 1))
            dve.tensor_tensor(f2(orr[:, lo, n + 2 * h:n + 2 * h + 2, :]), px[h][:], f2(orr[:, hi, n + 2 * h:n + 2 * h + 2, :]).bitcast(F32), ALU.subtract).then_inc(S("branch_lo"), 4)
        if R.w == "hg":
            dve.wait_ge(S("branch_lo"), 16)
            dve.tensor_copy(zr[:, 4:5], zr[:, 5:6]).then_inc(S("hg_bdone"), 1)
            dve.wait_ge(S("hg_bdone"), 1)

    LAG = 3
    put("act", 9, lb_act)
    put("dve", 8, lb_dve)
    put("dve", A0 - 2, nsa_norm_dve1)
    put("pool", 18, nsa_zero_pool)
    put("pe", A0, nsa_norm_pe)
    put("dve", A0, nsa_norm_dve2)
    put("act", A0 + LAG, nsa_norm_act)
    put("dve", A0 + 1, nsa_norm_dve3)
    put("pe", CM, nsa_turn_pe)
    put("dve", CM, nsa_turn_dve)
    put("act", CM + LAG, nsa_gate_act)
    for v in range(2):
        for part in range(4):
            put("pe", CM + 4 + 4 * v + part, cmp1_pe, v, part)
    put("dve", CM + 11, cmp_dve1)
    put("act", CM + 11 + LAG, cmp_act1)
    put("dve", CM + 11, cmp_dve2)
    put("pe", CM + 16, cmp2_pe)
    put("dve", CM + 16, cmp_dve3)
    put("act", CM + 16 + LAG, cmp_v_dma)
    put("pe", CM + 18, cmp3_pe)
    put("dve", CM + 18, cmp_dve4)
    put("act", CM + 18 + LAG, cmp_act2)
    put("dve", CM + 18, cmp_dve5)
    put("pe", CM + 23, cmp4_pe)
    put("dve", CM + 23, cmp_dve6)
    put("act", CM + 23 + LAG, cmp_act3)
    put("dve", CM + 23, cmp_dve7)
    put("pe", CM + 28, cmp5_pe)
    put("dve", CM + 28, cmp_dve8)
    for m in range(NAU + 4):
        pos = AT0 + 2 * m
        if m < NAU:
            put("pe", pos, att_scores, m)
            put("dve", pos, att_soft1, m)
            put("act", pos + LAG, att_exp, m)
        if 1 <= m <= NAU:
            put("dve", pos, att_soft2, m - 1)
        if 2 <= m < NAU + 2:
            put("pe", pos, att_turn, m - 2)
            put("dve", pos, att_pt, m - 2)
        if 3 <= m < NAU + 3:
            put("pe", pos, att_pv, m - 3)
            if (m - 3) % 2 == 1:
                put("act", pos + LAG, att_out_act, (m - 3) // 2)
                put("dve", pos + 1, att_out_dve, (m - 3) // 2)

    def rec_sched(R, r0):
        put("pool", r0, zero_st, R)
        for l in range(NL + 1):
            pos = r0 + 6 + R.step * l
            put("pe", pos, lev_pe, R, l)
            if l >= 1:
                put("dve", pos - R.step, lev_x, R, l)
                put("act", pos - R.step + LAG, lev_exp, R, l)
                put("dve", pos - R.step, lev_z, R, l)
            put("dve", pos, lev_st, R, l)
        e = r0 + 6 + R.step * (NL + 1)
        put("pe", e, rec_out, R)
        put("dve", e, out_dve1, R)
        put("act", e + LAG, out_act, R)
        put("dve", e, out_dve2, R)
        put("pe", e + 5, out_turn, R)
        put("act", e + 5 + LAG, out_hi, R)
        put("dve", e + 5, out_lo, R)
        return e + 9

    put("act", HG0 + 1, hg_act1)
    put("act", HG0 + 1, hg_act2)
    put("dve", HG0 + 1, hg_dve1)
    put("act", HG0 + 3, hg_act3)
    put("dve", HG0 + 1, hg_dve2)
    e_hg = rec_sched(HGR, HG0 + 4)
    G = e_hg
    put("act", G + 3, gl_act2)
    put("pe", G, gl_pe1)
    put("dve", G, gl_dve1)
    put("act", G + 3, gl_act1)
    put("dve", G, gl_dve2)
    e_gl = rec_sched(GLR_, G + 4)
    assert e_gl <= UB + 3, (e_gl, UB)
    for c in range(4):
        pos = min(UO - 4 + 2 * c, UO)
        put("pe", pos, m_turn_pe, c)
        put("act", pos + 3, m_hi_act, c)
        put("dve", pos + (c < 2), m_lo_dve, c)
    for c in range(3):
        pos = UO + 8 * (c + 1) + 2
        put("act", pos + LAG, r_sq_act, c)
        put("pe", pos, r_turn_pe, c)
        put("dve", pos, r_gain_dve, c)
        put("pe", pos + 3, r_logit_pe, c)

    block = nc.Block()
    block.__enter__()

    NOV = small("nov", [1, 20], I32)

    gu_items = [None]

    rt = small
    brt = rt("brt", [P, NROUTE])
    lg = rt("lg", [P, TT, NROUTE])
    gl8 = rt("gl8", [P, TT, 8])
    elm = rt("elm", [P, TT, NE])
    mx8 = rt("mx8", [P, TT, 2, 8])
    ix8 = rt("ix8", [P, TT, 2, 8], U32)
    ixf = rt("ixf", [P, TT, 4])
    ohg = rt("ohg", [P, TT, NG])
    ex8 = rt("ex8", [P, TT, 2, 8])
    rs = rt("rs", [P, TT, 8])
    junk2 = rt("junk2", [P, 512])
    RB = MX
    rb_off = [RB]

    def rb(name, shape, dt=F32):
        n = (4 * int(np.prod(shape[1:])) + 31) // 32 * 32
        t_ = at(name, shape, rb_off[0], dt)
        rb_off[0] += n
        assert rb_off[0] <= MX + 28 * K
        return t_
    ek = rb("ek", [P, TT, 2, NE])
    e12 = rb("e12", [P, TT, NE])
    rank = rb("rank", [P, 3, NE])
    above = rb("above", [P, 3, NE, T // SLOTS - 1])
    tile_ = rb("tile_", [P, 3, NE])
    base = rb("base", [P, NE])
    past = rb("past", [P, NE])
    item = rb("item", [P, TT, NE])
    pos_ = rb("pos_", [P, TT, NE])
    pick = rb("pick", [P, 2, TT, 2, NE])
    sel = rb("sel", [P, 2, TT, 2])
    oh48 = rb("oh48", [P, TT, 2, COLS])
    val = rb("val", [P, 2, TT, 2, COLS])
    tab = rb("tab", [P, 2, TT, COLS])
    oe = rb("oe", [P, 3, NE])
    oe32 = rb("oe32", [32, 2, 32])
    ahead = [at("ahead0", [P, 4096], HR_AT), at("ahead1", [P, 4096], rb_off[0])]
    h2t = rb("h2t", [P, KT, T])
    wro = rb("wro", [P, KT, NROUTE])

    def over(ap, dim, shape):
        return ap.unsqueeze(dim).to_broadcast(shape)

    def gate_load(sp, b):
        sp.wait_ge(S("gates_out0"), 16 * 6)
        sp.wait_ge(S("gates_out1"), 16 * 6)
        if b >= 2:
            sp.wait_ge(S("gate_used"), b - 1)
        else:
            sp.wait_ge(S("branch_lo"), 24)
            sp.wait_ge(S("branch_hi"), 24)
        sp.dma_start(gsb[:, b % 2, :], gates_d[b]).then_inc(S(f"gate_in{b % 2}"), 16)

    def item_loop(e, body, first=0):
        with e.Fori(first, NE) as n:
            body(n)
        e.wait_ge(S("overflow_known"), V("overflow_known") + 1)
        nov = e.value_load(NOV[0:1, 0:1], min_val=0, max_val=OVER)
        with e.If(nov > 0):
            with e.Fori(0, nov) as m:
                body(m + NE)
        return nov

    @block.sync
    def _(sp):
        def router_loads():
            sp.wait_ge(S("m_lo"), KT)
            sp.dma_start(wro[:, :, 0:NG], i_["w_grp"][0].rearrange("(k p) c -> p k c", p=P)).then_inc(S("router_in"), 16)
            sp.dma_start(wro[:, :, NG:NROUTE], i_["w_exp"][0].rearrange("(k p) c -> p k c", p=P)).then_inc(S("router_in"), 16)
            sp.dma_start(brt[:, 0:NG], i_["b_grp"].broadcast_to([P, NG])).then_inc(S("router_in"), 16)
            sp.dma_start(brt[:, NG:NROUTE], i_["b_exp"].broadcast_to([P, NE])).then_inc(S("router_in"), 16)

        def expert_slot(e, s_, place=None, loaded=None):
            if s_ < 4:
                src = gexp_w[bass.ds(e, 1), s_ * 512:(s_ + 1) * 512, :].rearrange("e (k p) c -> p (e k) c", p=P)
                dst = (RING[:, s_, :] if place is None else place[:]).rearrange("p (k c) -> p k c", k=4)
            else:
                src = down_w[bass.ds(e, 1), (s_ - 4) * 256:(s_ - 3) * 256, :].rearrange("e (k p) c -> p (e k) c", p=P)
                dst = RING[:, s_, :].rearrange("p (k c) -> p k c", k=2)
            sp.dma_start(dst, src).then_inc(S(loaded or f"expert{s_}"), 16)

        consts_loads(sp)
        for k_ in range(3):
            load_slot(sp, k_)
        small_loads(sp)
        sp.wait_ge(S("h_turned"), 8)
        sp.wait_ge(S("h_lo"), KT)
        for v in range(2):
            for half in range(2):
                sp.dma_start(w1[half * HD:(half + 1) * HD, v, :, :], i_["cmp_w1"][0, v].rearrange("(l d) c -> d l c", d=HD)).then_inc(S("w1_in"), 16)
        for k_ in range(3, len(slots)):
            pi, s_, _, _ = slots[k_]
            key = panels[pi]["key"]
            load_slot(sp, k_)
            old = panels[pi - 2]["key"] if pi >= 2 and s_ == len(panels[pi]["src"]) - 1 else ""
            if old.startswith("mg"):
                c = int(old[2:])
                sp.wait_ge(S("panel_read"), pi - 1)
                sp.dma_start(gates_d[c], stage(c)).then_inc(S(f"gates_out{c % 2}"), 16)
            if key.startswith("br"):
                b = int(key[2]) * 4 + int(key[3])
                if b >= 2:
                    gate_load(sp, b - 2)
            if k_ == len(slots) - 5:
                router_loads()
            if k_ in (len(slots) - 4, len(slots) - 3, len(slots) - 2):
                if k_ == len(slots) - 4:
                    sp.wait_ge(S("m_lo"), KT)
                expert_slot(0, k_ - len(slots) + 7)
            if k_ == len(slots) - 8:
                gate_load(sp, 10)
                gate_load(sp, 11)
                sp.wait_ge(S("branch_lo"), 24)
                sp.dma_start(x_sb[:], i_["x"][0].rearrange("(a p) d -> p a d", p=P)).then_inc(S("x_in"), 16)
        for k_ in range(len(slots) - 3, len(slots)):
            sp.wait_ge(S("split_lo"), slots[k_][3])
            expert_slot(0, k_ % 3)
        sp.wait_ge(S("unit_done"), NU)
        expert_slot(1, 0, ahead[0], "ahead0")
        sp.wait_ge(S("r_logit"), V("r_logit") + 1)
        expert_slot(1, 1, ahead[1], "ahead1")

        def expert(e, n, slots_=range(6)):
            for s_ in slots_:
                if s_ < 2:
                    sp.wait_ge(S(f"used{s_}"), n - 1)
                elif s_ < 4:
                    sp.wait_ge(S(f"used{s_}"), n)
                elif s_ == 4:
                    sp.wait_ge(S("down_done"), n * 4)
                expert_slot(e, s_)
        expert(2, 2, (0, 1))
        expert(1, 1, (2, 3, 4, 5))
        expert(2, 2, (2, 3, 4, 5))
        with sp.Fori(3, NE) as e:
            expert(e, e)
        sp.wait_ge(S("overflow_known"), V("overflow_known") + 1)
        nov = sp.value_load(NOV[0:1, 0:1], min_val=0, max_val=OVER)
        with sp.If(nov > 0):
            with sp.Fori(0, nov) as n:
                eo = sp.value_load(NOV[0:1, bass.ds(n + 1, 1)], min_val=0, max_val=NE - 1)
                expert(eo, n + NE)
        ov = out[0].rearrange("(a p) d -> p a d", p=P)
        for c in range(4):
            sp.wait_ge(S("summed"), (nov + NE) * 8 + (2 * c - 4))
            sp.dma_start(ov[:, :, c * 512:(c + 1) * 512], x_sb[:, :, c * 512:(c + 1) * 512]).then_inc(S("out_done"), 16)
        sp.wait_ge(S("out_done"), 64)
        sp.wait_ge(S("gates_out0"), 16 * 6)
        sp.wait_ge(S("gates_out1"), 16 * 6)

    @block.scalar
    def _(act):
        eng["act"] = act
        norm_act(act)
        for u in range(3):
            act_hi(act, u)
        for kt in range(KT):
            b = kt // 2
            act.wait_ge(S("h_turned"), b + 1)
            act.activation(hr[:, hi, kt, :], px[b % 4][:, (kt % 2) * T:(kt % 2 + 1) * T], ACT.Copy, scale=gmix[:, kt:kt + 1]).then_inc(S("h_hi"), 1)
        for u in range(NU):
            late = [(fn, a) for fn, a in sched["act"].get(u, ()) if fn is not m_hi_act]
            for fn, a in sched["act"].get(u, ()):
                if fn is m_hi_act:
                    fn(act, *a)
            if u >= 3:
                act_hi(act, u)
            for fn, a in late:
                fn(act, *a)
            if u > UB + 2 and (u - UB) % 2 == 1 and u < UO + 3:
                b = (u - UB - 3) // 2
                act.wait_ge(S(f"gate_in{b % 2}"), 16 * (b // 2 + 1))
                act.activation(gsb[:, b % 2, :], gsb[:, b % 2, :], ACT.Sigmoid).then_inc(S("gate_sig"), 1)
        r_sq_act(act, 3)
        root_act(act, "n2")
        act.wait_ge(S("n2_r"), 1)
        for tt in range(TT):
            act.activation(h2[:, tt, :], x_sb[:, tt, :], ACT.Copy, scale=stat[:, 8 + tt:9 + tt]).then_inc(S("n2_x"), 1)
        act.wait_ge(S("r_shift"), V("r_shift") + 1)
        act.activation(ex8[:], ex8[:], ACT.Exp).then_inc(S("r_exp"), 1)

        def chosen_rows(n):
            act.wait_ge(S("x_chosen"), n + 1)
            act.activation(xg[:], pj[0][:, 0:512], ACT.Copy).then_inc(S("x_rows"), 1)
        chosen_rows(0)

        def item_act(n):
            chosen_rows(n + 1)
            act.wait_ge(S("gt_turned"), n + 1)
            act.activation(sgm[:], px[1][:, 256:512].rearrange("p (h c) -> p h c", h=2)[:, :, 0:64], ACT.Sigmoid).then_inc(S("sig_done"), 1)
            for c in range(4):
                act.wait_ge(S("down_done"), n * 4 + (c + 1))
                act.activation(yt[:, c % 2, :], pj[1][:, c % 2 * 512:(c % 2 + 1) * 512], ACT.Copy).then_inc(S("y_ready"), 1)

        item_loop(act, item_act)

    @block.gpsimd
    def _(pool):
        for u in range(NU):
            pool_lo(pool, u)
            for fn, a in sched["pool"].get(u, ()):
                fn(pool, *a)

    @block.tensor
    def _(pe):
        eng["pe"] = pe
        rows_pe(pe)
        pe.wait_ge(S("n1_x"), 2)
        turn_pe(pe, x_sb, "h", range(4))
        for u in range(NU):
            for fn, a in sched["pe"].get(u, ()):
                if fn is m_turn_pe:
                    fn(pe, *a)
            pe_unit(pe, u)
            if u < 3:
                turn_pe(pe, x_sb, "h", ((4, 5), (6,), (7,))[u])
            for fn, a in sched["pe"].get(u, ()):
                if fn is not m_turn_pe:
                    fn(pe, *a)
        r_turn_pe(pe, 3)
        r_logit_pe(pe, 3)
        pe.wait_ge(S("r_lt"), V("r_lt") + 1)
        for tt in range(TT):
            mm = pe.transpose(px[0][:, tt * 64:tt * 64 + NROUTE], ltb[0:NROUTE, tt * P:(tt + 1) * P], C("ident")[0:NROUTE, 0:NROUTE])
        mm.then_inc(S("r_lturned"), 1)
        pe.wait_ge(S("r_onehot"), V("r_onehot") + 1)
        pe.matmul(px[0][:, 0:NE], C("before"), e12[:, 0, :], start=True, stop=True)
        pe.matmul(px[0][:, NE:2 * NE], C("ones"), e12[:, 0, :], start=True, stop=False)
        pe.matmul(px[0][:, NE:2 * NE], C("before"), e12[:, 1, :], start=False, stop=True)
        pe.matmul(px[0][:, 2 * NE:3 * NE], C("ones"), e12[:, 0, :], start=True, stop=False)
        pe.matmul(px[0][:, 2 * NE:3 * NE], C("ones"), e12[:, 1, :], start=False, stop=True).then_inc(S("r_rank"), 1)

        def choose_rows(n):
            pe.wait_ge(S("n2_x"), 2)
            pe.wait_ge(S("oh_ready"), n + 1)
            for tt in range(TT):
                for c in range(4):
                    mm = pe.matmul(pj[0][c * 32:(c + 1) * 32, 0:512], oh[:, tt, :], h2[:, tt, c * 512:(c + 1) * 512],
                                   start=tt == 0, stop=tt == TT - 1)
            mm.then_inc(S("x_chosen"), 1)

        def turn_rows(n):
            pe.wait_ge(S("x_rows"), n + 1)
            for j in range(4):
                mm = pe.transpose(px[0][:, j * P:(j + 1) * P], xg[:, j * P:(j + 1) * P], C("ident"))
            mm.then_inc(S("x_turned"), 1)

        def combine(n, c):
            pe.wait_ge(S("y_ready"), n * 4 + (c + 1))
            for tt in range(TT):
                pe.wait_ge(S("summed"), n * 8 + (2 * c + tt + 1))
                pe.matmul(px[2 + tt][:], ohwt[:, tt * P:(tt + 1) * P], yt[:, c % 2, :], start=True, stop=True).then_inc(S("combined"), 1)

        def item_pe(n, peeled=None):
            pe.wait_ge(S("xt_ready"), n + 1)
            for s_ in range(4):
                w, loaded = RING[:, s_, :], f"expert{s_}"
                if peeled == 1 and s_ < 2:
                    w, loaded = ahead[s_][:], f"ahead{s_}"
                    pe.wait_ge(S(loaded), 16)
                elif peeled == 0 or s_ >= 2:
                    pe.wait_ge(S(loaded), (n + 1) * 16)
                else:
                    pe.wait_ge(S(loaded), n * 16)
                for j in range(4):
                    for c in range(4):
                        mm = pe.matmul(px[1][c * 32:(c + 1) * 32, 0:256], xt[:, j, s_ * 32:(s_ + 1) * 32],
                                       w[:, j * 1024 + c * 256:j * 1024 + (c + 1) * 256],
                                       start=s_ == 0 and j == 0, stop=s_ == 3 and j == 3)
                if not (peeled == 1 and s_ < 2):
                    mm.then_inc(S(f"used{s_}"), 1)
            choose_rows(n + 1)
            pe.wait_ge(S("gu_ready"), n + 1)
            for h in range(2):
                mm = pe.transpose(px[1][:, 256 + h * P:256 + (h + 1) * P], gu[:, h * P:(h + 1) * P], C("ident"))
            mm.then_inc(S("gt_turned"), 1)
            pe.wait_ge(S("w_ready"), n * 2 + 2)
            for tt in range(TT):
                mm = pe.transpose(pj[0][:, 512 + tt * P:512 + (tt + 1) * P], ohw[:, tt, :], C("ident"))
            mm.then_inc(S("w_turned"), 1)
            turn_rows(n + 1)
            pe.wait_ge(S("act_ready"), n + 1)
            pe.wait_ge(S("expert4"), (n + 1) * 16)
            pe.wait_ge(S("expert5"), (n + 1) * 16)
            pe.wait_ge(S("ohwt_ready"), n + 1)
            for c in range(4):
                for f in range(4):
                    g, h = f // 2, f % 2
                    mm = pe.matmul(pj[1][f * 32:(f + 1) * 32, c % 2 * 512:(c % 2 + 1) * 512], act_t[:, h, g * 32:(g + 1) * 32],
                                   RING[:, 4 + g, h * 2048 + c * 512:h * 2048 + (c + 1) * 512], start=True, stop=True)
                mm.then_inc(S("down_done"), 1)
                if c:
                    combine(n, c - 1)
            combine(n, 3)
        choose_rows(0)
        turn_rows(0)
        item_pe(0, 0)
        item_pe(1, 1)
        item_loop(pe, item_pe, 2)

    @block.vector
    def _(dve):
        eng["dve"] = dve
        link = Chain(dve, S("dve_step"))
        rows_dve(dve, link)
        norm_dve(dve, link)
        for kt in range(KT):
            b = kt // 2
            dve.wait_ge(S("h_hi"), 2 * b + 2)
            dve.scalar_tensor_tensor(hr[:, lo, kt, :], px[b % 4][:, (kt % 2) * T:(kt % 2 + 1) * T], gmix[:, kt:kt + 1],
                                     hr[:, hi, kt, :].bitcast(F32), ALU.mult, ALU.subtract).then_inc(S("h_lo"), 1)
        ends = {pan["u1"]: pi for pi, pan in enumerate(panels)}
        for u in range(NU + 1):
            if u in ends:
                dve_read_panel(dve, ends[u])
            for fn, a in sched["dve"].get(u, ()):
                if fn in (m_lo_dve, r_gain_dve):
                    fn(dve, *a)
                else:
                    fn(dve, link, *a)
        link(dve.tensor_copy(gl8[:], over(C("padmax"), 1, [P, TT, 8])))
        r_gain_dve(dve, 3)
        dve.wait_ge(S("r_logit"), V("r_logit") + 1)
        dve.tensor_copy(ltb[0:NROUTE, :], px[3][0:NROUTE, 0:T]).then_inc(S("r_lt"), 1)
        dve.wait_ge(S("n2_sq"), 8)
        link(dve.tensor_reduce(stat[:, 4:6], stat[:, 12:20].rearrange("p (a c) -> p a c", a=TT), AX.X, ALU.add))
        rstd_dve(dve, link, "n2")
        dve.wait_ge(S("r_lturned"), V("r_lturned") + 1)
        dve.wait_ge(S("router_in"), 64)
        for tt in range(TT):
            link(dve.scalar_tensor_tensor(lg[:, tt, :], px[0][:, tt * 64:tt * 64 + NROUTE], stat[:, 8 + tt:9 + tt], brt[:], ALU.mult, ALU.add))
        link(dve.tensor_copy(gl8[:, :, 0:NG], lg[:, :, 0:NG]))
        for tt in range(TT):
            link(dve.max(mx8[:, tt, 0, :], gl8[:, tt, :]))
            link(dve.max_index(ix8[:, tt, 0, :], mx8[:, tt, 0, :], gl8[:, tt, :]))
        link(dve.tensor_copy(ixf[:, :, 0:1], ix8[:, :, 0, 0:1]))
        link(dve.tensor_tensor(ohg[:], over(C("iota32")[:, 0:NG], 1, [P, TT, NG]), ixf[:, :, 0:1].to_broadcast([P, TT, NG]), ALU.is_equal))
        link(dve.tensor_scalar(ohg[:], ohg[:], -1.0, 1e30, ALU.add, ALU.mult))
        for tt in range(TT):
            link(dve.tensor_tensor(elm[:, tt, :].rearrange("p (g e) -> p g e", g=NG), lg[:, tt, NG:NROUTE].rearrange("p (g e) -> p g e", g=NG),
                                   ohg[:, tt, :].unsqueeze(2).to_broadcast([P, NG, EPG]), ALU.add))
            link(dve.max(mx8[:, tt, 1, :], elm[:, tt, :]))
            link(dve.max_index(ix8[:, tt, 1, :], mx8[:, tt, 1, :], elm[:, tt, :]))
        link(dve.tensor_copy(ixf[:, :, 1:3], ix8[:, :, 1, 0:2]))
        dve.tensor_tensor(ex8[:], mx8[:], mx8[:, :, :, 0:1].to_broadcast([P, TT, 2, 8]), ALU.subtract).then_inc(S("r_shift"), 1)
        link(dve.tensor_tensor(ek[:], C("iota32").unsqueeze(1).unsqueeze(1).to_broadcast([P, TT, 2, NE]),
                               ixf[:, :, 1:3].unsqueeze(3).to_broadcast([P, TT, 2, NE]), ALU.is_equal))
        dve.tensor_tensor(e12[:], ek[:, :, 0, :], ek[:, :, 1, :], ALU.add).then_inc(S("r_onehot"), 1)
        dve.wait_ge(S("r_exp"), 1)
        link(dve.tensor_reduce(rs[:, :, 0:2], ex8[:], AX.X, ALU.add))
        link(dve.reciprocal(rs[:, :, 2:4], rs[:, :, 0:2]))
        link(dve.tensor_tensor(rs[:, :, 4:6], ex8[:, :, 1, 0:2], rs[:, :, 3:4].to_broadcast([P, TT, 2]), ALU.mult))
        link(dve.tensor_reduce(rs[:, :, 6:7], rs[:, :, 4:6], AX.X, ALU.add))
        link(dve.reciprocal(rs[:, :, 7:8], rs[:, :, 6:7]))
        link(dve.tensor_tensor(rs[:, :, 4:6], rs[:, :, 4:6], rs[:, :, 7:8].to_broadcast([P, TT, 2]), ALU.mult))
        link(dve.tensor_tensor(rs[:, :, 4:6], rs[:, :, 4:6], rs[:, :, 2:3].to_broadcast([P, TT, 2]), ALU.mult))
        dve.wait_ge(S("r_rank"), V("r_rank") + 1)
        link(dve.tensor_copy(f2(rank[:, 0:2, :]), px[0][:, 0:2 * NE]))
        link(dve.tensor_scalar(rank[:, 2, :], px[0][:, 2 * NE:3 * NE], -1.0, None, ALU.add))
        link(dve.tensor_tensor(above[:], rank[:].unsqueeze(3).to_broadcast([P, 3, NE, T // SLOTS - 1]),
                               C("steps").unsqueeze(1).unsqueeze(1).to_broadcast([P, 3, NE, T // SLOTS - 1]), ALU.is_ge))
        link(dve.tensor_reduce(tile_[:], above[:], AX.X, ALU.add))
        link(dve.scalar_tensor_tensor(pos_[:], tile_[:, 0:2, :], -float(SLOTS), rank[:, 0:2, :], ALU.mult, ALU.add))
        link(dve.tensor_tensor_scan(base[:], C("ones")[:, 0:NE], tile_[:, 2, :], 0.0, ALU.mult, ALU.add))
        link(dve.tensor_copy(oe[:, 0, :], base[:]))
        link(dve.tensor_tensor(base[:], base[:], tile_[:, 2, :], ALU.subtract))
        link(dve.tensor_tensor(past[:], base[:], C("iota32"), ALU.subtract))
        link(dve.scalar_tensor_tensor(item[:], tile_[:, 0:2, :], float(NE - 1), over(past[:], 1, [P, TT, NE]), ALU.add, ALU.add))
        link(dve.scalar_tensor_tensor(item[:], tile_[:, 0:2, :], 0.0, item[:], ALU.is_gt, ALU.mult))
        link(dve.tensor_tensor(item[:], item[:], over(C("iota32"), 1, [P, TT, NE]), ALU.add))
        for w, src in enumerate((item, pos_)):
            link(dve.tensor_tensor(pick[:, w], src[:].unsqueeze(2).to_broadcast([P, TT, 2, NE]), ek[:], ALU.mult))
            link(dve.tensor_reduce(sel[:, w], pick[:, w], AX.X, ALU.add))
        link(dve.tensor_tensor(oh48[:], C("iota48").unsqueeze(1).unsqueeze(1).to_broadcast([P, TT, 2, COLS]),
                               sel[:, 0].unsqueeze(3).to_broadcast([P, TT, 2, COLS]), ALU.is_equal))
        link(dve.tensor_scalar(sel[:, 1], sel[:, 1], 1.0, None, ALU.add))
        link(dve.tensor_tensor(val[:, 0], oh48[:], sel[:, 1].unsqueeze(3).to_broadcast([P, TT, 2, COLS]), ALU.mult))
        link(dve.tensor_tensor(val[:, 1], oh48[:], rs[:, :, 4:6].unsqueeze(3).to_broadcast([P, TT, 2, COLS]), ALU.mult))
        for w in range(2):
            link(dve.tensor_tensor(tab[:, w], val[:, w, :, 0, :], val[:, w, :, 1, :], ALU.add))

        def mark_rows(n):
            dve.tensor_tensor(oh[:], over(C("slot4")[:, 0:SLOTS], 1, [P, TT, SLOTS]),
                              tab[:, 0, :, bass.ds(n, 1)].to_broadcast([P, TT, SLOTS]), ALU.is_equal).then_inc(S("oh_ready"), 1)

        def turned_rows(n):
            dve.wait_ge(S("x_turned"), n + 1)
            dve.tensor_tensor(xt[:].rearrange("p j (q s) -> p j q s", q=4), px[0][:].rearrange("p (j q s) -> p j q s", j=4, q=4),
                              gffn[:].rearrange("p (q j) -> p j q", q=4).unsqueeze(3).to_broadcast([P, 4, 4, 32]), ALU.mult).then_inc(S("xt_ready"), 1)

        mark_rows(0)
        link(dve.tensor_scalar(oe[:, 1, :], oe[:, 0, :], C("part"), None, ALU.is_gt))
        link(dve.tensor_scalar(oe[:, 2, :], base[:], C("part"), None, ALU.is_le))
        link(dve.tensor_tensor(oe[:, 1, :], oe[:, 1, :], oe[:, 2, :], ALU.mult))
        link(dve.tensor_tensor(oe[:, 1, :], oe[:, 1, :], C("iota32"), ALU.mult))
        link(dve.memset(oe32[:], 0.0))
        link(dve.tensor_reduce(oe32[:, 0, 0:1], oe[0:32, 1, :], AX.X, ALU.add))
        link(dve.transpose(oe32[:, 1, :], oe32[:, 0, :]))
        link(dve.tensor_copy(NOV[0:1, 0:1], oe[0:1, 0, NE - 1:NE]))
        link(dve.tensor_copy(NOV[0:1, 1:1 + OVER], oe32[0:1, 1, 0:OVER]))
        dve.memset(oe32[:, 0, :], 0.0).then_inc(S("overflow_known"), 1)
        dve.memset(up[:], 0.0).then_inc(S("summed"), 2)
        turned_rows(0)

        def item_dve(n):
            dve.wait_ge(S("x_turned"), n + 1)
            mark_rows(n + 1)
            dve.tensor_copy(wc[:], tab[:, :, :, bass.ds(n, 1)].rearrange("p a b o -> p a (b o)")).then_inc(S("wc_ready"), 1)
            dve.wait_ge(S("wc_ready"), n + 1)
            for tt in range(TT):
                dve.tensor_scalar(ohw[:, tt, :], C("slot4"), wc[:, 0, tt:tt + 1], wc[:, 1, tt:tt + 1], ALU.is_equal, ALU.mult).then_inc(S("w_ready"), 1)
            dve.wait_ge(S("used3"), n + 1)
            dve.tensor_copy(gu[:], px[1][:, 0:256]).then_inc(S("gu_ready"), 1)
            dve.wait_ge(S("sig_done"), n + 1)
            dve.wait_ge(S("gt_turned"), n + 1)
            g3 = px[1][:, 256:512].rearrange("p (h c) -> p h c", h=2)
            dve.tensor_tensor(up[:], g3[:, :, 0:64], sgm[:], ALU.mult).then_inc(S("silu_done"), 1)
            dve.wait_ge(S("silu_done"), n + 1)
            dve.tensor_tensor(act_t[:], g3[:, :, 64:128], up[:], ALU.mult).then_inc(S("act_ready"), 1)
            dve.wait_ge(S("w_turned"), n + 1)
            dve.tensor_copy(ohwt[:], pj[0][:, 512:512 + T]).then_inc(S("ohwt_ready"), 1)
            turned_rows(n + 1)
            for c in range(4):
                for tt in range(TT):
                    dve.wait_ge(S("combined"), n * 8 + (2 * c + tt + 1))
                    xs = x_sb[:, tt, c * 512:(c + 1) * 512]
                    dve.tensor_tensor(xs, xs, px[2 + tt][:], ALU.add).then_inc(S("summed"), 1)
        item_loop(dve, item_dve)

    block.__exit__(None, None, None)


_INS = ["x", "norm_mix", "w_in", "cmp_pe", "cmp_w1", "cmp_w2", "q_norm", "k_norm", "hg_lb_logits", "hg_norm",
        "gla_w_a2", "gla_b_a", "gla_norm", "w_branch", "w_out", "norm_ffn", "w_grp", "b_grp", "w_exp", "b_exp",
        "w_gate_up", "w_down"]


def kernel(**inputs):
    import concourse.bacc as bacc
    from concourse.bass_utils import run_bass_kernel_spmd

    nc = bacc.Bacc("TRN2", target_bir_lowering=False, num_devices=1)
    arrays, aps = {}, {}
    for name in _INS:
        a = np.ascontiguousarray(inputs[name])
        arrays["in_" + name] = a
        aps[name] = nc.dram_tensor("in_" + name, a.shape, mybir.dt.from_np(a.dtype), kind="ExternalInput").ap()
    (ca, wa), (cb, wb) = constants()
    consts = {}
    for n, c, w in (("ca", ca, wa), ("cb", cb, wb)):
        w["_n"] = c.shape[1]
        arrays["const_" + n] = c
        consts[n] = nc.dram_tensor("const_" + n, c.shape, F32, kind="ExternalInput").ap()
    out = nc.dram_tensor("out_dram", (1, T, D), F32, kind="ExternalOutput").ap()
    build_program(nc, aps, consts, wa, wb, out)
    r = run_bass_kernel_spmd(nc, [arrays], core_ids=[0])
    return r.results[0]["out_dram"]
```
